# Optimizing a Trainium2 kernel written in Bass

```python
import math
import jax, jax.numpy as jnp
from jax import lax
import numpy as np

D_MODEL = 1024
BATCH = 1
SEQ = 256
DEPTH = 1
DEC_BATCH = 8
DEC_SEQ = 4
PAST_LEN = 2048
PAGE_SIZE = 128

N_META = 16
D_RNN = D_MODEL
N_RNN_HEADS = 16
RNN_HEAD_DIM = D_RNN // N_RNN_HEADS
RNN_CONV_W = 4
LRU_C = 8.0
D_CONV = D_MODEL
CONF_CONV_W = 31
N_GROUPS = 4
EXPERTS_PER_GROUP = 8
N_EXPERTS = N_GROUPS * EXPERTS_PER_GROUP
TOP_K_IN_GROUP = 2
D_EXPERT = D_MODEL // 4
EPS = 1e-6
SPLITS = (D_RNN, 2 * D_RNN, 2 * D_RNN + D_CONV, 2 * D_RNN + 2 * D_CONV, 2 * D_RNN + 2 * D_CONV + D_MODEL)
D_IN_TOTAL = 2 * D_RNN + 2 * D_CONV + 2 * D_MODEL

kernel_name = 'hybrid_rglru_conformer_hmoe_step'

def _rmsnorm(x, g):
    xf = x.astype(jnp.float32)
    y = xf * lax.rsqrt(jnp.mean(xf * xf, axis=-1, keepdims=True) + EPS)
    return (y * g.astype(jnp.float32)).astype(x.dtype)

def _layernorm(x, g, b):
    xf = x.astype(jnp.float32)
    mu = jnp.mean(xf, axis=-1, keepdims=True)
    var = jnp.mean(jnp.square(xf - mu), axis=-1, keepdims=True)
    y = (xf - mu) * lax.rsqrt(var + EPS)
    return (y * g.astype(jnp.float32) + b.astype(jnp.float32)).astype(x.dtype)

def _causal_dwconv(x, buf, w, b):
    width, chans = w.shape
    xp = jnp.concatenate([buf.astype(x.dtype), x], axis=1)
    y = lax.conv_general_dilated(xp, w.astype(x.dtype)[:, None, :], window_strides=(1,), padding='VALID',
                                 dimension_numbers=('NWC', 'WIO', 'NWC'), feature_group_count=chans)
    return y + b.astype(x.dtype), xp[:, -(width - 1):]

def _lru_scan(a, bseq, h0):
    def combine(left, right):
        a1, b1 = left
        a2, b2 = right
        return a1 * a2, a2 * b1 + b2
    a_cum, h_zero = lax.associative_scan(combine, (a, bseq), axis=1)
    h = h_zero + a_cum * h0.astype(jnp.float32)[:, None, :]
    return h, h[:, -1]

def _mixer(xn, h0, c4, c31, w_in, rnn_conv_w, rnn_conv_b, w_rg_a, b_rg_a, w_rg_i, b_rg_i, rg_lambda,
           w_rnn_proj, conf_conv_w, conf_conv_b, conf_ln_g, conf_ln_b, w_conv_proj, w_out):
    bsz, t = xn.shape[0], xn.shape[1]
    proj = xn @ w_in
    u_x, u_y, c_v, c_g, g_rnn, g_conv = jnp.split(proj, SPLITS, axis=-1)
    xc, new_c4 = _causal_dwconv(u_x, c4, rnn_conv_w, rnn_conv_b)
    xh = xc.reshape(bsz, t, N_RNN_HEADS, RNN_HEAD_DIM)
    r = jax.nn.sigmoid((jnp.einsum('bthi,hij->bthj', xh, w_rg_a).reshape(bsz, t, D_RNN) + b_rg_a).astype(jnp.float32))
    i = jax.nn.sigmoid((jnp.einsum('bthi,hij->bthj', xh, w_rg_i).reshape(bsz, t, D_RNN) + b_rg_i).astype(jnp.float32))
    log_a = -LRU_C * r * jax.nn.softplus(-rg_lambda.astype(jnp.float32))
    a = jnp.exp(log_a)
    bseq = jnp.sqrt(-jnp.expm1(2.0 * log_a)) * (i * xc.astype(jnp.float32))
    h, h_last = _lru_scan(a, bseq, h0)
    rnn_out = (h.astype(xn.dtype) * jax.nn.gelu(u_y)) @ w_rnn_proj
    glu = c_v * jax.nn.sigmoid(c_g)
    cc, new_c31 = _causal_dwconv(glu, c31, conf_conv_w, conf_conv_b)
    conv_out = jax.nn.silu(_layernorm(cc, conf_ln_g, conf_ln_b)) @ w_conv_proj
    merged = jax.nn.sigmoid(g_rnn) * rnn_out + jax.nn.sigmoid(g_conv) * conv_out
    return merged @ w_out, h_last, new_c4, new_c31

def _hier_moe(xn, w_group, b_group, w_erouter, b_erouter, w_exp_gate, w_exp_up, w_exp_down):
    xf = xn.reshape(-1, D_MODEL)
    n = xf.shape[0]
    gl = (xf @ w_group).astype(jnp.float32) + b_group.astype(jnp.float32)
    gp = jax.nn.softmax(gl, axis=-1)
    _, gidx = lax.top_k(gl, 1)
    gidx = gidx[:, 0]
    g_gate = jnp.take_along_axis(gp, gidx[:, None], axis=1)[:, 0]
    el = (xf @ w_erouter).astype(jnp.float32).reshape(n, N_GROUPS, EXPERTS_PER_GROUP) + b_erouter.astype(jnp.float32)
    el_sel = jnp.take_along_axis(el, gidx[:, None, None], axis=1)[:, 0]
    ev, eidx = lax.top_k(el_sel, TOP_K_IN_GROUP)
    ew = jax.nn.softmax(ev, axis=-1) * g_gate[:, None]
    flat_idx = gidx[:, None] * EXPERTS_PER_GROUP + eidx
    combine = jnp.sum(jax.nn.one_hot(flat_idx, N_EXPERTS, dtype=jnp.float32) * ew[..., None], axis=1)
    combine = combine.astype(xf.dtype)
    y = jnp.zeros_like(xf)
    for e in range(N_EXPERTS):
        he = jax.nn.silu(xf @ w_exp_gate[e]) * (xf @ w_exp_up[e])
        y = y + combine[:, e:e + 1] * (he @ w_exp_down[e])
    return y.reshape(xn.shape)

def _trunk(x, h0, c4, c31, norm1_g, w_in, rnn_conv_w, rnn_conv_b, w_rg_a, b_rg_a, w_rg_i, b_rg_i, rg_lambda,
           w_rnn_proj, conf_conv_w, conf_conv_b, conf_ln_g, conf_ln_b, w_conv_proj, w_out, norm2_g,
           w_group, b_group, w_erouter, b_erouter, w_exp_gate, w_exp_up, w_exp_down, final_norm_g):
    hs, c4s, c31s = [], [], []
    for l in range(DEPTH):
        mix, h_l, c4_l, c31_l = _mixer(_rmsnorm(x, norm1_g[l]), h0[l], c4[l], c31[l], w_in[l], rnn_conv_w[l],
                                       rnn_conv_b[l], w_rg_a[l], b_rg_a[l], w_rg_i[l], b_rg_i[l], rg_lambda[l],
                                       w_rnn_proj[l], conf_conv_w[l], conf_conv_b[l], conf_ln_g[l], conf_ln_b[l],
                                       w_conv_proj[l], w_out[l])
        x = x + mix
        x = x + _hier_moe(_rmsnorm(x, norm2_g[l]), w_group[l], b_group[l], w_erouter[l], b_erouter[l],
                          w_exp_gate[l], w_exp_up[l], w_exp_down[l])
        hs.append(h_l)
        c4s.append(c4_l)
        c31s.append(c31_l)
    return _rmsnorm(x, final_norm_g), jnp.stack(hs), jnp.stack(c4s), jnp.stack(c31s)

def setup_inputs(seed: int = 0) -> dict:
    key = jax.random.key(seed)
    ks = jax.random.split(key, 40)
    f32 = jnp.float32

    def nrm(k, shape, scale):
        return jax.random.normal(k, shape, f32) * scale

    u = jax.random.uniform(ks[12], (DEPTH, D_RNN), f32, minval=0.9, maxval=0.999)
    s = u ** (1.0 / LRU_C)
    rg_lambda = jnp.log(s) - jnp.log1p(-s)
    return {
        'x_prompt': nrm(ks[0], (BATCH, SEQ, D_MODEL), 1.0),
        'x_sample': nrm(ks[1], (DEC_BATCH, DEC_SEQ, D_MODEL), 1.0),
        'state_rglru_h': nrm(ks[2], (DEPTH, DEC_BATCH, D_RNN), 0.5),
        'state_rglru_conv': nrm(ks[3], (DEPTH, DEC_BATCH, RNN_CONV_W - 1, D_RNN), 1.0),
        'state_conformer_conv': nrm(ks[4], (DEPTH, DEC_BATCH, CONF_CONV_W - 1, D_CONV), 0.5),
        'meta_tokens': nrm(ks[5], (N_META, D_MODEL), 1.0),
        'norm1_g': 1.0 + nrm(ks[6], (DEPTH, D_MODEL), 0.02),
        'w_in': nrm(ks[7], (DEPTH, D_MODEL, D_IN_TOTAL), D_MODEL ** -0.5),
        'rnn_conv_w': nrm(ks[8], (DEPTH, RNN_CONV_W, D_RNN), RNN_CONV_W ** -0.5),
        'rnn_conv_b': nrm(ks[9], (DEPTH, D_RNN), 0.02),
        'w_rg_a': nrm(ks[10], (DEPTH, N_RNN_HEADS, RNN_HEAD_DIM, RNN_HEAD_DIM), RNN_HEAD_DIM ** -0.5),
        'b_rg_a': nrm(ks[11], (DEPTH, D_RNN), 0.02),
        'w_rg_i': nrm(ks[13], (DEPTH, N_RNN_HEADS, RNN_HEAD_DIM, RNN_HEAD_DIM), RNN_HEAD_DIM ** -0.5),
        'b_rg_i': nrm(ks[14], (DEPTH, D_RNN), 0.02),
        'rg_lambda': rg_lambda,
        'w_rnn_proj': nrm(ks[15], (DEPTH, D_RNN, D_MODEL), D_RNN ** -0.5),
        'conf_conv_w': nrm(ks[16], (DEPTH, CONF_CONV_W, D_CONV), CONF_CONV_W ** -0.5),
        'conf_conv_b': nrm(ks[17], (DEPTH, D_CONV), 0.02),
        'conf_ln_g': 1.0 + nrm(ks[18], (DEPTH, D_CONV), 0.02),
        'conf_ln_b': nrm(ks[19], (DEPTH, D_CONV), 0.02),
        'w_conv_proj': nrm(ks[20], (DEPTH, D_CONV, D_MODEL), D_CONV ** -0.5),
        'w_out': nrm(ks[21], (DEPTH, D_MODEL, D_MODEL), D_MODEL ** -0.5),
        'norm2_g': 1.0 + nrm(ks[22], (DEPTH, D_MODEL), 0.02),
        'w_group': nrm(ks[23], (DEPTH, D_MODEL, N_GROUPS), D_MODEL ** -0.5),
        'b_group': nrm(ks[24], (DEPTH, N_GROUPS), 0.01),
        'w_erouter': nrm(ks[25], (DEPTH, D_MODEL, N_GROUPS * EXPERTS_PER_GROUP), D_MODEL ** -0.5),
        'b_erouter': nrm(ks[26], (DEPTH, N_GROUPS, EXPERTS_PER_GROUP), 0.01),
        'w_exp_gate': nrm(ks[27], (DEPTH, N_EXPERTS, D_MODEL, D_EXPERT), D_MODEL ** -0.5),
        'w_exp_up': nrm(ks[28], (DEPTH, N_EXPERTS, D_MODEL, D_EXPERT), D_MODEL ** -0.5),
        'w_exp_down': nrm(ks[29], (DEPTH, N_EXPERTS, D_EXPERT, D_MODEL), D_EXPERT ** -0.5),
        'final_norm_g': 1.0 + nrm(ks[30], (D_MODEL,), 0.02),
    }

def reference(x_prompt, x_sample, state_rglru_h, state_rglru_conv, state_conformer_conv, meta_tokens,
              norm1_g, w_in, rnn_conv_w, rnn_conv_b, w_rg_a, b_rg_a, w_rg_i, b_rg_i, rg_lambda, w_rnn_proj,
              conf_conv_w, conf_conv_b, conf_ln_g, conf_ln_b, w_conv_proj, w_out, norm2_g, w_group, b_group,
              w_erouter, b_erouter, w_exp_gate, w_exp_up, w_exp_down, final_norm_g):
    weights = (norm1_g, w_in, rnn_conv_w, rnn_conv_b, w_rg_a, b_rg_a, w_rg_i, b_rg_i, rg_lambda, w_rnn_proj,
               conf_conv_w, conf_conv_b, conf_ln_g, conf_ln_b, w_conv_proj, w_out, norm2_g, w_group, b_group,
               w_erouter, b_erouter, w_exp_gate, w_exp_up, w_exp_down, final_norm_g)
    bsz = x_prompt.shape[0]
    meta = jnp.broadcast_to(meta_tokens.astype(x_prompt.dtype)[None], (bsz, N_META, D_MODEL))
    xp = jnp.concatenate([meta, x_prompt], axis=1)
    h0 = jnp.zeros((DEPTH, bsz, D_RNN), jnp.float32)
    c4_0 = jnp.zeros((DEPTH, bsz, RNN_CONV_W - 1, D_RNN), x_prompt.dtype)
    c31_0 = jnp.zeros((DEPTH, bsz, CONF_CONV_W - 1, D_CONV), x_prompt.dtype)
    yp, h_p, c4_p, c31_p = _trunk(xp, h0, c4_0, c31_0, *weights)
    ys, h_s, c4_s, c31_s = _trunk(x_sample, state_rglru_h, state_rglru_conv, state_conformer_conv, *weights)
    return (yp[:, N_META:], ys, h_p, c4_p, c31_p, h_s, c4_s, c31_s)


_drawn_inputs = setup_inputs


def setup_inputs(seed=0):
    import zlib

    import numpy as np

    out = dict(_drawn_inputs(seed))
    spreads = {}
    factors = {'b_rg_a': 8.0,
     'b_rg_i': 6.546,
     'conf_ln_g': 3.615,
     'conf_ln_b': 8.234,
     'b_group': 18.108,
     'b_erouter': 5.942,
     'final_norm_g': 7.68,
     'norm2_g': 3.048}
    for name, (base, spread) in spreads.items():
        noise = np.random.default_rng([zlib.crc32(name.encode()), seed]).standard_normal(out[name].shape)
        drawn = base * np.exp(spread * noise) if base else spread * noise
        out[name] = __import__('jax').numpy.asarray(drawn.astype(out[name].dtype))
    for name, factor in factors.items():
        out[name] = (out[name] * factor).astype(out[name].dtype)
    return out
```

```python
from contextlib import ExitStack

import numpy as np

import concourse.bass as bass
from concourse import mybir

ALU = mybir.AluOpType
ACT = mybir.ActivationFunctionType
F32 = mybir.dt.float32
I32 = mybir.dt.int32
BF16 = mybir.dt.bfloat16
AX_X = mybir.AxisListType.X

P = 128
D = 1024
KT = D // P
N_META = 16
SEQ = 256
TP = N_META + SEQ
NS, TS = 8, 4
T = TP + NS * TS
ROWS = (P, P, T - 2 * P)
NT = len(ROWS)
RW, CW = 4, 31
UXP, UXS = RW - 1 + TP, RW - 1 + TS
UXN = UXP + NS * UXS
GLP, GLS = CW - 1 + TP, CW - 1 + TS
GLN = GLP + NS * GLS
HS = TS + 1
HN = TP + NS * HS
NG, EG = 4, 8
NE = NG * EG
F = D // 4
FT = F // P
EPS = 1e-6
SLOTS = 2 * T
PT = -(-SLOTS // P)
C = 96
XS = SLOTS + C
BIG = 3.0e38
WB = 512
MB = WB // P
MIX_SLOTS = 4
EXP_SLOTS = 4
BLOCK_WORDS = KT * WB
HB = KT // 2
LRU_C = 8.0
WORK = 19616
MAX_PASSES = -(-T // C)
PASS_STEPS = 25
ST_DMAS = 6 + NS
WO_BANKS = (0, 1, 2, 3, 6, 7)
EXP_WORDS = 2 * KT * F + FT * D


class Steps:

    def __init__(self, eng, sem, base=0):
        self.eng, self.sem, self.base, self.n = eng, sem, base, 0

    def __call__(self, ins):
        self.n += 1
        ins.then_inc(self.sem, 1)
        self.eng.wait_ge(self.sem, self.base + self.n)


def trunk(nc, a, o):
    with ExitStack() as ctx:
        def sem(name):
            return ctx.enter_context(nc.semaphore(name))

        def sb(name, n, dt=F32):
            return ctx.enter_context(nc.sbuf_tensor(name, [P, n], dt))[:, :]

        bank = [ctx.enter_context(nc.psum_tensor(f"bank{i}", [P, 512], F32))[:, :] for i in range(8)]

        ring = sb("ring", EXP_SLOTS * EXP_WORDS)
        x = sb("x", NT * D).rearrange("p (t d) -> p t d", t=NT)
        work = sb("work", WORK)

        def cutter(buf, size):
            at = [0]

            def cut(n, at0=None):
                lo = at[0] if at0 is None else at0
                assert lo + n <= size, (lo + n, size)
                at[0] = lo + n
                return buf[:, lo:lo + n]
            return cut

        def chan(ap):
            return ap.rearrange("p (c n) -> p c n", c=KT)

        cut = cutter(work, WORK)
        xnT = chan(cut(KT * T))
        ux = chan(cut(KT * UXN))
        xc = chan(cut(KT * HN))
        glu = chan(cut(KT * GLN))
        cc = chan(cut(KT * T))
        gel = chan(cut(KT * T))
        h = chan(cut(KT * HN))
        sq = xnT
        sgr = chan(cut(KT * T, KT * T))
        sgc = chan(cut(KT * T, KT * (T + UXN)))
        cut = cutter(work, WORK)
        xn2 = cut(NT * D).rearrange("p (t d) -> p t d", t=NT)
        xs_f = cut(KT * XS)
        xs, xT2 = chan(xs_f), chan(xs_f[:, 0:KT * T])
        yrow = xs_f[:, 0:PT * D].rearrange("p (j d) -> p j d", j=PT)
        ys = chan(cut(KT * XS))
        sel = cut(NT * SLOTS).rearrange("p (t n) -> p t n", t=NT)
        junk = sel.rearrange("p t n -> p (t n)")[:, 0:D]
        wsel = cut(2 * SLOTS).rearrange("p (b n) -> p b n", b=2)
        wT = cut(PT * T)
        logit = cut((NG + NE) * NT).rearrange("p (t e) -> p t e", t=NT)
        el, oh1, oh2, rank, inw, rtmp = (cut(NE * NT).rearrange("p (t e) -> p t e", t=NT) for _ in range(6))
        goh, gtmp, gex = (cut(NG * NT).rearrange("p (t e) -> p t e", t=NT) for _ in range(3))
        rbias = sb("rbias", NG + NE)
        cnt, cwin, off = (sb(n, NE) for n in ("cnt", "cwin", "off"))
        off_i, npass = sb("off_i", NE, I32), sb("npass", 4, I32)
        pick = sb("pick", NT * 10).rearrange("p (k t) -> p k t", k=10)
        rbase, fpass, valid = sb("rbase", 1), sb("fpass", 2), sb("valid", NT)
        mo = sb("mo", NE * NT, BF16).rearrange("p (t e) -> p t e", t=NT)
        gpri, epri = sb("gpri", NG), sb("epri", NE)

        cut = cutter(ring, EXP_SLOTS * EXP_WORDS)
        mix_w = [cut(BLOCK_WORDS).rearrange("p (k n) -> p k n", k=KT) for _ in range(MIX_SLOTS)]
        gate_r, gate_i, tau, dec, inp = (cut(HB * HN).rearrange("p (c n) -> p c n", c=HB) for _ in range(5))
        cv_sb, sg_sb = (cut(2 * T).rearrange("p (b n) -> p b n", b=2) for _ in range(2))
        xn = ring[:, 2 * BLOCK_WORDS:2 * BLOCK_WORDS + NT * D].rearrange("p (t d) -> p t d", t=NT)
        cut(0, 3 * BLOCK_WORDS)
        prow = cut(6 * P).rearrange("p (i n) -> p i n", i=6)
        crow = cut(16 * P).rearrange("p (i n) -> p i n", i=16)
        e0 = [(EXP_SLOTS - 1 - s) * EXP_WORDS for s in range(EXP_SLOTS)]
        w_gu = [[ring[:, e0[s] + m * KT * F:e0[s] + (m + 1) * KT * F].rearrange("p (k m j) -> p k j m", k=KT, j=FT)
                 for m in range(2)] for s in range(EXP_SLOTS)]
        w_gu_flat = [[ring[:, e0[s] + m * KT * F:e0[s] + (m + 1) * KT * F] for m in range(2)] for s in range(EXP_SLOTS)]
        w_dn_flat = [ring[:, e0[s] + 2 * KT * F:e0[s] + EXP_WORDS] for s in range(EXP_SLOTS)]
        w_dn = [w.rearrange("p (j n) -> p j n", j=FT) for w in w_dn_flat]

        wbd_f = sb("gate_weights", 2 * KT * P)
        wbd = wbd_f.rearrange("p (g c n) -> p g c n", g=2, c=KT)
        g2_bc, gf_bc = wbd_f[:, 0:D], wbd_f[:, D:2 * D]
        cut = cutter(wbd_f, 2 * KT * P)
        st_ux, st_uxp, st_h, st_glup, st_glu = (cut(n) for n in (
            NS * (RW - 1) * KT, (RW - 1) * KT, NS * KT, (CW - 1) * KT, NS * TS * KT))
        par = sb("par", 408)
        pn1, pccb, plg, plb, prcb, pba, pbi, plam = (par[:, i * KT:(i + 1) * KT] for i in range(8))
        prw = par[:, 64:96].rearrange("p (w c) -> p w c", w=RW)
        pcw = par[:, 96:344].rearrange("p (w c) -> p w c", w=CW)
        ph0 = par[:, 344:408].rearrange("p (s c) -> p s c", s=NS)
        wr = par[:, 0:KT * (NG + NE)].rearrange("p (j e) -> p j e", j=KT)
        win = sb("windows", NS * TS * CW)
        win4 = win.rearrange("p (s t w) -> p s t w", s=NS, t=TS)
        iota = win[:, 0:SLOTS]
        hid = [win[:, SLOTS + b * FT * C:SLOTS + (b + 1) * FT * C].rearrange("p (f n) -> p f n", f=FT) for b in range(2)]
        cv4 = sb("conv4", UXN)
        outst = sb("outst", 9 * P)
        sg2 = [outst[:, b * FT * C:(b + 1) * FT * C].rearrange("p (f n) -> p f n", f=FT) for b in range(2)]
        wtmp = outst[:, 2 * FT * C:2 * FT * C + SLOTS]
        ident, ones_d = sb("ident", P), sb("ones_d", P)
        tri, ones_b = sb("tri", P, BF16), sb("ones_b", P, BF16)
        lam = sb("lam", 5 * KT).rearrange("p (i c) -> p i c", i=5)
        stat = sb("stat", 18)

        (par_in, cst_in, wbd_in, router_in, g_in, consts, zeros, dconst, dstep, astep, pstep, rstep,
         ss_done, ms_done, rs_done, xn_done, par_T, par_done, rst_T, rst_done, cst_T, cst_done, xT_done, xnT_done,
         lam_e, kappa_done, tile_mm, tile_act, tile_dve, glu_done, win_done, win_used, conv_done, xc_done,
         gate_mm, gate_act, dec_done, vsq_done, vrt_done, inp_done, scan_done, gelu_done, prod_done,
         st_cp, st_T, st_ev, st_out, mean_mm, cen_done, sq_done, var_mm, var_done, std_done, nrm_done, silu_done,
         merged, wo_mm, x1_done, ss2_done, ms2_done, rs2_done, xn2_done, xT2_mm, xT2_act, xT2_dve,
         log_mm, mo_done, ex_req, ex_done, pick_done, rank_mm, iota_done, sel_done, gat_mm, gat_act, gat_dve,
         wsel_done, wT_used, wT_done, gu_mm, silu2, hid_done, dn_mm, ys_act, ys_dve,
         yT_mm, yT_act, yT_dve, y_mm, y_done, x2_done, ss3_done, ms3_done, rs3_done, fin_done, y_out) = (sem(n) for n in (
            "par_in cst_in wbd_in router_in g_in consts zeros dconst dstep astep pstep rstep "
            "ss_done ms_done rs_done xn_done par_T par_done rst_T rst_done cst_T cst_done xT_done xnT_done "
            "lam_e kappa_done tile_mm tile_act tile_dve glu_done win_done win_used conv_done xc_done "
            "gate_mm gate_act dec_done vsq_done vrt_done inp_done scan_done gelu_done prod_done "
            "st_cp st_T st_ev st_out mean_mm cen_done sq_done var_mm var_done std_done nrm_done silu_done "
            "merged wo_mm x1_done ss2_done ms2_done rs2_done xn2_done xT2_mm xT2_act xT2_dve "
            "log_mm mo_done ex_req ex_done pick_done rank_mm iota_done sel_done gat_mm gat_act gat_dve "
            "wsel_done wT_used wT_done gu_mm silu2 hid_done dn_mm ys_act ys_dve "
            "yT_mm yT_act yT_dve y_mm y_done x2_done ss3_done ms3_done rs3_done fin_done y_out").split())
        x_in = [sem(f"x_in{t}") for t in range(NT)]
        mix_in = [sem(f"mix_in{s}") for s in range(MIX_SLOTS)]
        gu_in = [sem(f"gu_in{s}") for s in range(EXP_SLOTS)]
        dn_in = [sem(f"dn_in{s}") for s in range(EXP_SLOTS)]

        w_in = a["w_in"][0]
        first = {"ux": 0, "uy": D, "cv": 2 * D, "cg": 3 * D, "gr": 4 * D, "gc": 5 * D}
        after = {"rp": a["w_rnn_proj"][0], "cp": a["w_conv_proj"][0], "wo": a["w_out"][0]}
        blocks = [(k, i) for i in range(2) for k in ("cv", "cg")]
        blocks += [(k, i) for k in ("ux", "uy", "gr", "gc", "rp", "cp", "wo") for i in range(2)]
        NBLK = len(blocks)
        tiles = [(k, c) for c in range(KT) for k in ("cv", "cg")]
        tiles += [(k, c) for k in ("ux", "uy", "gr", "gc", "rp", "cp") for c in range(KT)]
        tile_at = {t: m for m, t in enumerate(tiles)}
        NACT = len(tiles) - 2 * KT

        def block_src(k, i):
            w = after[k][:, i * WB:(i + 1) * WB] if k in after else w_in[:, first[k] + i * WB:first[k] + (i + 1) * WB]
            return w.rearrange("(k p) n -> p k n", p=P)

        def seqs(ap, at, stride, lo, n):
            return ap[:, at:at + NS * stride].rearrange("p (s j) -> p s j", s=NS)[:, :, lo:lo + n]

        def state_cols(buf, at, stride):
            return buf[:, :, at:at + NS * stride].rearrange("p c (s j) -> p s j c", s=NS)

        def weight_block(j, t):
            return (t * PT + j) * P if t < NT - 1 else (NT - 1) * PT * P + j * ROWS[t]

        def block_used(b):
            k, i = blocks[b]
            return (wo_mm, (i + 1) * NT) if k == "wo" else (tile_mm, tile_at[k, i * MB + MB - 1] + 1)

        def wT_parts(i):
            runs = []
            for t in range(NT):
                for j in range(PT):
                    lo = weight_block(j, t) - 512 * i
                    if 0 <= lo < 512:
                        k = min(P, SLOTS - j * P)
                        if runs and runs[-1][2] == k:
                            runs[-1][1] = lo + ROWS[t]
                        else:
                            runs.append([lo, lo + ROWS[t], k])
            return runs

        block = ctx.enter_context(nc.Block())

        @block.sync
        def _(sp):
            sp.dma_start(x[0:N_META, 0], a["meta_tokens"]).then_inc(x_in[0], 16)
            sp.dma_start(x[N_META:P, 0], a["x_prompt"][0, 0:P - N_META]).then_inc(x_in[0], 16)
            sp.dma_start(x[:, 1], a["x_prompt"][0, P - N_META:2 * P - N_META]).then_inc(x_in[1], 16)
            sp.dma_start(x[0:TP - 2 * P, 2], a["x_prompt"][0, 2 * P - N_META:]).then_inc(x_in[2], 16)
            sp.dma_start(x[TP - 2 * P:ROWS[2], 2], a["x_sample"].rearrange("s t d -> (s t) d")).then_inc(x_in[2], 16)

            def load_block(b):
                if b == 2:
                    sp.wait_ge(xT_done, KT)
                if b == 3:
                    sp.wait_ge(cst_T, 4)
                if b >= MIX_SLOTS:
                    sp.wait_ge(*block_used(b - MIX_SLOTS))
                sp.dma_start(mix_w[b % MIX_SLOTS], block_src(*blocks[b])).then_inc(mix_in[b % MIX_SLOTS], 16)

            def load_expert(e, s):
                for m, n in enumerate(("w_exp_gate", "w_exp_up")):
                    sp.dma_start(w_gu_flat[s][m], a[n][0, bass.ds(e, 1)].rearrange("e (p k) f -> p (e k f)", p=P))\
                      .then_inc(gu_in[s], 16)
                sp.dma_start(w_dn_flat[s], a["w_exp_down"][0, bass.ds(e, 1)].rearrange("e (p k) n -> p (e k n)", p=P))\
                  .then_inc(dn_in[s], 16)

            for b in range(NBLK - 6):
                load_block(b)
            sp.wait_ge(scan_done, KT)
            sp.wait_ge(glu_done, KT)
            load_expert(0, 0)
            for b in range(NBLK - 6, NBLK):
                load_block(b)
            for e in range(1, EXP_SLOTS):
                last = min(MIX_SLOTS, -(-(e0[e] + EXP_WORDS) // BLOCK_WORDS)) - 1
                b = max(b for b in range(NBLK) if e0[e] // BLOCK_WORDS <= b % MIX_SLOTS <= last)
                sp.wait_ge(*block_used(b))
                load_expert(e, e)
            with sp.Fori(1, NE // EXP_SLOTS) as g:
                for s in range(EXP_SLOTS):
                    sp.wait_ge(dn_mm, g * EXP_SLOTS + (s + 1 - EXP_SLOTS))
                    load_expert(g * EXP_SLOTS + s, s)
            sp.wait_ge(pick_done, 1)
            passes = sp.value_load(npass[0:1, 0:1], min_val=1, max_val=MAX_PASSES)
            with sp.If(passes > 1):
                with sp.Fori(1, passes) as r:
                    with sp.Fori(0, NE // EXP_SLOTS) as g:
                        for s in range(EXP_SLOTS):
                            sp.wait_ge(dn_mm, r * NE + g * EXP_SLOTS + (s + 1 - EXP_SLOTS))
                            load_expert(g * EXP_SLOTS + s, s)
            with sp.Else():
                sp.nop()
            for t in range(NT):
                sp.wait_ge(fin_done, t + 1)
                if t == 0:
                    sp.dma_start(o["y_p"][0, 0:P - N_META], x[N_META:P, 0]).then_inc(y_out, 16)
                elif t == 1:
                    sp.dma_start(o["y_p"][0, P - N_META:2 * P - N_META], x[:, 1]).then_inc(y_out, 16)
                else:
                    sp.dma_start(o["y_p"][0, 2 * P - N_META:], x[0:TP - 2 * P, 2]).then_inc(y_out, 16)
                    sp.dma_start(o["y_s"].rearrange("s t d -> (s t) d"), x[TP - 2 * P:ROWS[2], 2]).then_inc(y_out, 16)
            sp.wait_ge(y_out, 16 * 4)
            sp.wait_ge(st_out, 16 * ST_DMAS)

        @block.gpsimd
        def _(pool):
            step = Steps(pool, pstep)
            step(nc.gpsimd.memset(ident, 0.0))
            nc.gpsimd.affine_select(out=ident, in_=ident, compare_op=ALU.not_equal, fill=1.0, base=0,
                                    pattern=[[-1, P]], channel_multiplier=1).then_inc(consts, 1)
            nc.gpsimd.memset(wbd_f, 0.0).then_inc(zeros, 1)
            step(nc.gpsimd.memset(tri, 1.0))
            nc.gpsimd.affine_select(out=tri, in_=tri, compare_op=ALU.is_gt, fill=0.0, base=0,
                                    pattern=[[1, P]], channel_multiplier=-1).then_inc(consts, 1)
            step(nc.gpsimd.memset(valid, 1.0))
            nc.gpsimd.affine_select(out=valid[:, NT - 1:NT], in_=valid[:, NT - 1:NT], compare_op=ALU.is_gt, fill=0.0,
                                    base=ROWS[-1], pattern=[[0, 1]], channel_multiplier=-1).then_inc(consts, 1)
            nc.gpsimd.iota(gpri, [[-1, NG]], base=NG, channel_multiplier=0,
                           allow_small_or_imprecise_dtypes=True).then_inc(consts, 1)
            nc.gpsimd.iota(epri, [[-1, NE]], base=NE, channel_multiplier=0,
                           allow_small_or_imprecise_dtypes=True).then_inc(consts, 1)

            for c in range(KT):
                pool.wait_ge(tile_act, 2 * c + 2)
                nc.gpsimd.tensor_tensor(glu[:, c, CW - 1:GLP], cv_sb[:, c % 2, 0:TP], sg_sb[:, c % 2, 0:TP], ALU.mult)
                nc.gpsimd.tensor_tensor(seqs(glu[:, c], GLP, GLS, CW - 1, TS), seqs(cv_sb[:, c % 2], TP, TS, 0, TS),
                                        seqs(sg_sb[:, c % 2], TP, TS, 0, TS), ALU.mult).then_inc(glu_done, 1)

            def gated_input(b):
                pool.wait_ge(gate_act, HB * (b + 1))
                if b:
                    pool.wait_ge(scan_done, HB)
                nc.gpsimd.tensor_tensor(inp, gate_i, xc[:, b * HB:(b + 1) * HB], ALU.mult).then_inc(inp_done, 1)

            def windows(c):
                if c == 0:
                    pool.wait_ge(cst_done, NS)
                    pool.wait_ge(glu_done, KT)
                else:
                    pool.wait_ge(win_used, c)
                g = glu[:, c, GLP:GLN].rearrange("p (s j) -> p s j", s=NS)
                for t in range(TS):
                    ins = nc.gpsimd.tensor_tensor(win4[:, :, t, :], g[:, :, t:t + CW],
                                                  pcw[:, :, c].unsqueeze(1).broadcast_to([P, NS, CW]), ALU.mult)
                ins.then_inc(win_done, 1)

            gated_input(0)
            windows(0)
            gated_input(1)
            pool.wait_ge(gate_mm, KT)
            nc.gpsimd.tensor_copy(st_ux.rearrange("p (s r c) -> p s r c", s=NS, r=RW - 1),
                                  state_cols(ux, UXP, UXS)[:, :, UXS - RW + 1:UXS])
            nc.gpsimd.tensor_copy(st_uxp.rearrange("p (r c) -> p c r", c=KT), ux[:, :, UXP - RW + 1:UXP]).then_inc(st_cp, 1)
            windows(1)
            pool.wait_ge(scan_done, KT)
            nc.gpsimd.tensor_copy(st_h.rearrange("p (s c) -> p s c", s=NS), state_cols(h, TP, HS)[:, :, HS - 1])
            nc.gpsimd.tensor_copy(st_glup.rearrange("p (r c) -> p c r", c=KT), glu[:, :, GLP - CW + 1:GLP])
            nc.gpsimd.tensor_copy(st_glu.rearrange("p (s r c) -> p s r c", s=NS, r=TS),
                                  state_cols(glu, GLP, GLS)[:, :, CW - 1:GLS]).then_inc(st_cp, 1)
            for c in range(2, KT):
                windows(c)
            pool.wait_ge(gelu_done, 1)
            pool.wait_ge(scan_done, KT)
            for c in range(KT):
                nc.gpsimd.tensor_tensor(gel[:, c, 0:TP], gel[:, c, 0:TP], h[:, c, 0:TP], ALU.mult)
                nc.gpsimd.tensor_tensor(seqs(gel[:, c], TP, TS, 0, TS), seqs(gel[:, c], TP, TS, 0, TS),
                                        seqs(h[:, c], TP, HS, 1, TS), ALU.mult).then_inc(prod_done, 1)
            pool.wait_ge(win_used, KT)
            nc.gpsimd.iota(iota, [[1, SLOTS]], base=1, channel_multiplier=0,
                           allow_small_or_imprecise_dtypes=True).then_inc(iota_done, 1)
            for c in range(KT):
                pool.wait_ge(tile_dve, KT + c + 1)
                nc.gpsimd.tensor_tensor(sgr[:, c], sgr[:, c], sgc[:, c], ALU.add).then_inc(merged, 1)
            nc.gpsimd.memset(ys[:, 0:KT // 2], 0.0).then_inc(ys_act, 1)
            nc.gpsimd.memset(ys[:, KT // 2:], 0.0).then_inc(ys_dve, 1)

        @block.scalar
        def _(act):
            for i, n in enumerate(("norm1_g", "conf_conv_b", "conf_ln_g", "conf_ln_b",
                                   "rnn_conv_b", "b_rg_a", "b_rg_i", "rg_lambda")):
                act.dma_start(prow[i * KT:(i + 1) * KT, 0], a[n][0].rearrange("(c p) -> c p", p=P)).then_inc(par_in, 16)
            act.dma_start(prow[64:96, 0], a["rnn_conv_w"][0].rearrange("w (c p) -> (w c) p", p=P)).then_inc(par_in, 16)
            act.dma_start(prow[0:124, 1:3], a["conf_conv_w"][0].rearrange("w (c p) -> (w c) p", p=P)
                          .rearrange("(i r) p -> r i p", i=2)).then_inc(par_in, 16)
            act.dma_start(prow[0:64, 3], a["state_rglru_h"][0].rearrange("s (c p) -> (s c) p", p=P)).then_inc(par_in, 16)
            act.dma_start(prow[0:96, 4:6], a["state_rglru_conv"][0].rearrange("s r (c p) -> (s r c) p", p=P)
                          .rearrange("(i q) p -> q i p", i=2)).then_inc(par_in, 16)
            act.dma_start(crow[0:120], a["state_conformer_conv"][0].rearrange("s r (c p) -> (s r c) p", p=P)
                          .rearrange("(i q) p -> q i p", i=16)).then_inc(cst_in, 16)
            act.wait_ge(zeros, 1)
            for g, n in enumerate(("w_rg_a", "w_rg_i")):
                for e in range(2):
                    act.dma_start(wbd[64 * e:64 * e + 64, g, :, 64 * e:64 * e + 64],
                                  a[n][0].rearrange("(c e) i j -> e i c j", e=2)[e]).then_inc(wbd_in, 16)
            act.dma_start(o["cc_s"][0][:, 0:CW - 1 - TS], a["state_conformer_conv"][0][:, TS:]).then_inc(st_out, 16)

            act.wait_ge(dconst, 1)
            for t in range(NT):
                act.wait_ge(x_in[t], 16 if t == 1 else 32)
                nc.scalar.activation(xn[0:ROWS[t], t], x[0:ROWS[t], t], ACT.Square,
                                     accum_out=stat[0:ROWS[t], t:t + 1]).then_inc(ss_done, 1)
            act.wait_ge(ms_done, 1)
            nc.scalar.activation(stat[:, 3:6], stat[:, 3:6], ACT.Sqrt).then_inc(rs_done, 1)
            act.wait_ge(par_done, 1)
            nc.scalar.activation(lam[:, 0], plam, ACT.Abs).then_inc(astep, 1)
            act.wait_ge(astep, 1)
            nc.scalar.activation(lam[:, 0], lam[:, 0], ACT.Exp, scale=-1.0).then_inc(lam_e, 1)

            def tile(m):
                k, c = tiles[m]
                act.wait_ge(tile_mm, m + 1)
                b = bank[m % 4][:, 0:T]
                if k == "cv":
                    if c >= 2:
                        act.wait_ge(glu_done, c - 1)
                    ins = nc.scalar.activation(cv_sb[:, c % 2], b, ACT.Copy)
                elif k == "cg":
                    ins = nc.scalar.activation(sg_sb[:, c % 2], b, ACT.Sigmoid)
                elif k == "ux":
                    nc.scalar.activation(ux[:, c, RW - 1:UXP], b[:, 0:TP], ACT.Copy)
                    ins = nc.scalar.activation(seqs(ux[:, c], UXP, UXS, RW - 1, TS), seqs(b, TP, TS, 0, TS), ACT.Copy)
                elif k == "uy":
                    ins = nc.scalar.activation(gel[:, c], b, ACT.Copy)
                elif k == "gr":
                    if c == 0:
                        act.wait_ge(st_cp, 1)
                        act.wait_ge(xc_done, KT)
                    ins = nc.scalar.activation(sgr[:, c], b, ACT.Sigmoid)
                else:
                    if c == 0:
                        act.wait_ge(inp_done, 2)
                    ins = nc.scalar.activation(sgc[:, c], b, ACT.Sigmoid)
                ins.then_inc(tile_act, 1)

            def gates(c):
                act.wait_ge(gate_mm, c + 1)
                if c == HB:
                    act.wait_ge(inp_done, 1)
                    act.wait_ge(vsq_done, 1)
                q = 4 + 2 * (c % 2)
                nc.scalar.activation(gate_r[:, c % HB], bank[q][:, 0:HN], ACT.Sigmoid, bias=pba[:, c:c + 1])
                nc.scalar.activation(gate_i[:, c % HB], bank[q + 1][:, 0:HN], ACT.Sigmoid,
                                     bias=pbi[:, c:c + 1]).then_inc(gate_act, 1)

            def decay(b):
                act.wait_ge(gate_act, HB * (b + 1))
                if b:
                    act.wait_ge(scan_done, HB)
                else:
                    act.wait_ge(kappa_done, 1)
                for c in range(HB):
                    ch = b * HB + c
                    nc.scalar.activation(tau[:, c], gate_r[:, c], ACT.Tanh, scale=lam[:, 1, ch:ch + 1])
                    ins = nc.scalar.activation(dec[:, c], gate_r[:, c], ACT.Exp, scale=lam[:, 2, ch:ch + 1])
                ins.then_inc(dec_done, 1)

            def root(b):
                act.wait_ge(vsq_done, b + 1)
                nc.scalar.activation(tau, tau, ACT.Sqrt).then_inc(vrt_done, 1)

            for m in range(NACT):
                tile(m)
                k, c = tiles[m]
                if k == "ux" and c >= 2:
                    gates(c - 2)
                if k == "uy" and c < 2:
                    gates(c + 6)
                if (k, c) == ("ux", 5):
                    decay(0)
                if (k, c) == ("ux", 6):
                    root(0)
                if (k, c) == ("uy", 2):
                    decay(1)
                if (k, c) == ("uy", 4):
                    root(1)
                if (k, c) == ("uy", 7):
                    act.wait_ge(tile_act, m + 1)
                    nc.scalar.activation(gel, gel, ACT.Gelu_apprx_tanh).then_inc(gelu_done, 1)
            act.wait_ge(cen_done, 1)
            nc.scalar.activation(sq, cc, ACT.Square).then_inc(sq_done, 1)
            act.wait_ge(var_done, 1)
            nc.scalar.activation(sq[:, 0], sq[:, 0], ACT.Sqrt).then_inc(std_done, 1)
            act.wait_ge(nrm_done, 1)
            for c in range(KT):
                nc.scalar.activation(cc[:, c], cc[:, c], ACT.Silu, scale=plg[:, c:c + 1],
                                     bias=plb[:, c:c + 1]).then_inc(silu_done, 1)
            act.wait_ge(st_ev, 3)
            act.dma_start(o["rc_s"][0].rearrange("s r (c p) -> (s r c) p", p=P).rearrange("(i q) p -> q i p", i=2),
                          outst[0:96, 0:2 * P].rearrange("q (i p) -> q i p", i=2)).then_inc(st_out, 16)
            act.dma_start(o["rc_p"][0, 0].rearrange("r (c p) -> (r c) p", p=P), outst[0:24, 2 * P:3 * P]).then_inc(st_out, 16)
            act.dma_start(o["h_p"][0, 0].rearrange("(c p) -> c p", p=P), outst[0:KT, 3 * P:4 * P]).then_inc(st_out, 16)
            act.dma_start(o["h_s"][0].rearrange("s (c p) -> (s c) p", p=P), outst[0:NS * KT, 4 * P:5 * P]).then_inc(st_out, 16)
            act.dma_start(o["cc_p"][0, 0].rearrange("r (c p) -> (r c) p", p=P).rearrange("(i q) p -> q i p", i=2),
                          outst[0:120, 5 * P:7 * P].rearrange("q (i p) -> q i p", i=2)).then_inc(st_out, 16)
            for s in range(NS):
                act.dma_start(o["cc_s"][0, s, CW - 1 - TS:].rearrange("t (c p) -> (t c) p", p=P),
                              outst[32 * (s % 4):32 * (s % 4) + 32, (7 + s // 4) * P:(8 + s // 4) * P]).then_inc(st_out, 16)
            act.wait_ge(st_T, 3)
            act.dma_start(g2_bc, a["norm2_g"][0:1, :].broadcast_to([P, D])).then_inc(g_in, 16)
            act.dma_start(gf_bc, a["final_norm_g"].unsqueeze(0).broadcast_to([P, D])).then_inc(g_in, 16)
            act.wait_ge(silu_done, KT)
            act.wait_ge(conv_done, KT)
            act.dma_start(wr[:, :, 0:NG], a["w_group"][0].rearrange("(p j) e -> p j e", p=P)).then_inc(router_in, 16)
            act.dma_start(wr[:, :, NG:], a["w_erouter"][0].rearrange("(p j) e -> p j e", p=P)).then_inc(router_in, 16)
            act.dma_start(rbias[:, 0:NG], a["b_group"][0:1, :].broadcast_to([P, NG])).then_inc(router_in, 16)
            act.dma_start(rbias[:, NG:], a["b_erouter"][0].rearrange("g e -> (g e)").unsqueeze(0).broadcast_to([P, NE]))\
               .then_inc(router_in, 16)
            for t in range(NT):
                act.wait_ge(x1_done, NT + t + 1)
                if t:
                    act.wait_ge(ss2_done, t)
                nc.scalar.activation(junk[0:ROWS[t]], x[0:ROWS[t], t], ACT.Square,
                                     accum_out=stat[0:ROWS[t], 6 + t:7 + t]).then_inc(ss2_done, 1)
            act.wait_ge(ms2_done, 1)
            nc.scalar.activation(stat[:, 9:12], stat[:, 9:12], ACT.Sqrt).then_inc(rs2_done, 1)
            for j in range(1, KT, 2):
                act.wait_ge(xT2_mm, j + 1)
                nc.scalar.activation(xT2[:, j], bank[j % 4][:, 0:T], ACT.Copy).then_inc(xT2_act, 1)
            act.wait_ge(ex_req, 1)
            nc.scalar.activation(gex, gex, ACT.Exp)
            nc.scalar.activation(pick[:, 3], pick[:, 2], ACT.Exp).then_inc(ex_done, 1)

            act.wait_ge(pick_done, 1)
            passes = act.value_load(npass[0:1, 0:1], min_val=1, max_val=MAX_PASSES)
            with act.Fori(0, passes) as r:
                for q in range(1, 2 * KT, 2):
                    act.wait_ge(gat_mm, r * (2 * KT) + (q + 1))
                    nc.scalar.activation(xs[:, q // 2, T:2 * T], bank[q % 4][:, 0:T], ACT.Copy).then_inc(gat_act, 1)

                with act.Fori(0, NE // EXP_SLOTS) as g:
                    def results(s):
                        act.wait_ge(dn_mm, r * NE + g * EXP_SLOTS + (s + 1))
                        act.wait_ge(ys_act, r * NE + g * EXP_SLOTS + (s + 1))
                        at = act.value_load(off_i[0:1, bass.ds(g * EXP_SLOTS + s, 1)], min_val=0, max_val=SLOTS)
                        nc.scalar.activation(ys[:, 0:4, bass.ds(at, C)],
                                             bank[2 + 2 * (s % 2)][:, 0:4 * C].rearrange("p (m n) -> p m n", m=4),
                                             ACT.Copy).then_inc(ys_act, 1)

                    for s in range(EXP_SLOTS):
                        act.wait_ge(gu_mm, r * NE + g * EXP_SLOTS + (s + 1))
                        nc.scalar.activation(sg2[s % 2], bank[s % 2][:, 0:2 * C].rearrange("p (f n) -> p f n", f=FT),
                                             ACT.Silu).then_inc(silu2, 1)
                        if s >= 1:
                            results(s - 1)
                    results(EXP_SLOTS - 1)
                for q in range(0, 2 * PT, 2):
                    w = min(P, SLOTS - q // 2 * P)
                    act.wait_ge(yT_mm, r * (2 * PT) + (q + 1))
                    nc.scalar.activation(yrow[0:w, q // 2, 0:512], bank[0][0:w], ACT.Copy).then_inc(yT_act, 1)
            for t in range(NT):
                act.wait_ge(x2_done, 1)
                if t:
                    act.wait_ge(ss3_done, t)
                nc.scalar.activation(junk[0:ROWS[t]], x[0:ROWS[t], t], ACT.Square,
                                     accum_out=stat[0:ROWS[t], 12 + t:13 + t]).then_inc(ss3_done, 1)
            act.wait_ge(ms3_done, 1)
            nc.scalar.activation(stat[:, 15:18], stat[:, 15:18], ACT.Sqrt).then_inc(rs3_done, 1)

        @block.vector
        def _(dve):
            step = Steps(dve, dstep)
            vec = nc.vector

            def bc(ap, n):
                return ap.unsqueeze(2).broadcast_to([P, NT, n])

            def bt(ap, n):
                return ap.unsqueeze(1).broadcast_to([P, NT, n])

            vec.memset(ones_b, 1.0)
            vec.memset(ones_d, 1.0 / D)
            vec.memset(ux[:, :, 0:RW - 1], 0.0)
            vec.memset(glu[:, :, 0:CW - 1], 0.0)
            vec.memset(xc[:, :, TP:HN].rearrange("p c (s j) -> p c s j", s=NS)[:, :, :, 0], 0.0)
            vec.memset(rbase, 0.0)
            vec.memset(stat, 1.0).then_inc(dconst, 1)

            def inverse_root(i, done, ms, rs):
                dve.wait_ge(done, NT)
                vec.tensor_scalar(stat[:, i + 3:i + 6], stat[:, i:i + 3], 1.0 / D, EPS, ALU.mult, ALU.add).then_inc(ms, 1)
                dve.wait_ge(rs, 1)
                step(vec.reciprocal(stat[:, i + 3:i + 6], stat[:, i + 3:i + 6]))

            inverse_root(0, ss_done, ms_done, rs_done)
            for t in range(NT):
                vec.tensor_scalar(xn[0:ROWS[t], t], x[0:ROWS[t], t], stat[0:ROWS[t], 3 + t:4 + t], None,
                                  ALU.mult).then_inc(xn_done, 1)
            dve.wait_ge(par_T, 1)
            vec.tensor_copy(par, bank[0][:, 0:408]).then_inc(par_done, 1)
            dve.wait_ge(rst_T, 1)
            vec.tensor_copy(state_cols(ux, UXP, UXS)[:, :, 0:RW - 1],
                            bank[1][:, 0:192].rearrange("p (s r c) -> p s r c", s=NS, r=RW - 1)).then_inc(rst_done, 1)
            dve.wait_ge(par_done, 1)
            for j in range(KT):
                dve.wait_ge(xT_done, j + 1)
                vec.tensor_scalar(xnT[:, j], bank[4 + j % 4][:, 0:T], pn1[:, j:j + 1], None, ALU.mult).then_inc(xnT_done, 1)
            for s in range(NS):
                dve.wait_ge(cst_T, s // 2 + 1)
                at = GLP + s * GLS
                b = bank[(2, 3, 0, 1)[s // 2]][:, 240 * (s % 2):240 * (s % 2) + 240]
                vec.tensor_copy(glu[:, :, at:at + CW - 1], b.rearrange("p (r c) -> p c r", c=KT)).then_inc(cst_done, 1)

            dve.wait_ge(lam_e, 1)
            e, z, z2, q = lam[:, 0], lam[:, 3], lam[:, 4], lam[:, 1]
            step(vec.tensor_scalar(z, e, 2.0, None, ALU.add))
            step(vec.reciprocal(z, z))
            step(vec.tensor_tensor(z, z, e, ALU.mult))
            step(vec.tensor_tensor(z2, z, z, ALU.mult))
            step(vec.tensor_scalar(q, z2, 1.0 / 17, None, ALU.mult))
            for k in range(7, 0, -1):
                step(vec.scalar_tensor_tensor(q, q, 1.0 / (2 * k + 1), z2, ALU.add, ALU.mult))
            step(vec.scalar_tensor_tensor(q, q, 1.0, z, ALU.add, ALU.mult))
            step(vec.tensor_scalar(z, plam, -1.0, 0.0, ALU.mult, ALU.max))
            step(vec.scalar_tensor_tensor(q, q, 2.0, z, ALU.mult, ALU.add))
            step(vec.tensor_scalar(lam[:, 2], q, -LRU_C, None, ALU.mult))
            vec.tensor_scalar(lam[:, 1], q, LRU_C, None, ALU.mult).then_inc(kappa_done, 1)

            def conv_prompt(c):
                dve.wait_ge(glu_done, c + 1)
                y = cc[:, c, 0:TP]
                step(vec.tensor_scalar(y, glu[:, c, 0:TP], pcw[:, 0, c:c + 1], pccb[:, c:c + 1], ALU.mult, ALU.add))
                for w in range(1, CW):
                    ins = vec.scalar_tensor_tensor(y, glu[:, c, w:w + TP], pcw[:, w, c:c + 1], y, ALU.mult, ALU.add)
                    step(ins)

            def conv_samples(c):
                y = cc[:, c, TP:T]
                dve.wait_ge(win_done, c + 1)
                ins = vec.tensor_reduce(y, win.rearrange("p (n w) -> p n w", w=CW), AX_X, ALU.add)
                ins.then_inc(win_used, 1)
                dve.wait_ge(win_used, c + 1)
                vec.tensor_scalar(y, y, pccb[:, c:c + 1], None, ALU.add).then_inc(conv_done, 1)

            def conv_rnn(c):
                dve.wait_ge(tile_act, tile_at["ux", c] + 1)
                n = UXN - RW + 1
                v = cv4[:, 0:n]
                if c:
                    dve.wait_ge(xc_done, c)
                step(vec.tensor_scalar(v, ux[:, c, 0:n], prw[:, 0, c:c + 1], prcb[:, c:c + 1], ALU.mult, ALU.add))
                for w in range(1, RW - 1):
                    step(vec.scalar_tensor_tensor(v, ux[:, c, w:w + n], prw[:, w, c:c + 1], v, ALU.mult, ALU.add))
                w3 = prw[:, RW - 1, c:c + 1]
                vec.scalar_tensor_tensor(xc[:, c, 0:TP], ux[:, c, RW - 1:UXP], w3, v[:, 0:TP], ALU.mult, ALU.add)
                vec.scalar_tensor_tensor(seqs(xc[:, c], TP, HS, 1, TS), seqs(ux[:, c], UXP, UXS, RW - 1, TS), w3,
                                         seqs(cv4, UXP, UXS, 0, TS), ALU.mult, ALU.add).then_inc(xc_done, 1)

            def variance(b):
                dve.wait_ge(dec_done, b + 1)
                step(vec.tensor_tensor(gate_r, dec, dec, ALU.mult))
                vec.scalar_tensor_tensor(tau, gate_r, 1.0, tau, ALU.add, ALU.mult).then_inc(vsq_done, 1)

            def scans(b):
                dve.wait_ge(inp_done, b + 1)
                dve.wait_ge(vrt_done, b + 1)
                dve.wait_ge(vsq_done, b + 1)
                step(vec.tensor_tensor(inp, inp, tau, ALU.mult))
                step(vec.memset(dec[:, :, TP:HN].rearrange("p c (s j) -> p c s j", s=NS)[:, :, :, 0], 0.0))
                step(vec.tensor_copy(inp[:, :, TP:HN].rearrange("p c (s j) -> p s j c", s=NS)[:, :, 0],
                                     ph0[:, :, b * HB:(b + 1) * HB]))
                for c in range(HB):
                    vec.tensor_tensor_scan(h[:, b * HB + c], dec[:, c], inp[:, c], 0.0, ALU.mult, ALU.add)\
                       .then_inc(scan_done, 1)

            def tile(k, c):
                m = tile_at[k, c]
                g = sgr if k == "rp" else sgc
                dve.wait_ge(tile_mm, m + 1)
                dve.wait_ge(tile_act, tile_at["gr" if k == "rp" else "gc", c] + 1)
                vec.tensor_tensor(g[:, c], bank[m % 4][:, 0:T], g[:, c], ALU.mult).then_inc(tile_dve, 1)

            dve.wait_ge(dconst, 1)
            for c in range(4):
                conv_prompt(c)
            dve.wait_ge(rst_done, 1)
            for c in range(6):
                conv_rnn(c)
            variance(0)
            for c in range(6, KT):
                conv_rnn(c)
            scans(0)
            conv_samples(0)
            variance(1)
            scans(1)
            conv_prompt(4)
            conv_samples(1)
            conv_prompt(5)
            conv_samples(2)
            conv_prompt(6)
            conv_samples(3)
            conv_prompt(7)
            for c in range(4, KT):
                conv_samples(c)
            dve.wait_ge(st_T, 1)
            vec.tensor_copy(outst[0:96, 0:2 * P], bank[4][0:96, 0:2 * P])
            vec.tensor_copy(outst[0:24, 2 * P:3 * P], bank[4][0:24, 2 * P:3 * P]).then_inc(st_ev, 1)
            dve.wait_ge(st_T, 2)
            vec.tensor_copy(outst[0:KT, 3 * P:4 * P], bank[5][0:KT, 0:P])
            vec.tensor_copy(outst[0:NS * KT, 4 * P:5 * P], bank[5][0:NS * KT, P:2 * P]).then_inc(st_ev, 1)
            dve.wait_ge(st_T, 3)
            vec.tensor_copy(outst[0:120, 5 * P:7 * P], bank[6][0:120, 0:2 * P])
            vec.tensor_copy(outst[:, 7 * P:9 * P], bank[6][:, 2 * P:4 * P]).then_inc(st_ev, 1)

            dve.wait_ge(mean_mm, 1)
            vec.tensor_tensor(cc, cc, bank[4][:, 0:T].unsqueeze(1).broadcast_to([P, KT, T]), ALU.subtract)\
               .then_inc(cen_done, 1)
            for c in range(3):
                tile("rp", c)
            dve.wait_ge(var_mm, 1)
            vec.tensor_scalar(sq[:, 0], bank[5][:, 0:T], EPS, None, ALU.add).then_inc(var_done, 1)
            tile("rp", 3)
            dve.wait_ge(std_done, 1)
            step(vec.reciprocal(sq[:, 0], sq[:, 0]))
            vec.tensor_tensor(cc, cc, sq[:, 0].unsqueeze(1).broadcast_to([P, KT, T]), ALU.mult).then_inc(nrm_done, 1)
            for c in range(4, KT):
                tile("rp", c)
            for c in range(KT):
                tile("cp", c)

            for n in range(2):
                for t in range(NT):
                    dve.wait_ge(wo_mm, n * NT + t + 1)
                    xt = x[0:ROWS[t], t, n * 512:(n + 1) * 512]
                    vec.tensor_tensor(xt, bank[WO_BANKS[n * NT + t]][0:ROWS[t]], xt, ALU.add).then_inc(x1_done, 1)
            inverse_root(6, ss2_done, ms2_done, rs2_done)
            dve.wait_ge(g_in, 32)
            for t in range(NT):
                vec.scalar_tensor_tensor(xn2[0:ROWS[t], t], x[0:ROWS[t], t], stat[0:ROWS[t], 9 + t:10 + t],
                                         g2_bc[0:ROWS[t]], ALU.mult, ALU.mult).then_inc(xn2_done, 1)
            vec.memset(logit, 0.0).then_inc(dconst, 1)
            for j in range(0, KT, 2):
                dve.wait_ge(xT2_mm, j + 1)
                vec.tensor_copy(xT2[:, j], bank[j % 4][:, 0:T]).then_inc(xT2_dve, 1)

            dve.wait_ge(log_mm, 1)
            dve.wait_ge(router_in, 64)
            dve.wait_ge(dconst, 2)
            for t in range(NT):
                ins = vec.tensor_tensor(logit[0:ROWS[t], t], bank[5][0:ROWS[t], t * 36:(t + 1) * 36],
                                        rbias[0:ROWS[t]], ALU.add)
                step(ins)
            dve.wait_ge(consts, 5)
            gl, m0, m1, dm, ex = logit[:, :, 0:NG], pick[:, 0], pick[:, 1], pick[:, 2], pick[:, 3]
            pos1, pos2, w1, w2, m2 = pick[:, 4], pick[:, 5], pick[:, 6], pick[:, 7], pick[:, 8]

            def first_of(oh, src, m, pri, n):
                step(vec.tensor_reduce(m, src, AX_X, ALU.max))
                step(vec.tensor_tensor(oh, src, bc(m, n), ALU.is_equal))
                step(vec.tensor_tensor(oh, oh, bt(pri, n), ALU.mult))
                step(vec.tensor_reduce(pick[:, 9], oh, AX_X, ALU.max))
                step(vec.tensor_tensor(oh, oh, bc(pick[:, 9], n), ALU.is_equal))

            first_of(goh, gl, m0, gpri, NG)
            step(vec.tensor_tensor(gex, gl, bc(m0, NG), ALU.subtract))
            step(vec.tensor_scalar(gtmp, goh, -1.0, BIG, ALU.add, ALU.mult))
            by_group = lambda ap: ap.rearrange("p t (g e) -> p t g e", g=NG)
            over = lambda ap: ap.unsqueeze(3).broadcast_to([P, NT, NG, EG])
            step(vec.tensor_tensor(by_group(el), by_group(logit[:, :, NG:]), over(goh), ALU.mult))
            step(vec.tensor_tensor(by_group(el), by_group(el), over(gtmp), ALU.add))
            first_of(oh1, el, m1, epri, NE)
            step(vec.scalar_tensor_tensor(el, oh1, -BIG, el, ALU.mult, ALU.add))
            first_of(oh2, el, m2, epri, NE)
            vec.tensor_tensor(dm, m2, m1, ALU.subtract).then_inc(ex_req, 1)
            step(vec.tensor_tensor(rtmp, oh1, oh2, ALU.add))
            vec.tensor_tensor(mo, rtmp, bc(valid, NE), ALU.mult).then_inc(mo_done, 1)
            dve.wait_ge(ex_done, 1)
            step(vec.tensor_reduce(m0, gex, AX_X, ALU.add))
            step(vec.tensor_scalar(m1, ex, 1.0, None, ALU.add))
            step(vec.tensor_tensor(m0, m0, m1, ALU.mult))
            step(vec.reciprocal(w1, m0))
            step(vec.tensor_tensor(w2, w1, ex, ALU.mult))
            dve.wait_ge(rank_mm, 1)
            step(vec.tensor_copy(rank, bank[6][:, 0:NE * NT].rearrange("p (t e) -> p t e", t=NT)))
            step(vec.tensor_copy(cnt, bank[6][:, NE * NT:NE * (NT + 1)]))
            step(vec.tensor_reduce(fpass[:, 0:1], cnt, AX_X, ALU.max))
            step(vec.tensor_scalar(fpass[:, 1:2], fpass[:, 0:1], float(C), 1.0, ALU.is_gt, ALU.add))
            for i in range(2, MAX_PASSES):
                step(vec.scalar_tensor_tensor(fpass[:, 1:2], fpass[:, 0:1], float(C * i), fpass[:, 1:2], ALU.is_gt, ALU.add))
            vec.tensor_copy(npass[:, 0:1], fpass[:, 1:2]).then_inc(pick_done, 1)
            dve.wait_ge(iota_done, 1)
            dve.wait_ge(st_out, 16 * ST_DMAS)
            dve.wait_ge(pick_done, 1)
            passes = dve.value_load(npass[0:1, 0:1], min_val=1, max_val=MAX_PASSES)

            with dve.Fori(0, passes) as r:
                step = Steps(dve, rstep, r * PASS_STEPS)
                step(vec.memset(xs[:, :, SLOTS:XS], 0.0))
                step(vec.tensor_scalar(rtmp, rank, rbase, None, ALU.subtract))
                step(vec.tensor_scalar(cwin, cnt, rbase, 0.0, ALU.subtract, ALU.max))
                step(vec.tensor_scalar(cwin, cwin, float(C), None, ALU.min))
                step(vec.tensor_tensor_scan(off, ones_b[:, 0:NE], cwin, 0.0, ALU.mult, ALU.add))
                step(vec.tensor_tensor(off, off, cwin, ALU.subtract))
                step(vec.tensor_copy(off_i, off))
                step(vec.scalar_tensor_tensor(inw, rtmp, 0.0, mo, ALU.is_ge, ALU.mult))
                step(vec.scalar_tensor_tensor(inw, rtmp, float(C), inw, ALU.is_lt, ALU.mult))
                step(vec.tensor_tensor(rtmp, rtmp, bt(off, NE), ALU.add))
                step(vec.scalar_tensor_tensor(rtmp, rtmp, 1.0, inw, ALU.add, ALU.mult))
                for oh, pos in ((oh1, pos1), (oh2, pos2)):
                    step(vec.tensor_tensor(inw, rtmp, oh, ALU.mult))
                    step(vec.tensor_reduce(pos, inw, AX_X, ALU.add))
                for t in range(NT):
                    n = ROWS[t]
                    step(vec.tensor_scalar(sel[0:n, t], iota[0:n], pos2[0:n, t:t + 1], None, ALU.is_equal))
                    vec.scalar_tensor_tensor(sel[0:n, t], iota[0:n], pos1[0:n, t:t + 1], sel[0:n, t],
                                             ALU.is_equal, ALU.add).then_inc(sel_done, 1)
                def weights(t):
                    n, w = ROWS[t], wsel[0:ROWS[t], t % 2]
                    if t == NT - 1:
                        dve.wait_ge(wT_used, r * NT + 1)
                    step(vec.tensor_scalar(w, iota[0:n], pos1[0:n, t:t + 1], w1[0:n, t:t + 1], ALU.is_equal, ALU.mult))
                    step(vec.tensor_scalar(wtmp[0:n], iota[0:n], pos2[0:n, t:t + 1], w2[0:n, t:t + 1],
                                           ALU.is_equal, ALU.mult))
                    vec.tensor_tensor(w, w, wtmp[0:n], ALU.add).then_inc(wsel_done, 1)
                    dve.wait_ge(wsel_done, r * NT + (t + 1))

                for q in range(0, 2 * KT, 2):
                    dve.wait_ge(gat_mm, r * (2 * KT) + (q + 1))
                    vec.tensor_copy(xs[:, q // 2, 0:T], bank[q % 4][:, 0:T]).then_inc(gat_dve, 1)
                    if q in (2, 6):
                        weights((q - 2) // 4)
                weights(NT - 1)
                dve.wait_ge(wT_used, r * NT + NT)
                for i in range(3):
                    for lo, hi, k in wT_parts(i):
                        ins = vec.tensor_copy(wT[0:k, 512 * i + lo:512 * i + hi], bank[4 + i][0:k, lo:hi])
                    ins.then_inc(wT_done, 1)

                with dve.Fori(0, NE // EXP_SLOTS) as g:
                    def results(s):
                        dve.wait_ge(dn_mm, r * NE + g * EXP_SLOTS + (s + 1))
                        dve.wait_ge(ys_dve, r * NE + g * EXP_SLOTS + (s + 1))
                        at = dve.value_load(off_i[0:1, bass.ds(g * EXP_SLOTS + s, 1)], min_val=0, max_val=SLOTS)
                        vec.tensor_copy(ys[:, 4:8, bass.ds(at, C)],
                                        bank[3 + 2 * (s % 2)][:, 0:4 * C].rearrange("p (m n) -> p m n", m=4)).then_inc(ys_dve, 1)

                    for s in range(EXP_SLOTS):
                        dve.wait_ge(silu2, r * NE + g * EXP_SLOTS + (s + 1))
                        vec.tensor_tensor(hid[s % 2], bank[s % 2][:, 2 * C:4 * C].rearrange("p (f n) -> p f n", f=FT),
                                          sg2[s % 2], ALU.mult).then_inc(hid_done, 1)
                        if s >= 1:
                            results(s - 1)
                    results(EXP_SLOTS - 1)
                for q in range(1, 2 * PT, 2):
                    w = min(P, SLOTS - q // 2 * P)
                    dve.wait_ge(yT_mm, r * (2 * PT) + (q + 1))
                    vec.tensor_copy(yrow[0:w, q // 2, 512:1024], bank[1][0:w]).then_inc(yT_dve, 1)
                for t in range(NT):
                    for n in range(2):
                        dve.wait_ge(y_mm, r * (2 * NT) + (2 * t + n + 1))
                        xt = x[0:ROWS[t], t, n * 512:(n + 1) * 512]
                        vec.tensor_tensor(xt, bank[2 + 2 * t + n][0:ROWS[t]], xt, ALU.add).then_inc(y_done, 1)
                step(vec.tensor_scalar(rbase, rbase, float(C), None, ALU.add))
                assert step.n == PASS_STEPS, step.n

            dve.nop().then_inc(x2_done, 1)
            dve.wait_ge(ss3_done, NT)
            vec.tensor_scalar(stat[:, 15:18], stat[:, 12:15], 1.0 / D, EPS, ALU.mult, ALU.add).then_inc(ms3_done, 1)
            dve.wait_ge(rs3_done, 1)
            vec.reciprocal(stat[:, 15:18], stat[:, 15:18]).then_inc(ms3_done, 1)
            dve.wait_ge(ms3_done, 2)
            for t in range(NT):
                xt = x[0:ROWS[t], t]
                vec.scalar_tensor_tensor(xt, xt, stat[0:ROWS[t], 15 + t:16 + t], gf_bc[0:ROWS[t]],
                                         ALU.mult, ALU.mult).then_inc(fin_done, 1)

        @block.tensor
        def _(pe):
            mm, tp = nc.tensor.matmul, nc.tensor.transpose

            pe.wait_ge(consts, 1)
            pe.wait_ge(par_in, 16 * 12)
            for n, i, at in ((96, 0, 0), (124, 1, 96), (124, 2, 220), (64, 3, 344)):
                ins = tp(bank[0][:, at:at + n], prow[0:n, i], ident[0:n, 0:n])
            ins.then_inc(par_T, 1)
            for i in range(2):
                ins = tp(bank[1][:, 96 * i:96 * i + 96], prow[0:96, 4 + i], ident[0:96, 0:96])
            ins.then_inc(rst_T, 1)

            def conf_states(g):
                for i in range(4):
                    ins = tp(bank[(2, 3, 0, 1)[g]][:, 120 * i:120 * i + 120], crow[0:120, 4 * g + i], ident[0:120, 0:120])
                ins.then_inc(cst_T, 1)

            pe.wait_ge(cst_in, 16)
            conf_states(0)
            conf_states(1)
            pe.wait_ge(xn_done, NT)
            for j in range(KT):
                if j >= 4:
                    pe.wait_ge(xnT_done, j - 3)
                for t in range(NT):
                    n = ROWS[t]
                    ins = tp(bank[4 + j % 4][:, t * P:t * P + n], xn[0:n, t, j * P:(j + 1) * P], ident[0:n, 0:n])
                ins.then_inc(xT_done, 1)
            pe.wait_ge(par_done, 1)
            conf_states(2)
            pe.wait_ge(rst_done, 1)
            conf_states(3)
            pe.wait_ge(xnT_done, KT)
            pe.wait_ge(cst_done, NS)

            def tile(m):
                k, c = tiles[m]
                b = blocks.index((k, c // MB))
                if c % MB == 0:
                    pe.wait_ge(mix_in[b % MIX_SLOTS], 16 * (b // MIX_SLOTS + 1))
                if m >= 4:
                    if m - 4 < NACT:
                        pe.wait_ge(tile_act, m - 3)
                    else:
                        pe.wait_ge(tile_dve, m - 3 - NACT)
                src = {"rp": gel, "cp": cc}.get(k, xnT)
                for i in range(KT):
                    if k == "rp" and c == 0:
                        pe.wait_ge(prod_done, i + 1)
                    if k == "cp" and c == 0:
                        pe.wait_ge(silu_done, i + 1)
                    ins = mm(bank[m % 4][:, 0:T], mix_w[b % MIX_SLOTS][:, i, (c % MB) * P:(c % MB + 1) * P], src[:, i],
                             start=(i == 0), stop=(i == KT - 1))
                ins.then_inc(tile_mm, 1)

            def gates(c):
                q = 4 + 2 * (c % 2)
                pe.wait_ge(xc_done, c + 1)
                if c == 0:
                    pe.wait_ge(wbd_in, 64)
                if c >= 2:
                    pe.wait_ge(gate_act, c - 1)
                mm(bank[q][:, 0:HN], wbd[:, 0, c], xc[:, c], start=True, stop=True)
                mm(bank[q + 1][:, 0:HN], wbd[:, 1, c], xc[:, c], start=True, stop=True).then_inc(gate_mm, 1)

            for m in range(len(tiles)):
                k, c = tiles[m]
                if (k, c) == ("gc", 0):
                    pe.wait_ge(gate_act, KT)
                    pe.wait_ge(st_cp, 2)
                    for i in range(2):
                        tp(bank[4][0:96, i * P:(i + 1) * P], st_ux[:, 96 * i:96 * i + 96], ident)
                    tp(bank[4][0:24, 2 * P:3 * P], st_uxp, ident).then_inc(st_T, 1)
                    tp(bank[5][0:KT, 0:P], h[:, :, TP - 1], ident)
                    tp(bank[5][0:NS * KT, P:2 * P], st_h, ident).then_inc(st_T, 1)
                    for i in range(2):
                        tp(bank[6][0:120, i * P:(i + 1) * P], st_glup[:, 120 * i:120 * i + 120], ident)
                    for i in range(2):
                        ins = tp(bank[6][:, (2 + i) * P:(3 + i) * P], st_glu[:, i * P:(i + 1) * P], ident)
                    ins.then_inc(st_T, 1)
                if (k, c) == ("rp", 0):
                    pe.wait_ge(conv_done, KT)
                    pe.wait_ge(st_ev, 2)
                    for i in range(KT):
                        ins = mm(bank[4][:, 0:T], ones_d, cc[:, i], start=(i == 0), stop=(i == KT - 1))
                    ins.then_inc(mean_mm, 1)
                if (k, c) == ("rp", 3):
                    pe.wait_ge(sq_done, 1)
                    for i in range(KT):
                        ins = mm(bank[5][:, 0:T], ones_d, sq[:, i], start=(i == 0), stop=(i == KT - 1))
                    ins.then_inc(var_mm, 1)
                tile(m)
                if k == "ux" and c >= 2:
                    gates(c - 2)
                if k == "uy" and c < 2:
                    gates(c + 6)

            pe.wait_ge(st_ev, 3)
            for n in range(2):
                b = blocks.index(("wo", n))
                pe.wait_ge(mix_in[b % MIX_SLOTS], 16 * (b // MIX_SLOTS + 1))
                for t in range(NT):
                    q = WO_BANKS[n * NT + t]
                    if q < 4:
                        pe.wait_ge(tile_dve, 2 * KT - 3 + q)
                    for i in range(KT):
                        if n == 0 and t == 0:
                            pe.wait_ge(merged, i + 1)
                        ins = mm(bank[WO_BANKS[n * NT + t]][0:ROWS[t]], sgr[:, i, t * P:t * P + ROWS[t]],
                                 mix_w[b % MIX_SLOTS][:, i], start=(i == 0), stop=(i == KT - 1))
                    ins.then_inc(wo_mm, 1)

            xj = xn2.rearrange("p t (m j) -> p t j m", j=KT)
            for j in range(KT):
                if j == 0:
                    pe.wait_ge(xn2_done, NT)
                if j >= 4:
                    pe.wait_ge(xT2_dve if j % 2 == 0 else xT2_act, (j - 4) // 2 + 1)
                for t in range(NT):
                    n = ROWS[t]
                    ins = tp(bank[j % 4][:, t * P:t * P + n], xj[0:n, t, j], ident[0:n, 0:n])
                ins.then_inc(xT2_mm, 1)
            pe.wait_ge(router_in, 64)
            pe.wait_ge(xT2_dve, KT // 2)
            pe.wait_ge(xT2_act, KT // 2)
            for t in range(NT):
                for j in range(KT):
                    ins = mm(bank[5][0:ROWS[t], t * 36:(t + 1) * 36], xT2[:, j, t * P:t * P + ROWS[t]], wr[:, j],
                             start=(j == 0), stop=(j == KT - 1))
            ins.then_inc(log_mm, 1)
            pe.wait_ge(mo_done, 1)
            pe.wait_ge(consts, 2)
            for t in range(NT + 1):
                last = min(t, NT - 1)
                for i in range(last + 1):
                    w = tri if i == t else ones_b
                    ins = mm(bank[6][:, t * NE:(t + 1) * NE], w, mo[:, i], start=(i == 0), stop=(i == last))
            ins.then_inc(rank_mm, 1)

            pe.wait_ge(pick_done, 1)
            passes = pe.value_load(npass[0:1, 0:1], min_val=1, max_val=MAX_PASSES)
            with pe.Fori(0, passes) as r:
                pe.wait_ge(sel_done, r * NT + NT)
                for q in range(2 * KT):
                    if q >= 4:
                        pe.wait_ge(gat_dve if q % 2 == 0 else gat_act, r * KT + ((q - 4) // 2 + 1))
                    for t in range(NT):
                        n = ROWS[t]
                        ins = mm(bank[q % 4][:, 0:T], xj[0:n, t, q // 2], sel[0:n, t, (q % 2) * T:(q % 2 + 1) * T],
                                 start=(t == 0), stop=(t == NT - 1))
                    ins.then_inc(gat_mm, 1)
                for t in range(NT):
                    if t == 0:
                        pe.wait_ge(gat_dve, r * KT + KT)
                        pe.wait_ge(gat_act, r * KT + KT)
                    if t < NT - 1:
                        pe.wait_ge(wsel_done, r * NT + (t + 1))
                    for j in range(PT):
                        if t == NT - 2 and j == PT - 1:
                            pe.wait_ge(wsel_done, r * NT + NT)
                        w = min(P, SLOTS - j * P)
                        at = weight_block(j, t)
                        ins = tp(bank[4 + at // 512][0:w, at % 512:at % 512 + ROWS[t]],
                                 wsel[0:ROWS[t], t % 2, j * P:j * P + w], ident[0:ROWS[t], 0:ROWS[t]])
                    ins.then_inc(wT_used, 1)

                with pe.Fori(0, NE // EXP_SLOTS) as g:
                    def gate_up(s):
                        at = pe.value_load(off_i[0:1, bass.ds(g * EXP_SLOTS + s, 1)], min_val=0, max_val=SLOTS)
                        pe.wait_ge(gu_in[s], r * (32 * NE // EXP_SLOTS) + g * 32 + 32)
                        if s >= 2:
                            pe.wait_ge(hid_done, r * NE + g * EXP_SLOTS + (s - 1))
                        for m in range(2):
                            for f in range(FT):
                                for k in range(KT):
                                    ins = mm(bank[s % 2][:, (2 * m + f) * C:(2 * m + f + 1) * C], w_gu[s][m][:, k, f],
                                             xs[:, k, bass.ds(at, C)], start=(k == 0), stop=(k == KT - 1))
                        ins.then_inc(gu_mm, 1)

                    def down(s):
                        pe.wait_ge(dn_in[s], r * (16 * NE // EXP_SLOTS) + g * 16 + 16)
                        pe.wait_ge(hid_done, r * NE + g * EXP_SLOTS + (s + 1))
                        if s == 1:
                            pe.wait_ge(wT_done, r * 3 + 3)
                        done = r * NE + g * EXP_SLOTS + (1 if s < 2 else s)
                        pe.wait_ge(ys_act, done)
                        pe.wait_ge(ys_dve, done)
                        for m in range(KT):
                            for f in range(FT):
                                ins = mm(bank[2 + 2 * (s % 2) + m // 4][:, (m % 4) * C:(m % 4 + 1) * C],
                                         w_dn[s][:, f, m * P:(m + 1) * P], hid[s % 2][:, f], start=(f == 0), stop=(f == FT - 1))
                        ins.then_inc(dn_mm, 1)

                    gate_up(0)
                    for s in range(1, EXP_SLOTS):
                        gate_up(s)
                        down(s - 1)
                    down(EXP_SLOTS - 1)

                pe.wait_ge(ys_act, r * NE + (NE + 1))
                pe.wait_ge(ys_dve, r * NE + (NE + 1))

                def turn(q):
                    if q >= 2:
                        pe.wait_ge(yT_act if q % 2 == 0 else yT_dve, r * PT + q // 2)
                    j, w = q // 2, min(P, SLOTS - q // 2 * P)
                    for i in range(4):
                        ins = tp(bank[q % 2][0:w, i * P:(i + 1) * P], ys[:, 4 * (q % 2) + i, j * P:j * P + w], ident)
                    ins.then_inc(yT_mm, 1)

                turn(0)
                turn(1)
                for j in range(PT):
                    if j + 1 < PT:
                        turn(2 * j + 2)
                        turn(2 * j + 3)
                    pe.wait_ge(yT_act, r * PT + (j + 1))
                    pe.wait_ge(yT_dve, r * PT + (j + 1))
                    w = min(P, SLOTS - j * P)
                    for t in range(NT):
                        for n in range(2):
                            at = weight_block(j, t)
                            ins = mm(bank[2 + 2 * t + n][0:ROWS[t]], wT[0:w, at:at + ROWS[t]],
                                     yrow[0:w, j, n * 512:(n + 1) * 512], start=(j == 0), stop=(j == PT - 1))
                            if j == PT - 1:
                                ins.then_inc(y_mm, 1)


_OUTS = {"y_p": (1, SEQ, D), "y_s": (NS, TS, D), "h_p": (1, 1, D), "rc_p": (1, 1, RW - 1, D), "cc_p": (1, 1, CW - 1, D),
         "h_s": (1, NS, D), "rc_s": (1, NS, RW - 1, D), "cc_s": (1, NS, CW - 1, D)}


def kernel(**inputs):
    import concourse.bacc as bacc
    from concourse.bass_utils import run_bass_kernel_spmd

    nc = bacc.Bacc("TRN2", target_bir_lowering=False, num_devices=1)
    arrays, a, o = {}, {}, {}
    for name, value in inputs.items():
        arrays[name] = np.ascontiguousarray(value)
        a[name] = nc.dram_tensor(name, arrays[name].shape, F32, kind="ExternalInput").ap()
    for name, shape in _OUTS.items():
        o[name] = nc.dram_tensor(f"out_{name}", shape, F32, kind="ExternalOutput").ap()
    trunk(nc, a, o)
    got = run_bass_kernel_spmd(nc, [arrays], core_ids=[0]).results[0]
    return tuple(got[f"out_{name}"] for name in _OUTS)
```

```python
from contextlib import ExitStack

import numpy as np

import concourse.bass as bass
from concourse import mybir

ALU = mybir.AluOpType
ACT = mybir.ActivationFunctionType
F32 = mybir.dt.float32
F32R = mybir.dt.float32r
I32 = mybir.dt.int32
BF16 = mybir.dt.bfloat16
AX_X = mybir.AxisListType.X

P = 128
D = 1024
KT = D // P
N_META = 16
SEQ = 256
TP = N_META + SEQ
NS, TS = 8, 4
T = TP + NS * TS
ROWS = (P, P, T - 2 * P)
NT = len(ROWS)
RW, CW = 4, 31
UXP, UXS = RW - 1 + TP, RW - 1 + TS
UXN = UXP + NS * UXS
GLP, GLS = CW - 1 + TP, CW - 1 + TS
GLN = GLP + NS * GLS
HS = TS + 1
HN = TP + NS * HS
NG, EG = 4, 8
NE = NG * EG
F = D // 4
FT = F // P
EPS = 1e-6
SLOTS = 2 * T
PT = -(-SLOTS // P)
C = 96
XS = SLOTS + C
BIG = 3.0e38
WB = 512
MB = WB // P
MIX_SLOTS = 4
EXP_SLOTS = 4
BLOCK_WORDS = KT * WB
HB = KT // 2
LRU_C = 8.0
WORK = 19616
MAX_PASSES = -(-T // C)
PASS_STEPS = 26
ST_DMAS = 6 + NS
WO_BANKS = (0, 1, 2, 3, 6, 7)
EXP_WORDS = 2 * KT * F + FT * D


class Steps:

    def __init__(self, eng, sem, base=0):
        self.eng, self.sem, self.base, self.n = eng, sem, base, 0

    def __call__(self, ins):
        self.n += 1
        ins.then_inc(self.sem, 1)
        self.eng.wait_ge(self.sem, self.base + self.n)


def trunk(nc, a, o):
    with ExitStack() as ctx:
        def sem(name):
            return ctx.enter_context(nc.semaphore(name))

        start = {}

        def sb(name, n, dt=F32):
            start[name] = -(-nc.sbuf_base // 32) * 32
            return ctx.enter_context(nc.sbuf_tensor(name, [P, n], dt))[:, :]

        def rounded(name, buf, at, n):
            return nc.alloc_sbuf_tensor_at(name, [P, n], F32R, offset=start[buf] + 4 * at)[:, :]

        def as_f32(ap):
            return ap.bitcast(F32)

        bank = [ctx.enter_context(nc.psum_tensor(f"bank{i}", [P, 512], F32))[:, :] for i in range(8)]

        ring = sb("ring", EXP_SLOTS * EXP_WORDS)
        x = sb("x", NT * D).rearrange("p (t d) -> p t d", t=NT)
        work = sb("work", WORK)

        def cutter(buf, size):
            at = [0]

            def cut(n, at0=None):
                lo = at[0] if at0 is None else at0
                assert lo + n <= size, (lo + n, size)
                at[0] = lo + n
                return buf[:, lo:lo + n]
            return cut

        def chan(ap):
            return ap.rearrange("p (c n) -> p c n", c=KT)

        cut = cutter(work, WORK)
        xnT = chan(cut(KT * T))
        ux = chan(cut(KT * UXN))
        xc = chan(cut(KT * HN))
        glu = chan(cut(KT * GLN))
        cc = chan(cut(KT * T))
        gel = chan(cut(KT * T))
        h = chan(cut(KT * HN))
        sq = xnT
        sgr = chan(cut(KT * T, KT * T))
        sgc = chan(cut(KT * T, KT * (T + UXN)))
        cut = cutter(work, WORK)
        xn2 = cut(NT * D).rearrange("p (t d) -> p t d", t=NT)
        xs_f = cut(KT * XS)
        xs, xT2 = chan(xs_f), chan(xs_f[:, 0:KT * T])
        yrow_hi = rounded("yrow_hi", "work", NT * D, PT * D).rearrange("p (j d) -> p j d", j=PT)
        yrow_lo = rounded("yrow_lo", "ring", 0, PT * D).rearrange("p (j d) -> p j d", j=PT)
        ys = chan(cut(KT * XS))
        junk = cut(NT * SLOTS)[:, 0:D]
        sel = rounded("sel", "work", NT * D + 2 * KT * XS, NT * SLOTS).rearrange("p (t n) -> p t n", t=NT)
        wsel = cut(2 * SLOTS).rearrange("p (b n) -> p b n", b=2)
        cut(PT * T)
        selT = rounded("selT", "work", NT * D + 2 * KT * XS + (NT + 2) * SLOTS, PT * T)
        logit = cut((NG + NE) * NT).rearrange("p (t e) -> p t e", t=NT)
        el, oh1, oh2, rank, inw, rtmp = (cut(NE * NT).rearrange("p (t e) -> p t e", t=NT) for _ in range(6))
        goh, gtmp, gex = (cut(NG * NT).rearrange("p (t e) -> p t e", t=NT) for _ in range(3))
        rbias = sb("rbias", NG + NE)
        cnt, cwin, off = (sb(n, NE) for n in ("cnt", "cwin", "off"))
        off_i, npass = sb("off_i", NE, I32), sb("npass", 4, I32)
        pick = sb("pick", NT * 10).rearrange("p (k t) -> p k t", k=10)
        rbase, fpass, valid = sb("rbase", 1), sb("fpass", 2), sb("valid", NT)
        mo = sb("mo", NE * NT, BF16).rearrange("p (t e) -> p t e", t=NT)
        gpri, epri = sb("gpri", NG), sb("epri", NE)

        cut = cutter(ring, EXP_SLOTS * EXP_WORDS)
        mix_w = [cut(BLOCK_WORDS).rearrange("p (k n) -> p k n", k=KT) for _ in range(MIX_SLOTS)]
        gate_r, gate_i, tau, dec, inp = (cut(HB * HN).rearrange("p (c n) -> p c n", c=HB) for _ in range(5))
        cv_sb, sg_sb = (cut(2 * T).rearrange("p (b n) -> p b n", b=2) for _ in range(2))
        xn = ring[:, 2 * BLOCK_WORDS:2 * BLOCK_WORDS + NT * D].rearrange("p (t d) -> p t d", t=NT)
        cut(0, 3 * BLOCK_WORDS)
        prow = cut(6 * P).rearrange("p (i n) -> p i n", i=6)
        crow = cut(16 * P).rearrange("p (i n) -> p i n", i=16)
        e0 = [(EXP_SLOTS - 1 - s) * EXP_WORDS for s in range(EXP_SLOTS)]
        w_gu = [[ring[:, e0[s] + m * KT * F:e0[s] + (m + 1) * KT * F].rearrange("p (k m j) -> p k j m", k=KT, j=FT)
                 for m in range(2)] for s in range(EXP_SLOTS)]
        w_gu_flat = [[ring[:, e0[s] + m * KT * F:e0[s] + (m + 1) * KT * F] for m in range(2)] for s in range(EXP_SLOTS)]
        w_dn_flat = [ring[:, e0[s] + 2 * KT * F:e0[s] + EXP_WORDS] for s in range(EXP_SLOTS)]
        w_dn = [w.rearrange("p (j n) -> p j n", j=FT) for w in w_dn_flat]

        wbd_f = sb("gate_weights", 2 * KT * P)
        wbd = wbd_f.rearrange("p (g c n) -> p g c n", g=2, c=KT)
        g2_bc, gf_bc = wbd_f[:, 0:D], wbd_f[:, D:2 * D]
        halves = [rounded(f"half{i}", "work", NT * D + KT * XS + i * D, D) for i in range(2 * NT - 1)]
        halves.append(rounded("half5", "gate_weights", 0, D))
        xn2_hi, xn2_lo = halves[:NT], halves[NT:]
        cut = cutter(wbd_f, 2 * KT * P)
        st_ux, st_uxp, st_h, st_glup, st_glu = (cut(n) for n in (
            NS * (RW - 1) * KT, (RW - 1) * KT, NS * KT, (CW - 1) * KT, NS * TS * KT))
        par = sb("par", 408)
        pn1, pccb, plg, plb, prcb, pba, pbi, plam = (par[:, i * KT:(i + 1) * KT] for i in range(8))
        prw = par[:, 64:96].rearrange("p (w c) -> p w c", w=RW)
        pcw = par[:, 96:344].rearrange("p (w c) -> p w c", w=CW)
        ph0 = par[:, 344:408].rearrange("p (s c) -> p s c", s=NS)
        wr = par[:, 0:KT * (NG + NE)].rearrange("p (j e) -> p j e", j=KT)
        g2_row = par[:, KT * (NG + NE):KT * (NG + NE) + KT]
        win = sb("windows", NS * TS * CW)
        win4 = win.rearrange("p (s t w) -> p s t w", s=NS, t=TS)
        iota = win[:, 0:SLOTS]
        hid = [win[:, SLOTS + b * FT * C:SLOTS + (b + 1) * FT * C].rearrange("p (f n) -> p f n", f=FT) for b in range(2)]
        outst = sb("outst", 9 * P)
        cv4 = [sb("conv4", UXN), outst[:, 0:UXN]]
        sg2 = [outst[:, b * FT * C:(b + 1) * FT * C].rearrange("p (f n) -> p f n", f=FT) for b in range(2)]
        wtmp = outst[:, 2 * FT * C:2 * FT * C + SLOTS]
        wpair_t = outst[:, 2 * FT * C + SLOTS:2 * FT * C + SLOTS + NT * PT].rearrange("p (t j) -> p t j", t=NT)
        wpair = outst[:, 2 * FT * C + SLOTS + NT * PT:2 * FT * C + SLOTS + NT * PT + PT]
        ident, ones_d = sb("ident", P), sb("ones_d", P)
        tri, ones_b = sb("tri", P, BF16), sb("ones_b", P, BF16)
        lam = sb("lam", 5 * KT).rearrange("p (i c) -> p i c", i=5)
        stat = sb("stat", 18)

        (par_in, cst_in, wbd_in, router_in, g_in, consts, zeros, dconst, dstep, astep, pstep, rstep,
         ss_done, ms_done, rs_done, xn_done, par_T, par_done, rst_T, rst_done, cst_T, cst_done, xT_done, xnT_done,
         lam_e, kappa_done, tile_mm, tile_act, tile_dve, glu_done, win_done, win_used, conv_done, xc_done,
         gate_mm, gate_act, dec_done, vsq_done, vrt_done, inp_done, scan_done, gelu_done, prod_done,
         st_cp, st_T, st_ev, st_out, mean_mm, cen_done, sq_done, var_mm, var_done, std_done, nrm_done, silu_done,
         merged, wo_mm, x1_done, ss2_done, ms2_done, rs2_done, xn2_done, xT2_mm, xT2_act, xT2_dve,
         log_mm, mo_done, ex_req, ex_done, pick_done, rank_mm, iota_done, sel_done, gat_mm, gat_act, gat_dve,
         wsel_done, wT_used, wT_done, xsc_done, hi_done, lo_done, tail_done, wr_done, gu_mm, silu2, hid_done, dn_mm, ys_act, ys_dve,
         yT_mm, yT_act, yT_dve, y_mm, y_done, x2_done, ss3_done, ms3_done, rs3_done, fin_done, y_out) = (sem(n) for n in (
            "par_in cst_in wbd_in router_in g_in consts zeros dconst dstep astep pstep rstep "
            "ss_done ms_done rs_done xn_done par_T par_done rst_T rst_done cst_T cst_done xT_done xnT_done "
            "lam_e kappa_done tile_mm tile_act tile_dve glu_done win_done win_used conv_done xc_done "
            "gate_mm gate_act dec_done vsq_done vrt_done inp_done scan_done gelu_done prod_done "
            "st_cp st_T st_ev st_out mean_mm cen_done sq_done var_mm var_done std_done nrm_done silu_done "
            "merged wo_mm x1_done ss2_done ms2_done rs2_done xn2_done xT2_mm xT2_act xT2_dve "
            "log_mm mo_done ex_req ex_done pick_done rank_mm iota_done sel_done gat_mm gat_act gat_dve "
            "wsel_done wT_used wT_done xsc_done hi_done lo_done tail_done wr_done gu_mm silu2 hid_done dn_mm ys_act ys_dve "
            "yT_mm yT_act yT_dve y_mm y_done x2_done ss3_done ms3_done rs3_done fin_done y_out").split())
        tap_done = [sem(f"tap_done{b}") for b in range(2)]
        rtap_done = [sem(f"rtap_done{b}") for b in range(2)]
        x_in = [sem(f"x_in{t}") for t in range(NT)]
        mix_in = [sem(f"mix_in{s}") for s in range(MIX_SLOTS)]
        gu_in = [sem(f"gu_in{s}") for s in range(EXP_SLOTS)]
        dn_in = [sem(f"dn_in{s}") for s in range(EXP_SLOTS)]

        w_in = a["w_in"][0]
        first = {"ux": 0, "uy": D, "cv": 2 * D, "cg": 3 * D, "gr": 4 * D, "gc": 5 * D}
        after = {"rp": a["w_rnn_proj"][0], "cp": a["w_conv_proj"][0], "wo": a["w_out"][0]}
        blocks = [(k, i) for i in range(2) for k in ("cv", "cg")]
        blocks += [(k, i) for k in ("ux", "uy", "gr", "gc", "rp", "cp", "wo") for i in range(2)]
        NBLK = len(blocks)
        tiles = [(k, c) for c in range(KT) for k in ("cv", "cg")]
        tiles += [(k, c) for k in ("ux", "uy", "gr", "gc", "rp", "cp") for c in range(KT)]
        tile_at = {t: m for m, t in enumerate(tiles)}
        NACT = len(tiles) - 2 * KT

        def block_src(k, i):
            w = after[k][:, i * WB:(i + 1) * WB] if k in after else w_in[:, first[k] + i * WB:first[k] + (i + 1) * WB]
            return w.rearrange("(k p) n -> p k n", p=P)

        def seqs(ap, at, stride, lo, n):
            return ap[:, at:at + NS * stride].rearrange("p (s j) -> p s j", s=NS)[:, :, lo:lo + n]

        def state_cols(buf, at, stride):
            return buf[:, :, at:at + NS * stride].rearrange("p c (s j) -> p s j c", s=NS)

        def weight_block(j, t):
            return (t * PT + j) * P if t < NT - 1 else (NT - 1) * PT * P + j * ROWS[t]

        def block_used(b):
            k, i = blocks[b]
            return (wo_mm, (i + 1) * NT) if k == "wo" else (tile_mm, tile_at[k, i * MB + MB - 1] + 1)

        def wT_parts(i):
            runs = []
            for t in range(NT):
                for j in range(PT):
                    lo = weight_block(j, t) - 512 * i
                    if 0 <= lo < 512:
                        k = min(P, SLOTS - j * P)
                        if runs and runs[-1][2] == k:
                            runs[-1][1] = lo + ROWS[t]
                        else:
                            runs.append([lo, lo + ROWS[t], k])
            return runs

        block = ctx.enter_context(nc.Block())

        @block.sync
        def _(sp):
            sp.dma_start(x[0:N_META, 0], a["meta_tokens"]).then_inc(x_in[0], 16)
            sp.dma_start(x[N_META:P, 0], a["x_prompt"][0, 0:P - N_META]).then_inc(x_in[0], 16)
            sp.dma_start(x[:, 1], a["x_prompt"][0, P - N_META:2 * P - N_META]).then_inc(x_in[1], 16)
            sp.dma_start(x[0:TP - 2 * P, 2], a["x_prompt"][0, 2 * P - N_META:]).then_inc(x_in[2], 16)
            sp.dma_start(x[TP - 2 * P:ROWS[2], 2], a["x_sample"].rearrange("s t d -> (s t) d")).then_inc(x_in[2], 16)

            for i, n in enumerate(("norm1_g", "conf_conv_b", "conf_ln_g", "conf_ln_b",
                                   "rnn_conv_b", "b_rg_a", "b_rg_i", "rg_lambda")):
                sp.dma_start(prow[i * KT:(i + 1) * KT, 0], a[n][0].rearrange("(c p) -> c p", p=P)).then_inc(par_in, 16)
            sp.dma_start(prow[64:96, 0], a["rnn_conv_w"][0].rearrange("w (c p) -> (w c) p", p=P)).then_inc(par_in, 16)
            sp.dma_start(prow[0:124, 1:3], a["conf_conv_w"][0].rearrange("w (c p) -> (w c) p", p=P)
                          .rearrange("(i r) p -> r i p", i=2)).then_inc(par_in, 16)
            sp.dma_start(prow[0:64, 3], a["state_rglru_h"][0].rearrange("s (c p) -> (s c) p", p=P)).then_inc(par_in, 16)
            sp.dma_start(prow[0:96, 4:6], a["state_rglru_conv"][0].rearrange("s r (c p) -> (s r c) p", p=P)
                          .rearrange("(i q) p -> q i p", i=2)).then_inc(par_in, 16)

            def load_block(b):
                if b == 2:
                    sp.wait_ge(xT_done, KT)
                if b == 3:
                    sp.wait_ge(cst_T, 4)
                if b >= MIX_SLOTS:
                    sp.wait_ge(*block_used(b - MIX_SLOTS))
                sp.dma_start(mix_w[b % MIX_SLOTS], block_src(*blocks[b])).then_inc(mix_in[b % MIX_SLOTS], 16)

            def load_expert(e, s):
                for m, n in enumerate(("w_exp_gate", "w_exp_up")):
                    sp.dma_start(w_gu_flat[s][m], a[n][0, bass.ds(e, 1)].rearrange("e (p k) f -> p (e k f)", p=P))\
                      .then_inc(gu_in[s], 16)
                sp.dma_start(w_dn_flat[s], a["w_exp_down"][0, bass.ds(e, 1)].rearrange("e (p k) n -> p (e k n)", p=P))\
                  .then_inc(dn_in[s], 16)

            for b in range(NBLK - 6):
                load_block(b)
            sp.wait_ge(scan_done, KT)
            sp.wait_ge(glu_done, KT)
            load_expert(0, 0)
            for b in range(NBLK - 6, NBLK):
                load_block(b)
            for e in range(1, EXP_SLOTS):
                last = min(MIX_SLOTS, -(-(e0[e] + EXP_WORDS) // BLOCK_WORDS)) - 1
                b = max(b for b in range(NBLK) if e0[e] // BLOCK_WORDS <= b % MIX_SLOTS <= last)
                sp.wait_ge(*block_used(b))
                load_expert(e, e)
            with sp.Fori(1, NE // EXP_SLOTS) as g:
                for s in range(EXP_SLOTS):
                    sp.wait_ge(dn_mm, g * EXP_SLOTS + (s + 1 - EXP_SLOTS))
                    load_expert(g * EXP_SLOTS + s, s)
            sp.wait_ge(pick_done, 1)
            passes = sp.value_load(npass[0:1, 0:1], min_val=1, max_val=MAX_PASSES)
            with sp.If(passes > 1):
                with sp.Fori(1, passes) as r:
                    for s in range(EXP_SLOTS):
                        sp.wait_ge(y_mm, r * (2 * NT))
                        load_expert(s, s)
                    with sp.Fori(1, NE // EXP_SLOTS) as g:
                        for s in range(EXP_SLOTS):
                            sp.wait_ge(dn_mm, r * NE + g * EXP_SLOTS + (s + 1 - EXP_SLOTS))
                            load_expert(g * EXP_SLOTS + s, s)
            with sp.Else():
                sp.nop()
            for t in range(NT):
                sp.wait_ge(fin_done, t + 1)
                if t == 0:
                    sp.dma_start(o["y_p"][0, 0:P - N_META], x[N_META:P, 0]).then_inc(y_out, 16)
                elif t == 1:
                    sp.dma_start(o["y_p"][0, P - N_META:2 * P - N_META], x[:, 1]).then_inc(y_out, 16)
                else:
                    sp.dma_start(o["y_p"][0, 2 * P - N_META:], x[0:TP - 2 * P, 2]).then_inc(y_out, 16)
                    sp.dma_start(o["y_s"].rearrange("s t d -> (s t) d"), x[TP - 2 * P:ROWS[2], 2]).then_inc(y_out, 16)
            sp.wait_ge(y_out, 16 * 4)
            sp.wait_ge(st_out, 16 * ST_DMAS)

        @block.gpsimd
        def _(pool):
            step = Steps(pool, pstep)
            step(nc.gpsimd.memset(ident, 0.0))
            nc.gpsimd.affine_select(out=ident, in_=ident, compare_op=ALU.not_equal, fill=1.0, base=0,
                                    pattern=[[-1, P]], channel_multiplier=1).then_inc(consts, 1)
            nc.gpsimd.memset(wbd_f, 0.0).then_inc(zeros, 1)
            step(nc.gpsimd.memset(tri, 1.0))
            nc.gpsimd.affine_select(out=tri, in_=tri, compare_op=ALU.is_gt, fill=0.0, base=0,
                                    pattern=[[1, P]], channel_multiplier=-1).then_inc(consts, 1)
            step(nc.gpsimd.memset(valid, 1.0))
            nc.gpsimd.affine_select(out=valid[:, NT - 1:NT], in_=valid[:, NT - 1:NT], compare_op=ALU.is_gt, fill=0.0,
                                    base=ROWS[-1], pattern=[[0, 1]], channel_multiplier=-1).then_inc(consts, 1)
            nc.gpsimd.iota(gpri, [[-1, NG]], base=NG, channel_multiplier=0,
                           allow_small_or_imprecise_dtypes=True).then_inc(consts, 1)
            nc.gpsimd.iota(epri, [[-1, NE]], base=NE, channel_multiplier=0,
                           allow_small_or_imprecise_dtypes=True).then_inc(consts, 1)

            for c in range(KT):
                pool.wait_ge(tile_act, 2 * c + 2)
                nc.gpsimd.tensor_tensor(glu[:, c, CW - 1:GLP], cv_sb[:, c % 2, 0:TP], sg_sb[:, c % 2, 0:TP], ALU.mult)
                nc.gpsimd.tensor_tensor(seqs(glu[:, c], GLP, GLS, CW - 1, TS), seqs(cv_sb[:, c % 2], TP, TS, 0, TS),
                                        seqs(sg_sb[:, c % 2], TP, TS, 0, TS), ALU.mult).then_inc(glu_done, 1)

            def gated_input(b):
                pool.wait_ge(gate_act, HB * (b + 1))
                if b:
                    pool.wait_ge(scan_done, HB)
                nc.gpsimd.tensor_tensor(inp, gate_i, xc[:, b * HB:(b + 1) * HB], ALU.mult).then_inc(inp_done, 1)

            def windows(c):
                if c == 0:
                    pool.wait_ge(cst_done, NS)
                    pool.wait_ge(glu_done, KT)
                else:
                    pool.wait_ge(win_used, c)
                g = glu[:, c, GLP:GLN].rearrange("p (s j) -> p s j", s=NS)
                for t in range(TS):
                    ins = nc.gpsimd.tensor_tensor(win4[:, :, t, :], g[:, :, t:t + CW],
                                                  pcw[:, :, c].unsqueeze(1).broadcast_to([P, NS, CW]), ALU.mult)
                ins.then_inc(win_done, 1)

            gated_input(0)
            windows(0)
            gated_input(1)
            pool.wait_ge(gate_mm, KT)
            nc.gpsimd.tensor_copy(st_ux.rearrange("p (s r c) -> p s r c", s=NS, r=RW - 1),
                                  state_cols(ux, UXP, UXS)[:, :, UXS - RW + 1:UXS])
            nc.gpsimd.tensor_copy(st_uxp.rearrange("p (r c) -> p c r", c=KT), ux[:, :, UXP - RW + 1:UXP]).then_inc(st_cp, 1)
            windows(1)
            pool.wait_ge(scan_done, KT)
            nc.gpsimd.tensor_copy(st_h.rearrange("p (s c) -> p s c", s=NS), state_cols(h, TP, HS)[:, :, HS - 1])
            nc.gpsimd.tensor_copy(st_glup.rearrange("p (r c) -> p c r", c=KT), glu[:, :, GLP - CW + 1:GLP])
            nc.gpsimd.tensor_copy(st_glu.rearrange("p (s r c) -> p s r c", s=NS, r=TS),
                                  state_cols(glu, GLP, GLS)[:, :, CW - 1:GLS]).then_inc(st_cp, 1)
            windows(2)
            windows(3)
            pool.wait_ge(gelu_done, 1)
            pool.wait_ge(scan_done, KT)
            for c in range(KT):
                nc.gpsimd.tensor_tensor(gel[:, c, 0:TP], gel[:, c, 0:TP], h[:, c, 0:TP], ALU.mult)
                nc.gpsimd.tensor_tensor(seqs(gel[:, c], TP, TS, 0, TS), seqs(gel[:, c], TP, TS, 0, TS),
                                        seqs(h[:, c], TP, HS, 1, TS), ALU.mult).then_inc(prod_done, 1)
            for c in range(4, KT):
                windows(c)
            pool.wait_ge(win_used, KT)
            nc.gpsimd.iota(iota, [[1, SLOTS]], base=1, channel_multiplier=0,
                           allow_small_or_imprecise_dtypes=True).then_inc(iota_done, 1)
            for c in range(KT):
                pool.wait_ge(tile_dve, KT + c + 1)
                nc.gpsimd.tensor_tensor(sgr[:, c], sgr[:, c], sgc[:, c], ALU.add).then_inc(merged, 1)
            nc.gpsimd.memset(ys[:, 0:KT // 2], 0.0).then_inc(ys_act, 1)
            nc.gpsimd.memset(ys[:, KT // 2:], 0.0).then_inc(ys_dve, 1)
            pool.wait_ge(g_in, 48)
            for t in range(NT):
                pool.wait_ge(xsc_done, t + 1)
                xt = xn2[0:ROWS[t], t]
                nc.gpsimd.tensor_tensor(xt, xt, g2_bc[0:ROWS[t]], ALU.mult).then_inc(xn2_done, 1)
            pool.wait_ge(xn2_done, NT)
            for t in range(NT):
                n = ROWS[t]
                pool.wait_ge(hi_done, t + 1)
                nc.gpsimd.tensor_tensor(xn2_lo[t][0:n], xn2[0:n, t], as_f32(xn2_hi[t][0:n]), ALU.subtract)\
                  .then_inc(lo_done, 1)
            pool.wait_ge(log_mm, 1)
            nc.gpsimd.memset(xs[:, :, SLOTS:XS], 0.0).then_inc(tail_done, 1)

        @block.scalar
        def _(act):
            act.wait_ge(dconst, 1)
            for t in range(NT):
                act.wait_ge(x_in[t], 16 if t == 1 else 32)
                nc.scalar.activation(xn[0:ROWS[t], t], x[0:ROWS[t], t], ACT.Square,
                                     accum_out=stat[0:ROWS[t], t:t + 1]).then_inc(ss_done, 1)
            act.wait_ge(ms_done, 1)
            nc.scalar.activation(stat[:, 3:6], stat[:, 3:6], ACT.Sqrt).then_inc(rs_done, 1)
            act.dma_start(crow[0:120], a["state_conformer_conv"][0].rearrange("s r (c p) -> (s r c) p", p=P)
                          .rearrange("(i q) p -> q i p", i=16)).then_inc(cst_in, 16)
            act.wait_ge(zeros, 1)
            for g, n in enumerate(("w_rg_a", "w_rg_i")):
                for e in range(2):
                    act.dma_start(wbd[64 * e:64 * e + 64, g, :, 64 * e:64 * e + 64],
                                  a[n][0].rearrange("(c e) i j -> e i c j", e=2)[e]).then_inc(wbd_in, 16)
            act.dma_start(o["cc_s"][0][:, 0:CW - 1 - TS], a["state_conformer_conv"][0][:, TS:]).then_inc(st_out, 16)

            act.wait_ge(par_done, 1)
            nc.scalar.activation(lam[:, 0], plam, ACT.Abs).then_inc(astep, 1)
            act.wait_ge(astep, 1)
            nc.scalar.activation(lam[:, 0], lam[:, 0], ACT.Exp, scale=-1.0).then_inc(lam_e, 1)

            def tile(m):
                k, c = tiles[m]
                act.wait_ge(tile_mm, m + 1)
                b = bank[m % 4][:, 0:T]
                if k == "cv":
                    if c >= 2:
                        act.wait_ge(glu_done, c - 1)
                    ins = nc.scalar.activation(cv_sb[:, c % 2], b, ACT.Copy)
                elif k == "cg":
                    ins = nc.scalar.activation(sg_sb[:, c % 2], b, ACT.Sigmoid)
                elif k == "ux":
                    nc.scalar.activation(ux[:, c, RW - 1:UXP], b[:, 0:TP], ACT.Copy)
                    ins = nc.scalar.activation(seqs(ux[:, c], UXP, UXS, RW - 1, TS), seqs(b, TP, TS, 0, TS), ACT.Copy)
                elif k == "uy":
                    ins = nc.scalar.activation(gel[:, c], b, ACT.Copy)
                elif k == "gr":
                    if c == 0:
                        act.wait_ge(st_cp, 1)
                        act.wait_ge(xc_done, KT)
                    ins = nc.scalar.activation(sgr[:, c], b, ACT.Sigmoid)
                else:
                    if c == 0:
                        act.wait_ge(inp_done, 2)
                    ins = nc.scalar.activation(sgc[:, c], b, ACT.Sigmoid)
                ins.then_inc(tile_act, 1)

            def gates(c):
                act.wait_ge(gate_mm, c + 1)
                if c == HB:
                    act.wait_ge(inp_done, 1)
                    act.wait_ge(vsq_done, 1)
                q = 4 + 2 * (c % 2)
                nc.scalar.activation(gate_r[:, c % HB], bank[q][:, 0:HN], ACT.Sigmoid, bias=pba[:, c:c + 1])
                nc.scalar.activation(gate_i[:, c % HB], bank[q + 1][:, 0:HN], ACT.Sigmoid,
                                     bias=pbi[:, c:c + 1]).then_inc(gate_act, 1)

            def decay(b):
                act.wait_ge(gate_act, HB * (b + 1))
                if b:
                    act.wait_ge(scan_done, HB)
                else:
                    act.wait_ge(kappa_done, 1)
                for c in range(HB):
                    ch = b * HB + c
                    nc.scalar.activation(tau[:, c], gate_r[:, c], ACT.Tanh, scale=lam[:, 1, ch:ch + 1])
                    ins = nc.scalar.activation(dec[:, c], gate_r[:, c], ACT.Exp, scale=lam[:, 2, ch:ch + 1])
                ins.then_inc(dec_done, 1)

            def root(b):
                act.wait_ge(vsq_done, b + 1)
                nc.scalar.activation(tau, tau, ACT.Sqrt).then_inc(vrt_done, 1)

            for m in range(NACT):
                tile(m)
                k, c = tiles[m]
                if k == "ux" and c >= 2:
                    gates(c - 2)
                if k == "uy" and c < 2:
                    gates(c + 6)
                if (k, c) == ("ux", 5):
                    decay(0)
                if (k, c) == ("ux", 6):
                    root(0)
                if (k, c) == ("uy", 2):
                    decay(1)
                if (k, c) == ("uy", 4):
                    root(1)
                if (k, c) == ("uy", 7):
                    act.wait_ge(tile_act, m + 1)
                    nc.scalar.activation(gel, gel, ACT.Gelu_apprx_tanh).then_inc(gelu_done, 1)
            act.wait_ge(cen_done, 1)
            nc.scalar.activation(sq, cc, ACT.Square).then_inc(sq_done, 1)
            act.wait_ge(var_done, 1)
            nc.scalar.activation(sq[:, 0], sq[:, 0], ACT.Sqrt).then_inc(std_done, 1)
            for c in range(KT):
                act.wait_ge(nrm_done, c + 1)
                nc.scalar.activation(cc[:, c], cc[:, c], ACT.Silu, scale=plg[:, c:c + 1],
                                     bias=plb[:, c:c + 1]).then_inc(silu_done, 1)
            act.wait_ge(st_ev, 3)
            act.dma_start(o["rc_s"][0].rearrange("s r (c p) -> (s r c) p", p=P).rearrange("(i q) p -> q i p", i=2),
                          outst[0:96, 0:2 * P].rearrange("q (i p) -> q i p", i=2)).then_inc(st_out, 16)
            act.dma_start(o["rc_p"][0, 0].rearrange("r (c p) -> (r c) p", p=P), outst[0:24, 2 * P:3 * P]).then_inc(st_out, 16)
            act.dma_start(o["h_p"][0, 0].rearrange("(c p) -> c p", p=P), outst[0:KT, 3 * P:4 * P]).then_inc(st_out, 16)
            act.dma_start(o["h_s"][0].rearrange("s (c p) -> (s c) p", p=P), outst[0:NS * KT, 4 * P:5 * P]).then_inc(st_out, 16)
            act.dma_start(o["cc_p"][0, 0].rearrange("r (c p) -> (r c) p", p=P).rearrange("(i q) p -> q i p", i=2),
                          outst[0:120, 5 * P:7 * P].rearrange("q (i p) -> q i p", i=2)).then_inc(st_out, 16)
            for s in range(NS):
                act.dma_start(o["cc_s"][0, s, CW - 1 - TS:].rearrange("t (c p) -> (t c) p", p=P),
                              outst[32 * (s % 4):32 * (s % 4) + 32, (7 + s // 4) * P:(8 + s // 4) * P]).then_inc(st_out, 16)
            act.wait_ge(st_T, 3)
            act.dma_start(g2_bc, a["norm2_g"][0:1, :].broadcast_to([P, D])).then_inc(g_in, 16)
            act.dma_start(gf_bc, a["final_norm_g"].unsqueeze(0).broadcast_to([P, D])).then_inc(g_in, 16)
            act.wait_ge(silu_done, KT)
            act.wait_ge(conv_done, KT)
            act.dma_start(g2_row, a["norm2_g"][0].rearrange("(p j) -> p j", p=P)).then_inc(g_in, 16)
            act.dma_start(wr[:, :, 0:NG], a["w_group"][0].rearrange("(p j) e -> p j e", p=P)).then_inc(router_in, 16)
            act.dma_start(wr[:, :, NG:], a["w_erouter"][0].rearrange("(p j) e -> p j e", p=P)).then_inc(router_in, 16)
            act.dma_start(rbias[:, 0:NG], a["b_group"][0:1, :].broadcast_to([P, NG])).then_inc(router_in, 16)
            act.dma_start(rbias[:, NG:], a["b_erouter"][0].rearrange("g e -> (g e)").unsqueeze(0).broadcast_to([P, NE]))\
               .then_inc(router_in, 16)
            for t in range(NT + 1):
                if t < NT:
                    act.wait_ge(x1_done, NT + t + 1)
                    if t:
                        act.wait_ge(ss2_done, t)
                    nc.scalar.activation(junk[0:ROWS[t]], x[0:ROWS[t], t], ACT.Square,
                                         accum_out=stat[0:ROWS[t], 6 + t:7 + t]).then_inc(ss2_done, 1)
                j = 2 * t + 1
                act.wait_ge(xT2_mm, j + 1)
                nc.scalar.activation(xT2[:, j], bank[j % 4][:, 0:T], ACT.Copy).then_inc(xT2_act, 1)
            act.wait_ge(ms2_done, 1)
            nc.scalar.activation(stat[:, 9:12], stat[:, 9:12], ACT.Sqrt).then_inc(rs2_done, 1)
            act.wait_ge(ms2_done, 2)
            for t in range(NT):
                nc.scalar.activation(xn2[0:ROWS[t], t], x[0:ROWS[t], t], ACT.Copy,
                                     scale=stat[0:ROWS[t], 9 + t:10 + t]).then_inc(xsc_done, 1)

            def high_parts():
                for t in range(NT):
                    n = ROWS[t]
                    nc.scalar.activation(xn2_hi[t][0:n], xn2[0:n, t], ACT.Copy).then_inc(hi_done, 1)

            act.wait_ge(ys_act, 1)
            act.wait_ge(ys_dve, 1)
            act.wait_ge(xn2_done, NT)
            high_parts()
            act.wait_ge(ex_req, 1)
            nc.scalar.activation(gex, gex, ACT.Exp)
            nc.scalar.activation(pick[:, 3], pick[:, 2], ACT.Exp).then_inc(ex_done, 1)

            act.wait_ge(pick_done, 1)
            passes = act.value_load(npass[0:1, 0:1], min_val=1, max_val=MAX_PASSES)
            with act.Fori(0, passes) as r:
                with act.If(r > 0):
                    act.wait_ge(yT_mm, r * (2 * PT))
                    high_parts()
                with act.Else():
                    act.nop()
                for q in range(1, 2 * KT, 2):
                    act.wait_ge(gat_mm, r * (2 * KT) + (q + 1))
                    nc.scalar.activation(xs[:, q // 2, T:2 * T], bank[q % 4][:, 0:T], ACT.Copy).then_inc(gat_act, 1)

                with act.Fori(0, NE // EXP_SLOTS) as g:
                    def results(s):
                        act.wait_ge(dn_mm, r * NE + g * EXP_SLOTS + (s + 1))
                        act.wait_ge(ys_act, r * NE + g * EXP_SLOTS + (s + 1))
                        at = act.value_load(off_i[0:1, bass.ds(g * EXP_SLOTS + s, 1)], min_val=0, max_val=SLOTS)
                        nc.scalar.activation(ys[:, 0:4, bass.ds(at, C)],
                                             bank[2 + 2 * (s % 2)][:, 0:4 * C].rearrange("p (m n) -> p m n", m=4),
                                             ACT.Copy).then_inc(ys_act, 1)

                    for s in range(EXP_SLOTS):
                        act.wait_ge(gu_mm, r * NE + g * EXP_SLOTS + (s + 1))
                        nc.scalar.activation(sg2[s % 2], bank[s % 2][:, 0:2 * C].rearrange("p (f n) -> p f n", f=FT),
                                             ACT.Silu).then_inc(silu2, 1)
                        if s >= 1:
                            results(s - 1)
                    results(EXP_SLOTS - 1)
                act.wait_ge(wT_done, r * 4 + 4)
                for q in range(2 * PT):
                    j, w = q // 2, min(P, SLOTS - q // 2 * P)
                    act.wait_ge(yT_mm, r * (2 * PT) + (q + 1))
                    nc.scalar.activation(yrow_hi[0:w, j, q % 2 * 512:(q % 2 + 1) * 512], bank[q % 2][0:w],
                                         ACT.Copy, scale=wpair[0:w, j:j + 1]).then_inc(yT_act, 1)
            for t in range(NT):
                act.wait_ge(x2_done, 1)
                if t:
                    act.wait_ge(ss3_done, t)
                nc.scalar.activation(junk[0:ROWS[t]], x[0:ROWS[t], t], ACT.Square,
                                     accum_out=stat[0:ROWS[t], 12 + t:13 + t]).then_inc(ss3_done, 1)
            act.wait_ge(ms3_done, 1)
            nc.scalar.activation(stat[:, 15:18], stat[:, 15:18], ACT.Sqrt).then_inc(rs3_done, 1)

        @block.vector
        def _(dve):
            step = Steps(dve, dstep)
            vec = nc.vector

            def bc(ap, n):
                return ap.unsqueeze(2).broadcast_to([P, NT, n])

            def bt(ap, n):
                return ap.unsqueeze(1).broadcast_to([P, NT, n])

            vec.memset(ones_b, 1.0)
            vec.memset(ones_d, 1.0 / D)
            vec.memset(ux[:, :, 0:RW - 1], 0.0)
            vec.memset(glu[:, :, 0:CW - 1], 0.0)
            vec.memset(xc[:, :, TP:HN].rearrange("p c (s j) -> p c s j", s=NS)[:, :, :, 0], 0.0)
            vec.memset(rbase, 0.0)
            vec.memset(stat, 1.0).then_inc(dconst, 1)

            def inverse_root(i, done, ms, rs):
                dve.wait_ge(done, NT)
                vec.tensor_scalar(stat[:, i + 3:i + 6], stat[:, i:i + 3], 1.0 / D, EPS, ALU.mult, ALU.add).then_inc(ms, 1)
                dve.wait_ge(rs, 1)
                step(vec.reciprocal(stat[:, i + 3:i + 6], stat[:, i + 3:i + 6]))

            inverse_root(0, ss_done, ms_done, rs_done)
            for t in range(NT):
                vec.tensor_scalar(xn[0:ROWS[t], t], x[0:ROWS[t], t], stat[0:ROWS[t], 3 + t:4 + t], None,
                                  ALU.mult).then_inc(xn_done, 1)
            dve.wait_ge(par_T, 1)
            vec.tensor_copy(par, bank[0][:, 0:408]).then_inc(par_done, 1)
            dve.wait_ge(rst_T, 1)
            vec.tensor_copy(state_cols(ux, UXP, UXS)[:, :, 0:RW - 1],
                            bank[1][:, 0:192].rearrange("p (s r c) -> p s r c", s=NS, r=RW - 1)).then_inc(rst_done, 1)
            dve.wait_ge(par_done, 1)
            for j in range(KT):
                dve.wait_ge(xT_done, j + 1)
                vec.tensor_scalar(xnT[:, j], bank[4 + j % 4][:, 0:T], pn1[:, j:j + 1], None, ALU.mult).then_inc(xnT_done, 1)
            dve.wait_ge(lam_e, 1)
            e, z, z2, q = lam[:, 0], lam[:, 3], lam[:, 4], lam[:, 1]
            step(vec.tensor_scalar(z, e, 2.0, None, ALU.add))
            step(vec.reciprocal(z, z))
            step(vec.tensor_tensor(z, z, e, ALU.mult))
            step(vec.tensor_tensor(z2, z, z, ALU.mult))
            step(vec.tensor_scalar(q, z2, 1.0 / 17, None, ALU.mult))
            for k in range(7, 0, -1):
                step(vec.scalar_tensor_tensor(q, q, 1.0 / (2 * k + 1), z2, ALU.add, ALU.mult))
            step(vec.scalar_tensor_tensor(q, q, 1.0, z, ALU.add, ALU.mult))
            step(vec.tensor_scalar(z, plam, -1.0, 0.0, ALU.mult, ALU.max))
            step(vec.scalar_tensor_tensor(q, q, 2.0, z, ALU.mult, ALU.add))
            step(vec.tensor_scalar(lam[:, 2], q, -LRU_C, None, ALU.mult))
            vec.tensor_scalar(lam[:, 1], q, LRU_C, None, ALU.mult).then_inc(kappa_done, 1)

            for s in range(NS):
                dve.wait_ge(cst_T, s // 2 + 1)
                at = GLP + s * GLS
                b = bank[4 + s // 2][:, 240 * (s % 2):240 * (s % 2) + 240]
                vec.tensor_copy(glu[:, :, at:at + CW - 1], b.rearrange("p (r c) -> p c r", c=KT)).then_inc(cst_done, 1)

            def conv_prompts(c):
                dve.wait_ge(glu_done, c + 2)
                for w in range(CW):
                    for b in range(2):
                        y, ch = cc[:, c + b, 0:TP], c + b
                        if w:
                            dve.wait_ge(tap_done[b], (c // 2) * CW + w)
                            ins = vec.scalar_tensor_tensor(y, glu[:, ch, w:w + TP], pcw[:, w, ch:ch + 1], y, ALU.mult, ALU.add)
                        else:
                            ins = vec.tensor_scalar(y, glu[:, ch, 0:TP], pcw[:, 0, ch:ch + 1], pccb[:, ch:ch + 1],
                                                    ALU.mult, ALU.add)
                        ins.then_inc(tap_done[b], 1)
                for b in range(2):
                    dve.wait_ge(tap_done[b], (c // 2 + 1) * CW)

            def conv_samples(c):
                y = cc[:, c, TP:T]
                dve.wait_ge(win_done, c + 1)
                ins = vec.tensor_reduce(y, win.rearrange("p (n w) -> p n w", w=CW), AX_X, ALU.add)
                ins.then_inc(win_used, 1)
                dve.wait_ge(win_used, c + 1)
                vec.tensor_scalar(y, y, pccb[:, c:c + 1], None, ALU.add).then_inc(conv_done, 1)

            def conv_rnn(c):
                n = UXN - RW + 1
                for w in range(RW):
                    for b in range(2):
                        ch = c + b
                        v, u, tap = cv4[b][:, 0:n], ux[:, ch, w:w + n], prw[:, w, ch:ch + 1]
                        if w:
                            dve.wait_ge(rtap_done[b], (c // 2) * (RW - 1) + w)
                        else:
                            dve.wait_ge(tile_act, tile_at["ux", ch] + 1)
                            if ch >= 2:
                                dve.wait_ge(xc_done, ch - 1)
                        if w == 0:
                            vec.tensor_scalar(v, u, tap, prcb[:, ch:ch + 1], ALU.mult, ALU.add).then_inc(rtap_done[b], 1)
                        elif w < RW - 1:
                            vec.scalar_tensor_tensor(v, u, tap, v, ALU.mult, ALU.add).then_inc(rtap_done[b], 1)
                        else:
                            vec.scalar_tensor_tensor(xc[:, ch, 0:TP], ux[:, ch, RW - 1:UXP], tap, v[:, 0:TP], ALU.mult, ALU.add)
                            vec.scalar_tensor_tensor(seqs(xc[:, ch], TP, HS, 1, TS), seqs(ux[:, ch], UXP, UXS, RW - 1, TS), tap,
                                                     seqs(cv4[b], UXP, UXS, 0, TS), ALU.mult, ALU.add).then_inc(xc_done, 1)

            def variance(b):
                dve.wait_ge(dec_done, b + 1)
                step(vec.tensor_tensor(gate_r, dec, dec, ALU.mult))
                vec.scalar_tensor_tensor(tau, gate_r, 1.0, tau, ALU.add, ALU.mult).then_inc(vsq_done, 1)

            def scans(b):
                dve.wait_ge(inp_done, b + 1)
                dve.wait_ge(vrt_done, b + 1)
                dve.wait_ge(vsq_done, b + 1)
                step(vec.tensor_tensor(inp, inp, tau, ALU.mult))
                step(vec.memset(dec[:, :, TP:HN].rearrange("p c (s j) -> p c s j", s=NS)[:, :, :, 0], 0.0))
                step(vec.tensor_copy(inp[:, :, TP:HN].rearrange("p c (s j) -> p s j c", s=NS)[:, :, 0],
                                     ph0[:, :, b * HB:(b + 1) * HB]))
                for c in range(HB):
                    vec.tensor_tensor_scan(h[:, b * HB + c], dec[:, c], inp[:, c], 0.0, ALU.mult, ALU.add)\
                       .then_inc(scan_done, 1)

            def tile(k, c):
                m = tile_at[k, c]
                g = sgr if k == "rp" else sgc
                dve.wait_ge(tile_mm, m + 1)
                dve.wait_ge(tile_act, tile_at["gr" if k == "rp" else "gc", c] + 1)
                vec.tensor_tensor(g[:, c], bank[m % 4][:, 0:T], g[:, c], ALU.mult).then_inc(tile_dve, 1)

            dve.wait_ge(dconst, 1)
            conv_prompts(0)
            conv_prompts(2)
            dve.wait_ge(rst_done, 1)
            conv_rnn(0)
            conv_rnn(2)
            conv_rnn(4)
            variance(0)
            conv_rnn(6)
            scans(0)
            conv_samples(0)
            variance(1)
            scans(1)
            conv_prompts(4)
            for c in range(1, 4):
                conv_samples(c)
            conv_prompts(6)
            for c in range(4, KT):
                conv_samples(c)
            dve.wait_ge(st_T, 1)
            vec.tensor_copy(outst[0:96, 0:2 * P], bank[4][0:96, 0:2 * P])
            vec.tensor_copy(outst[0:24, 2 * P:3 * P], bank[4][0:24, 2 * P:3 * P]).then_inc(st_ev, 1)
            dve.wait_ge(st_T, 2)
            vec.tensor_copy(outst[0:KT, 3 * P:4 * P], bank[5][0:KT, 0:P])
            vec.tensor_copy(outst[0:NS * KT, 4 * P:5 * P], bank[5][0:NS * KT, P:2 * P]).then_inc(st_ev, 1)
            dve.wait_ge(st_T, 3)
            vec.tensor_copy(outst[0:120, 5 * P:7 * P], bank[6][0:120, 0:2 * P])
            vec.tensor_copy(outst[:, 7 * P:9 * P], bank[6][:, 2 * P:4 * P]).then_inc(st_ev, 1)

            for c in range(3):
                tile("rp", c)
            dve.wait_ge(mean_mm, 1)
            vec.tensor_tensor(cc, cc, bank[4][:, 0:T].unsqueeze(1).broadcast_to([P, KT, T]), ALU.subtract)\
               .then_inc(cen_done, 1)
            for c in range(3, 6):
                tile("rp", c)
            dve.wait_ge(var_mm, 1)
            vec.tensor_scalar(sq[:, 0], bank[5][:, 0:T], EPS, None, ALU.add).then_inc(var_done, 1)
            dve.wait_ge(std_done, 1)
            step(vec.reciprocal(sq[:, 0], sq[:, 0]))
            for c in range(KT):
                vec.tensor_tensor(cc[:, c], cc[:, c], sq[:, 0], ALU.mult).then_inc(nrm_done, 1)
            for c in range(6, KT):
                tile("rp", c)
            for c in range(KT):
                tile("cp", c)

            for n in range(2):
                for t in range(NT):
                    dve.wait_ge(wo_mm, n * NT + t + 1)
                    xt = x[0:ROWS[t], t, n * 512:(n + 1) * 512]
                    vec.tensor_tensor(xt, bank[WO_BANKS[n * NT + t]][0:ROWS[t]], xt, ALU.add).then_inc(x1_done, 1)
            vec.memset(logit, 0.0).then_inc(dconst, 1)
            dve.wait_ge(router_in, 64)
            dve.wait_ge(g_in, 48)
            vec.tensor_tensor(wr, wr, g2_row.unsqueeze(2).broadcast_to([P, KT, NG + NE]), ALU.mult).then_inc(wr_done, 1)
            for j in range(0, KT, 2):
                dve.wait_ge(xT2_mm, j + 1)
                vec.tensor_copy(xT2[:, j], bank[j % 4][:, 0:T]).then_inc(xT2_dve, 1)
            dve.wait_ge(ss2_done, NT)
            vec.tensor_scalar(stat[:, 9:12], stat[:, 6:9], 1.0 / D, EPS, ALU.mult, ALU.add).then_inc(ms2_done, 1)
            dve.wait_ge(rs2_done, 1)
            vec.reciprocal(stat[:, 9:12], stat[:, 9:12]).then_inc(ms2_done, 1)
            dve.wait_ge(ms2_done, 2)

            dve.wait_ge(log_mm, 1)
            dve.wait_ge(router_in, 64)
            dve.wait_ge(dconst, 2)
            for t in range(NT):
                ins = vec.scalar_tensor_tensor(logit[0:ROWS[t], t], bank[5][0:ROWS[t], t * 36:(t + 1) * 36],
                                               stat[0:ROWS[t], 9 + t:10 + t], rbias[0:ROWS[t]], ALU.mult, ALU.add)
                step(ins)
            dve.wait_ge(consts, 5)
            gl, m0, m1, dm, ex = logit[:, :, 0:NG], pick[:, 0], pick[:, 1], pick[:, 2], pick[:, 3]
            pos1, pos2, w1, w2, m2 = pick[:, 4], pick[:, 5], pick[:, 6], pick[:, 7], pick[:, 8]

            def first_of(oh, src, m, pri, n):
                step(vec.tensor_reduce(m, src, AX_X, ALU.max))
                step(vec.tensor_tensor(oh, src, bc(m, n), ALU.is_equal))
                step(vec.tensor_tensor(oh, oh, bt(pri, n), ALU.mult))
                step(vec.tensor_reduce(pick[:, 9], oh, AX_X, ALU.max))
                step(vec.tensor_tensor(oh, oh, bc(pick[:, 9], n), ALU.is_equal))

            first_of(goh, gl, m0, gpri, NG)
            step(vec.tensor_tensor(gex, gl, bc(m0, NG), ALU.subtract))
            step(vec.tensor_scalar(gtmp, goh, -1.0, BIG, ALU.add, ALU.mult))
            by_group = lambda ap: ap.rearrange("p t (g e) -> p t g e", g=NG)
            over = lambda ap: ap.unsqueeze(3).broadcast_to([P, NT, NG, EG])
            step(vec.tensor_tensor(by_group(el), by_group(logit[:, :, NG:]), over(goh), ALU.mult))
            step(vec.tensor_tensor(by_group(el), by_group(el), over(gtmp), ALU.add))
            first_of(oh1, el, m1, epri, NE)
            step(vec.scalar_tensor_tensor(el, oh1, -BIG, el, ALU.mult, ALU.add))
            first_of(oh2, el, m2, epri, NE)
            vec.tensor_tensor(dm, m2, m1, ALU.subtract).then_inc(ex_req, 1)
            step(vec.tensor_tensor(rtmp, oh1, oh2, ALU.add))
            vec.tensor_tensor(mo, rtmp, bc(valid, NE), ALU.mult).then_inc(mo_done, 1)
            dve.wait_ge(ex_done, 1)
            step(vec.tensor_reduce(m0, gex, AX_X, ALU.add))
            step(vec.tensor_scalar(m1, ex, 1.0, None, ALU.add))
            step(vec.tensor_tensor(m0, m0, m1, ALU.mult))
            step(vec.reciprocal(w1, m0))
            step(vec.tensor_tensor(w2, w1, ex, ALU.mult))
            dve.wait_ge(rank_mm, 1)
            step(vec.tensor_copy(rank, bank[6][:, 0:NE * NT].rearrange("p (t e) -> p t e", t=NT)))
            step(vec.tensor_copy(cnt, bank[6][:, NE * NT:NE * (NT + 1)]))
            step(vec.tensor_reduce(fpass[:, 0:1], cnt, AX_X, ALU.max))
            step(vec.tensor_scalar(fpass[:, 1:2], fpass[:, 0:1], float(C), 1.0, ALU.is_gt, ALU.add))
            for i in range(2, MAX_PASSES):
                step(vec.scalar_tensor_tensor(fpass[:, 1:2], fpass[:, 0:1], float(C * i), fpass[:, 1:2], ALU.is_gt, ALU.add))
            vec.tensor_copy(npass[:, 0:1], fpass[:, 1:2]).then_inc(pick_done, 1)
            dve.wait_ge(iota_done, 1)
            dve.wait_ge(st_out, 16 * ST_DMAS)
            dve.wait_ge(pick_done, 1)
            passes = dve.value_load(npass[0:1, 0:1], min_val=1, max_val=MAX_PASSES)

            with dve.Fori(0, passes) as r:
                step = Steps(dve, rstep, r * PASS_STEPS)
                with dve.If(r > 0):
                    for t in range(NT):
                        n = ROWS[t]
                        dve.wait_ge(hi_done, r * NT + (t + 1))
                        vec.tensor_tensor(xn2_lo[t][0:n], xn2[0:n, t], as_f32(xn2_hi[t][0:n]), ALU.subtract)\
                           .then_inc(lo_done, 1)
                with dve.Else():
                    dve.nop()
                step(vec.tensor_scalar(rtmp, rank, rbase, None, ALU.subtract))
                step(vec.tensor_scalar(cwin, cnt, rbase, 0.0, ALU.subtract, ALU.max))
                step(vec.tensor_scalar(cwin, cwin, float(C), None, ALU.min))
                step(vec.tensor_tensor_scan(off, ones_b[:, 0:NE], cwin, 0.0, ALU.mult, ALU.add))
                step(vec.tensor_tensor(off, off, cwin, ALU.subtract))
                step(vec.tensor_copy(off_i, off))
                step(vec.scalar_tensor_tensor(inw, rtmp, 0.0, mo, ALU.is_ge, ALU.mult))
                step(vec.scalar_tensor_tensor(inw, rtmp, float(C), inw, ALU.is_lt, ALU.mult))
                step(vec.tensor_tensor(rtmp, rtmp, bt(off, NE), ALU.add))
                step(vec.scalar_tensor_tensor(rtmp, rtmp, 1.0, inw, ALU.add, ALU.mult))
                for oh, pos in ((oh1, pos1), (oh2, pos2)):
                    step(vec.tensor_tensor(inw, rtmp, oh, ALU.mult))
                    step(vec.tensor_reduce(pos, inw, AX_X, ALU.add))
                for t in range(NT):
                    n = ROWS[t]
                    step(vec.tensor_scalar(sel[0:n, t], iota[0:n], pos2[0:n, t:t + 1], None, ALU.is_equal))
                    vec.scalar_tensor_tensor(sel[0:n, t], iota[0:n], pos1[0:n, t:t + 1], as_f32(sel[0:n, t]),
                                             ALU.is_equal, ALU.add).then_inc(sel_done, 1)
                def weights(t):
                    n, w = ROWS[t], wsel[0:ROWS[t], t % 2]
                    if t == NT - 1:
                        dve.wait_ge(wT_used, r * NT + 1)
                    step(vec.tensor_scalar(w, iota[0:n], pos1[0:n, t:t + 1], w1[0:n, t:t + 1], ALU.is_equal, ALU.mult))
                    step(vec.tensor_scalar(wtmp[0:n], iota[0:n], pos2[0:n, t:t + 1], w2[0:n, t:t + 1],
                                           ALU.is_equal, ALU.mult))
                    vec.tensor_tensor(w, w, wtmp[0:n], ALU.add).then_inc(wsel_done, 1)
                    dve.wait_ge(wsel_done, r * NT + (t + 1))

                for q in range(0, 2 * KT, 2):
                    dve.wait_ge(gat_mm, r * (2 * KT) + (q + 1))
                    vec.tensor_copy(xs[:, q // 2, 0:T], bank[q % 4][:, 0:T]).then_inc(gat_dve, 1)
                    if q in (2, 6):
                        weights((q - 2) // 4)
                weights(NT - 1)
                dve.wait_ge(wT_used, r * NT + NT)
                step(vec.memset(wpair_t, 0.0))
                for t in range(NT):
                    for j in range(PT):
                        at, k = weight_block(j, t), min(P, SLOTS - j * P)
                        ins = vec.tensor_reduce(wpair_t[0:k, t, j:j + 1], bank[4 + at // 512][0:k, at % 512:at % 512 + ROWS[t]],
                                                AX_X, ALU.add)
                step(ins)
                vec.tensor_reduce(wpair, wpair_t.rearrange("p t j -> p j t"), AX_X, ALU.add).then_inc(wT_done, 1)
                for i in range(3):
                    for lo, hi, k in wT_parts(i):
                        ins = vec.tensor_scalar(selT[0:k, 512 * i + lo:512 * i + hi], bank[4 + i][0:k, lo:hi],
                                                0.0, None, ALU.is_gt)
                    ins.then_inc(wT_done, 1)

                with dve.Fori(0, NE // EXP_SLOTS) as g:
                    def results(s):
                        dve.wait_ge(dn_mm, r * NE + g * EXP_SLOTS + (s + 1))
                        dve.wait_ge(ys_dve, r * NE + g * EXP_SLOTS + (s + 1))
                        at = dve.value_load(off_i[0:1, bass.ds(g * EXP_SLOTS + s, 1)], min_val=0, max_val=SLOTS)
                        vec.tensor_copy(ys[:, 4:8, bass.ds(at, C)],
                                        bank[3 + 2 * (s % 2)][:, 0:4 * C].rearrange("p (m n) -> p m n", m=4)).then_inc(ys_dve, 1)

                    for s in range(EXP_SLOTS):
                        dve.wait_ge(silu2, r * NE + g * EXP_SLOTS + (s + 1))
                        vec.tensor_tensor(hid[s % 2], bank[s % 2][:, 2 * C:4 * C].rearrange("p (f n) -> p f n", f=FT),
                                          sg2[s % 2], ALU.mult).then_inc(hid_done, 1)
                        if s >= 1:
                            results(s - 1)
                    results(EXP_SLOTS - 1)
                dve.wait_ge(wT_done, r * 4 + 4)
                for q in range(2 * PT):
                    j, w = q // 2, min(P, SLOTS - q // 2 * P)
                    lo, hi = q % 2 * 512, (q % 2 + 1) * 512
                    dve.wait_ge(yT_act, r * (2 * PT) + (q + 1))
                    vec.scalar_tensor_tensor(yrow_lo[0:w, j, lo:hi], bank[q % 2][0:w], wpair[0:w, j:j + 1],
                                             as_f32(yrow_hi[0:w, j, lo:hi]), ALU.mult, ALU.subtract).then_inc(yT_dve, 1)
                for t in range(NT):
                    for n in range(2):
                        dve.wait_ge(y_mm, r * (2 * NT) + (2 * t + n + 1))
                        xt = x[0:ROWS[t], t, n * 512:(n + 1) * 512]
                        vec.tensor_tensor(xt, bank[2 + 2 * t + n][0:ROWS[t]], xt, ALU.add).then_inc(y_done, 1)
                step(vec.tensor_scalar(rbase, rbase, float(C), None, ALU.add))
                assert step.n == PASS_STEPS, step.n

            dve.nop().then_inc(x2_done, 1)
            dve.wait_ge(ss3_done, NT)
            vec.tensor_scalar(stat[:, 15:18], stat[:, 12:15], 1.0 / D, EPS, ALU.mult, ALU.add).then_inc(ms3_done, 1)
            dve.wait_ge(rs3_done, 1)
            vec.reciprocal(stat[:, 15:18], stat[:, 15:18]).then_inc(ms3_done, 1)
            dve.wait_ge(ms3_done, 2)
            for t in range(NT):
                xt = x[0:ROWS[t], t]
                vec.scalar_tensor_tensor(xt, xt, stat[0:ROWS[t], 15 + t:16 + t], gf_bc[0:ROWS[t]],
                                         ALU.mult, ALU.mult).then_inc(fin_done, 1)

        @block.tensor
        def _(pe):
            mm, tp = nc.tensor.matmul, nc.tensor.transpose

            pe.wait_ge(consts, 1)
            pe.wait_ge(par_in, 16 * 12)
            for n, i, at in ((96, 0, 0), (124, 1, 96), (124, 2, 220), (64, 3, 344)):
                ins = tp(bank[0][:, at:at + n], prow[0:n, i], ident[0:n, 0:n])
            ins.then_inc(par_T, 1)
            for i in range(2):
                ins = tp(bank[1][:, 96 * i:96 * i + 96], prow[0:96, 4 + i], ident[0:96, 0:96])
            ins.then_inc(rst_T, 1)

            def conf_states(g):
                for i in range(4):
                    ins = tp(bank[4 + g][:, 120 * i:120 * i + 120], crow[0:120, 4 * g + i], ident[0:120, 0:120])
                ins.then_inc(cst_T, 1)

            pe.wait_ge(xn_done, NT)
            for j in range(KT):
                if j >= 4:
                    pe.wait_ge(xnT_done, j - 3)
                for t in range(NT):
                    n = ROWS[t]
                    ins = tp(bank[4 + j % 4][:, t * P:t * P + n], xn[0:n, t, j * P:(j + 1) * P], ident[0:n, 0:n])
                ins.then_inc(xT_done, 1)
            pe.wait_ge(par_done, 1)
            pe.wait_ge(rst_done, 1)
            pe.wait_ge(xnT_done, KT)

            def tile(m):
                k, c = tiles[m]
                b = blocks.index((k, c // MB))
                if c % MB == 0:
                    pe.wait_ge(mix_in[b % MIX_SLOTS], 16 * (b // MIX_SLOTS + 1))
                if m >= 4:
                    if m - 4 < NACT:
                        pe.wait_ge(tile_act, m - 3)
                    else:
                        pe.wait_ge(tile_dve, m - 3 - NACT)
                src = {"rp": gel, "cp": cc}.get(k, xnT)
                for i in range(KT):
                    if k == "rp" and c == 0:
                        pe.wait_ge(prod_done, i + 1)
                    if k == "cp" and c == 0:
                        pe.wait_ge(silu_done, i + 1)
                    ins = mm(bank[m % 4][:, 0:T], mix_w[b % MIX_SLOTS][:, i, (c % MB) * P:(c % MB + 1) * P], src[:, i],
                             start=(i == 0), stop=(i == KT - 1))
                ins.then_inc(tile_mm, 1)

            def gates(c):
                q = 4 + 2 * (c % 2)
                pe.wait_ge(xc_done, c + 1)
                if c == 0:
                    pe.wait_ge(wbd_in, 64)
                    pe.wait_ge(cst_done, NS)
                if c >= 2:
                    pe.wait_ge(gate_act, c - 1)
                mm(bank[q][:, 0:HN], wbd[:, 0, c], xc[:, c], start=True, stop=True)
                mm(bank[q + 1][:, 0:HN], wbd[:, 1, c], xc[:, c], start=True, stop=True).then_inc(gate_mm, 1)

            for m in range(len(tiles)):
                k, c = tiles[m]
                if (k, c) == ("gc", 0):
                    pe.wait_ge(gate_act, KT)
                    pe.wait_ge(st_cp, 2)
                    for i in range(2):
                        tp(bank[4][0:96, i * P:(i + 1) * P], st_ux[:, 96 * i:96 * i + 96], ident)
                    tp(bank[4][0:24, 2 * P:3 * P], st_uxp, ident).then_inc(st_T, 1)
                    tp(bank[5][0:KT, 0:P], h[:, :, TP - 1], ident)
                    tp(bank[5][0:NS * KT, P:2 * P], st_h, ident).then_inc(st_T, 1)
                    for i in range(2):
                        tp(bank[6][0:120, i * P:(i + 1) * P], st_glup[:, 120 * i:120 * i + 120], ident)
                    for i in range(2):
                        ins = tp(bank[6][:, (2 + i) * P:(3 + i) * P], st_glu[:, i * P:(i + 1) * P], ident)
                    ins.then_inc(st_T, 1)
                if (k, c) == ("rp", 3):
                    pe.wait_ge(conv_done, KT)
                    pe.wait_ge(st_ev, 2)
                    for i in range(KT):
                        ins = mm(bank[4][:, 0:T], ones_d, cc[:, i], start=(i == 0), stop=(i == KT - 1))
                    ins.then_inc(mean_mm, 1)
                if (k, c) == ("rp", 6):
                    pe.wait_ge(sq_done, 1)
                    for i in range(KT):
                        ins = mm(bank[5][:, 0:T], ones_d, sq[:, i], start=(i == 0), stop=(i == KT - 1))
                    ins.then_inc(var_mm, 1)
                tile(m)
                if m == 2:
                    pe.wait_ge(cst_in, 16)
                    for g in range(4):
                        conf_states(g)
                if k == "ux" and c >= 2:
                    gates(c - 2)
                if k == "uy" and c < 2:
                    gates(c + 6)

            pe.wait_ge(st_ev, 3)
            for n in range(2):
                b = blocks.index(("wo", n))
                pe.wait_ge(mix_in[b % MIX_SLOTS], 16 * (b // MIX_SLOTS + 1))
                for t in range(NT):
                    q = WO_BANKS[n * NT + t]
                    if q < 4:
                        pe.wait_ge(tile_dve, 2 * KT - 3 + q)
                    for i in range(KT):
                        if n == 0 and t == 0:
                            pe.wait_ge(merged, i + 1)
                        ins = mm(bank[WO_BANKS[n * NT + t]][0:ROWS[t]], sgr[:, i, t * P:t * P + ROWS[t]],
                                 mix_w[b % MIX_SLOTS][:, i], start=(i == 0), stop=(i == KT - 1))
                    ins.then_inc(wo_mm, 1)

            by_j = lambda ap: ap.rearrange("p t (m j) -> p t j m", j=KT)
            for j in range(KT):
                if j == 0:
                    pe.wait_ge(x1_done, 2 * NT)
                if j >= 4:
                    pe.wait_ge(xT2_dve if j % 2 == 0 else xT2_act, (j - 4) // 2 + 1)
                for t in range(NT):
                    n = ROWS[t]
                    ins = tp(bank[j % 4][:, t * P:t * P + n], by_j(x)[0:n, t, j], ident[0:n, 0:n])
                ins.then_inc(xT2_mm, 1)
            pe.wait_ge(wr_done, 1)
            pe.wait_ge(xT2_dve, KT // 2)
            pe.wait_ge(xT2_act, KT // 2)
            for t in range(NT):
                for j in range(KT):
                    ins = mm(bank[5][0:ROWS[t], t * 36:(t + 1) * 36], xT2[:, j, t * P:t * P + ROWS[t]], wr[:, j],
                             start=(j == 0), stop=(j == KT - 1))
            ins.then_inc(log_mm, 1)
            pe.wait_ge(mo_done, 1)
            pe.wait_ge(consts, 2)
            for t in range(NT + 1):
                last = min(t, NT - 1)
                for i in range(last + 1):
                    w = tri if i == t else ones_b
                    ins = mm(bank[6][:, t * NE:(t + 1) * NE], w, mo[:, i], start=(i == 0), stop=(i == last))
            ins.then_inc(rank_mm, 1)

            pe.wait_ge(pick_done, 1)
            passes = pe.value_load(npass[0:1, 0:1], min_val=1, max_val=MAX_PASSES)
            with pe.Fori(0, passes) as r:
                def gather(q, t):
                    n = ROWS[t]
                    for part in (xn2_hi, xn2_lo):
                        ins = mm(bank[q % 4][:, 0:T], part[t][0:n].rearrange("p (m j) -> p j m", j=KT)[:, q // 2],
                                 sel[0:n, t, (q % 2) * T:(q % 2 + 1) * T],
                                 start=(t == 0 and part is xn2_hi), stop=(t == NT - 1 and part is xn2_lo))
                    return ins

                for t in range(NT):
                    if t == 0:
                        pe.wait_ge(hi_done, r * NT + NT)
                        pe.wait_ge(lo_done, r * NT + NT)
                    pe.wait_ge(sel_done, r * NT + (t + 1))
                    for q in range(4):
                        ins = gather(q, t)
                        if t == NT - 1:
                            ins.then_inc(gat_mm, 1)
                for q in range(4, 2 * KT):
                    pe.wait_ge(gat_dve if q % 2 == 0 else gat_act, r * KT + ((q - 4) // 2 + 1))
                    for t in range(NT):
                        ins = gather(q, t)
                    ins.then_inc(gat_mm, 1)
                for t in range(NT):
                    if t == 0:
                        pe.wait_ge(gat_dve, r * KT + KT)
                        pe.wait_ge(gat_act, r * KT + KT)
                        pe.wait_ge(tail_done, 1)
                    if t < NT - 1:
                        pe.wait_ge(wsel_done, r * NT + (t + 1))
                    for j in range(PT):
                        if t == NT - 2 and j == PT - 1:
                            pe.wait_ge(wsel_done, r * NT + NT)
                        w = min(P, SLOTS - j * P)
                        at = weight_block(j, t)
                        ins = tp(bank[4 + at // 512][0:w, at % 512:at % 512 + ROWS[t]],
                                 wsel[0:ROWS[t], t % 2, j * P:j * P + w], ident[0:ROWS[t], 0:ROWS[t]])
                    ins.then_inc(wT_used, 1)

                with pe.Fori(0, NE // EXP_SLOTS) as g:
                    def gate_up(s):
                        at = pe.value_load(off_i[0:1, bass.ds(g * EXP_SLOTS + s, 1)], min_val=0, max_val=SLOTS)
                        pe.wait_ge(gu_in[s], r * (32 * NE // EXP_SLOTS) + g * 32 + 32)
                        if s >= 2:
                            pe.wait_ge(hid_done, r * NE + g * EXP_SLOTS + (s - 1))
                        for m in range(2):
                            for f in range(FT):
                                for k in range(KT):
                                    ins = mm(bank[s % 2][:, (2 * m + f) * C:(2 * m + f + 1) * C], w_gu[s][m][:, k, f],
                                             xs[:, k, bass.ds(at, C)], start=(k == 0), stop=(k == KT - 1))
                        ins.then_inc(gu_mm, 1)

                    def down(s):
                        pe.wait_ge(dn_in[s], r * (16 * NE // EXP_SLOTS) + g * 16 + 16)
                        pe.wait_ge(hid_done, r * NE + g * EXP_SLOTS + (s + 1))
                        if s == 1:
                            pe.wait_ge(wT_done, r * 4 + 4)
                        done = r * NE + g * EXP_SLOTS + (1 if s < 2 else s)
                        pe.wait_ge(ys_act, done)
                        pe.wait_ge(ys_dve, done)
                        for m in range(KT):
                            for f in range(FT):
                                ins = mm(bank[2 + 2 * (s % 2) + m // 4][:, (m % 4) * C:(m % 4 + 1) * C],
                                         w_dn[s][:, f, m * P:(m + 1) * P], hid[s % 2][:, f], start=(f == 0), stop=(f == FT - 1))
                        ins.then_inc(dn_mm, 1)

                    gate_up(0)
                    for s in range(1, EXP_SLOTS):
                        gate_up(s)
                        down(s - 1)
                    down(EXP_SLOTS - 1)

                pe.wait_ge(ys_act, r * NE + (NE + 1))
                pe.wait_ge(ys_dve, r * NE + (NE + 1))

                def turn(q):
                    if q >= 2:
                        pe.wait_ge(yT_dve, r * (2 * PT) + (q - 1))
                    j, w = q // 2, min(P, SLOTS - q // 2 * P)
                    for i in range(4):
                        ins = tp(bank[q % 2][0:w, i * P:(i + 1) * P], ys[:, 4 * (q % 2) + i, j * P:j * P + w], ident)
                    ins.then_inc(yT_mm, 1)

                turn(0)
                turn(1)
                for j in range(PT):
                    if j + 1 < PT:
                        turn(2 * j + 2)
                        turn(2 * j + 3)
                    pe.wait_ge(yT_dve, r * (2 * PT) + (2 * j + 2))
                    w = min(P, SLOTS - j * P)
                    for t in range(NT):
                        at = weight_block(j, t)
                        for n in range(2):
                            for part in (yrow_hi, yrow_lo):
                                ins = mm(bank[2 + 2 * t + n][0:ROWS[t]], selT[0:w, at:at + ROWS[t]],
                                         part[0:w, j, n * 512:(n + 1) * 512],
                                         start=(j == 0 and part is yrow_hi), stop=(j == PT - 1 and part is yrow_lo))
                            if j == PT - 1:
                                ins.then_inc(y_mm, 1)


_OUTS = {"y_p": (1, SEQ, D), "y_s": (NS, TS, D), "h_p": (1, 1, D), "rc_p": (1, 1, RW - 1, D), "cc_p": (1, 1, CW - 1, D),
         "h_s": (1, NS, D), "rc_s": (1, NS, RW - 1, D), "cc_s": (1, NS, CW - 1, D)}


def kernel(**inputs):
    import concourse.bacc as bacc
    from concourse.bass_utils import run_bass_kernel_spmd

    nc = bacc.Bacc("TRN2", target_bir_lowering=False, num_devices=1)
    arrays, a, o = {}, {}, {}
    for name, value in inputs.items():
        arrays[name] = np.ascontiguousarray(value)
        a[name] = nc.dram_tensor(name, arrays[name].shape, F32, kind="ExternalInput").ap()
    for name, shape in _OUTS.items():
        o[name] = nc.dram_tensor(f"out_{name}", shape, F32, kind="ExternalOutput").ap()
    trunk(nc, a, o)
    got = run_bass_kernel_spmd(nc, [arrays], core_ids=[0]).results[0]
    return tuple(got[f"out_{name}"] for name in _OUTS)
```

```python
from contextlib import ExitStack

import numpy as np

import concourse.bass as bass
from concourse import mybir

ALU = mybir.AluOpType
ACT = mybir.ActivationFunctionType
F32 = mybir.dt.float32
F32R = mybir.dt.float32r
I32 = mybir.dt.int32
BF16 = mybir.dt.bfloat16
AX_X = mybir.AxisListType.X

P = 128
D = 1024
KT = D // P
N_META = 16
SEQ = 256
TP = N_META + SEQ
NS, TS = 8, 4
T = TP + NS * TS
ROWS = (P, P, T - 2 * P)
NT = len(ROWS)
RW, CW = 4, 31
UXP, UXS = RW - 1 + TP, RW - 1 + TS
UXN = UXP + NS * UXS
GLP, GLS = CW - 1 + TP, CW - 1 + TS
GLN = GLP + NS * GLS
HS = TS + 1
HN = TP + NS * HS
NG, EG = 4, 8
NE = NG * EG
F = D // 4
FT = F // P
EPS = 1e-6
SLOTS = 2 * T
PT = -(-SLOTS // P)
C = 96
XS = SLOTS + C
BIG = 3.0e38
WB = 512
MB = WB // P
MIX_SLOTS = 4
EXP_SLOTS = 4
SPLIT_ORDER = (2, 0, 1)
POOL_UNITS = (3, 5, 7)
HI_SLOTS = 3
BLOCK_WORDS = KT * WB
HB = KT // 2
LRU_C = 8.0
WORK = 19616
MAX_PASSES = -(-T // C)
PASS_STEPS = 14
PLACE_STEPS = 17
ST_DMAS = 6 + NS
WO_BANKS = (0, 1, 2, 3, 6, 7)
EXP_WORDS = 2 * KT * F + FT * D


class Steps:

    def __init__(self, eng, sem, base=0):
        self.eng, self.sem, self.base, self.n = eng, sem, base, 0

    def __call__(self, ins):
        self.n += 1
        ins.then_inc(self.sem, 1)
        self.eng.wait_ge(self.sem, self.base + self.n)

    def beside(self, ins):
        self.n += 1
        ins.then_inc(self.sem, 1)


def trunk(nc, a, o):
    with ExitStack() as ctx:
        def sem(name):
            return ctx.enter_context(nc.semaphore(name))

        start = {}

        def sb(name, n, dt=F32):
            start[name] = -(-nc.sbuf_base // 32) * 32
            return ctx.enter_context(nc.sbuf_tensor(name, [P, n], dt))[:, :]

        def rounded(name, buf, at, n):
            return nc.alloc_sbuf_tensor_at(name, [P, n], F32R, offset=start[buf] + 4 * at)[:, :]

        def as_f32(ap):
            return ap.bitcast(F32)

        bank = [ctx.enter_context(nc.psum_tensor(f"bank{i}", [P, 512], F32))[:, :] for i in range(8)]

        ring = sb("ring", EXP_SLOTS * EXP_WORDS)
        x = sb("x", NT * D).rearrange("p (t d) -> p t d", t=NT)
        work = sb("work", WORK)

        def cutter(buf, size):
            at = [0]

            def cut(n, at0=None):
                lo = at[0] if at0 is None else at0
                assert lo + n <= size, (lo + n, size)
                at[0] = lo + n
                return buf[:, lo:lo + n]
            return cut

        def chan(ap):
            return ap.rearrange("p (c n) -> p c n", c=KT)

        cut = cutter(work, WORK)
        xnT = chan(cut(KT * T))
        ux = chan(cut(KT * UXN))
        xc = chan(cut(KT * HN))
        glu = chan(cut(KT * GLN))
        cc = chan(cut(KT * T))
        gel = chan(cut(KT * T))
        h = chan(cut(KT * HN))
        sq = xnT
        sgr = chan(cut(KT * T, KT * T))
        sgc = chan(cut(KT * T, KT * (T + UXN)))
        at_glu, at_cc = KT * (T + UXN + HN), KT * (T + UXN + HN + GLN)
        gel_lo, gel_hi = (chan(rounded(n, "work", at, KT * T)) for n, at in
                          (("gel_lo", at_cc + KT * T), ("gel_hi", at_cc + 2 * KT * T)))
        cc_lo, cc_hi = (chan(rounded(n, "work", at, KT * T)) for n, at in (("cc_lo", at_cc), ("cc_hi", at_glu)))
        mrg_lo, mrg_hi = (chan(rounded(n, "work", at, KT * T)) for n, at in
                          (("mrg_lo", KT * T), ("mrg_hi", at_cc + 2 * KT * T)))
        xn_lo = chan(rounded("xn_lo", "work", 0, KT * T))
        cut = cutter(work, WORK)
        xn2 = cut(NT * D).rearrange("p (t d) -> p t d", t=NT)
        xs_f = cut(KT * XS)
        xs, xT2 = chan(xs_f), chan(xs_f[:, 0:KT * T])
        yrow_hi = rounded("yrow_hi", "work", NT * D, PT * D).rearrange("p (j d) -> p j d", j=PT)
        yrow_lo = rounded("yrow_lo", "ring", 0, PT * D).rearrange("p (j d) -> p j d", j=PT)
        ys = chan(cut(KT * XS))
        junk = cut(NT * SLOTS)[:, 0:D]
        sel = rounded("sel", "work", NT * D + 2 * KT * XS, NT * SLOTS).rearrange("p (t n) -> p t n", t=NT)
        wsel = cut(2 * SLOTS).rearrange("p (b n) -> p b n", b=2)
        cut(PT * T)
        selT = rounded("selT", "work", NT * D + 2 * KT * XS + (NT + 2) * SLOTS, PT * T)
        logit = cut((NG + NE) * NT).rearrange("p (t e) -> p t e", t=NT)
        el, oh1, oh2, rank, inw, rtmp = (cut(NE * NT).rearrange("p (t e) -> p t e", t=NT) for _ in range(6))
        goh, gtmp, gex = (cut(NG * NT).rearrange("p (t e) -> p t e", t=NT) for _ in range(3))
        rbias = sb("rbias", NG + NE)
        cnt, cwin, off = (sb(n, NE) for n in ("cnt", "cwin", "off"))
        off_i, npass = sb("off_i", NE, I32), sb("npass", 4, I32)
        pick = sb("pick", NT * 10).rearrange("p (k t) -> p k t", k=10)
        rbase, fpass = sb("rbase", 1), sb("fpass", 2)
        mo = sb("mo", NE * NT, BF16).rearrange("p (t e) -> p t e", t=NT)
        gpri, epri = sb("gpri", NG), sb("epri", NE)

        cut = cutter(ring, EXP_SLOTS * EXP_WORDS)
        e_hi = (EXP_SLOTS - 1) * EXP_WORDS
        mix_w = [cut(BLOCK_WORDS).rearrange("p (k n) -> p k n", k=KT) for _ in range(MIX_SLOTS)]
        gate_r, gate_i, tau, dec, inp = (cut(HB * HN).rearrange("p (c n) -> p c n", c=HB) for _ in range(5))
        cv_sb, sg_sb = (cut(2 * T).rearrange("p (b n) -> p b n", b=2) for _ in range(2))
        w_lo = [rounded(f"w_lo{s}", "ring", s * BLOCK_WORDS, BLOCK_WORDS).rearrange("p (k n) -> p k n", k=KT)
                for s in range(MIX_SLOTS)]
        w_hi = [rounded(f"w_hi{s}", "ring", e_hi + s * BLOCK_WORDS // 2, BLOCK_WORDS // 2) for s in range(HI_SLOTS)]
        xn = ring[:, 2 * BLOCK_WORDS:2 * BLOCK_WORDS + NT * D].rearrange("p (t d) -> p t d", t=NT)
        cut(0, 3 * BLOCK_WORDS)
        prow = cut(6 * P).rearrange("p (i n) -> p i n", i=6)
        crow = cut(16 * P).rearrange("p (i n) -> p i n", i=16)
        e0 = [(EXP_SLOTS - 1 - s) * EXP_WORDS for s in range(EXP_SLOTS)]
        w_gu = [[ring[:, e0[s] + m * KT * F:e0[s] + (m + 1) * KT * F].rearrange("p (k m j) -> p k j m", k=KT, j=FT)
                 for m in range(2)] for s in range(EXP_SLOTS)]
        w_gu_flat = [[ring[:, e0[s] + m * KT * F:e0[s] + (m + 1) * KT * F] for m in range(2)] for s in range(EXP_SLOTS)]
        w_dn_flat = [ring[:, e0[s] + 2 * KT * F:e0[s] + EXP_WORDS] for s in range(EXP_SLOTS)]
        w_dn = [w.rearrange("p (j n) -> p j n", j=FT) for w in w_dn_flat]

        wbd_f = sb("gate_weights", 2 * KT * P)
        wbd = wbd_f.rearrange("p (g c n) -> p g c n", g=2, c=KT)
        g2_bc, gf_bc = wbd_f[:, 0:D], wbd_f[:, D:2 * D]
        halves = [rounded(f"half{i}", "work", NT * D + KT * XS + i * D, D) for i in range(2 * NT - 1)]
        halves.append(rounded("half5", "gate_weights", 0, D))
        xn2_hi, xn2_lo = halves[:NT], halves[NT:]
        cut = cutter(wbd_f, 2 * KT * P)
        st_ux, st_uxp, st_h, st_glup, st_glu = (cut(n) for n in (
            NS * (RW - 1) * KT, (RW - 1) * KT, NS * KT, (CW - 1) * KT, NS * TS * KT))
        xn_hi = [rounded(f"xn_hi{c}", *(("gate_weights", 2 * KT * P - (HB - c) * T) if c < HB else
                                        ("ring", MIX_SLOTS * BLOCK_WORDS + (c - HB) * T)), T) for c in range(KT)]
        par = sb("par", 408)
        pn1, pccb, plg, plb, prcb, pba, pbi, plam = (par[:, i * KT:(i + 1) * KT] for i in range(8))
        prw = par[:, 64:96].rearrange("p (w c) -> p w c", w=RW)
        pcw = par[:, 96:344].rearrange("p (w c) -> p w c", w=CW)
        ph0 = par[:, 344:408].rearrange("p (s c) -> p s c", s=NS)
        wr = par[:, 0:KT * (NG + NE)].rearrange("p (j e) -> p j e", j=KT)
        g2_row = par[:, KT * (NG + NE):KT * (NG + NE) + KT]
        win = sb("windows", NS * TS * CW)
        win4 = win.rearrange("p (s t w) -> p s t w", s=NS, t=TS)
        iota = win[:, 0:SLOTS]
        hid = [win[:, SLOTS + b * FT * C:SLOTS + (b + 1) * FT * C].rearrange("p (f n) -> p f n", f=FT) for b in range(2)]
        outst = sb("outst", 9 * P)
        cv4 = [sb("conv4", UXN), outst[:, 0:UXN]]
        csum = cv4[0][:, 0:T]
        sg2 = [outst[:, b * FT * C:(b + 1) * FT * C].rearrange("p (f n) -> p f n", f=FT) for b in range(2)]
        wtmp = outst[:, 2 * FT * C:2 * FT * C + SLOTS]
        wpair_t = outst[:, 2 * FT * C + SLOTS:2 * FT * C + SLOTS + NT * PT].rearrange("p (t j) -> p t j", t=NT)
        wpair = outst[:, 2 * FT * C + SLOTS + NT * PT:2 * FT * C + SLOTS + NT * PT + PT]
        ident, ones_d = sb("ident", P), sb("ones_d", P)
        tri, ones_b = sb("tri", P, BF16), sb("ones_b", P, BF16)
        lam = sb("lam", 5 * KT).rearrange("p (i c) -> p i c", i=5)
        stat, spare = sb("stat", 18), sb("spare", 1)

        (xhi_done, xlo_done, wlo_pool, par_in, first_in, cst_in, wbd_in, router_in, g_in, consts, zeros, dconst, dstep, astep, pstep, rstep,
         ss_done, ms_done, rs_done, xn_done, par_T, par_done, rst_T, rst_done, cst_T, cst_done, xT_done, xnT_done, xnT_act,
         lam_e, kappa_done, tile_mm, tile_act, tile_dve, glu_done, win_done, win_used, conv_done, xc_done,
         gate_mm, gate_act, dec_done, vsq_done, vrt_done, inp_done, scan_done, gelu_done, prod_done,
         st_cp, st_T, st_ev, st_out, mean_mm, cen_done, sq_done, sum_done, var_mm, var_done, std_done, nrm_done, silu_done,
         merged, wo_mm, x1_done, ss2_done, ms2_done, rs2_done, xn2_done, xn2_last, xT2_mm, xT2_act, xT2_dve,
         log_mm, place_step, mo_done, ex_req, ex_done, pick_done, rank_mm, iota_done, sel_done, gat_mm, gat_done,
         wsel_done, wT_used, wT_done, xsc_done, hi_done, lo_done, tail_done, wr_done, table, whi_done, wlo_done, half_mm, ghi_done, glo_done,
         chi_done, clo_done, mhi_done, mlo_done, gu_mm, silu2, hid_done, dn_mm, ys_act, ys_dve,
         yT_mm, yT_act, yT_dve, y_mm, y_done, ss3_done, ms3_done, rs3_done, fin_done, y_out) = (sem(n) for n in (
            "xhi_done xlo_done wlo_pool par_in first_in cst_in wbd_in router_in g_in consts zeros dconst dstep astep pstep rstep "
            "ss_done ms_done rs_done xn_done par_T par_done rst_T rst_done cst_T cst_done xT_done xnT_done xnT_act "
            "lam_e kappa_done tile_mm tile_act tile_dve glu_done win_done win_used conv_done xc_done "
            "gate_mm gate_act dec_done vsq_done vrt_done inp_done scan_done gelu_done prod_done "
            "st_cp st_T st_ev st_out mean_mm cen_done sq_done sum_done var_mm var_done std_done nrm_done silu_done "
            "merged wo_mm x1_done ss2_done ms2_done rs2_done xn2_done xn2_last xT2_mm xT2_act xT2_dve "
            "log_mm place_step mo_done ex_req ex_done pick_done rank_mm iota_done sel_done gat_mm gat_done "
            "wsel_done wT_used wT_done xsc_done hi_done lo_done tail_done wr_done table whi_done wlo_done half_mm ghi_done glo_done "
            "chi_done clo_done mhi_done mlo_done gu_mm silu2 hid_done dn_mm ys_act ys_dve "
            "yT_mm yT_act yT_dve y_mm y_done ss3_done ms3_done rs3_done fin_done y_out").split())
        tap_done = [sem(f"tap_done{b}") for b in range(2)]
        rtap_done = [sem(f"rtap_done{b}") for b in range(2)]
        x_in = [sem(f"x_in{t}") for t in range(NT)]
        mix_in = [sem(f"mix_in{s}") for s in range(MIX_SLOTS)]
        gu_in = [sem(f"gu_in{s}") for s in range(EXP_SLOTS)]
        dn_in = [sem(f"dn_in{s}") for s in range(EXP_SLOTS)]

        w_in = a["w_in"][0]
        first = {"ux": 0, "uy": D, "cv": 2 * D, "cg": 3 * D, "gr": 4 * D, "gc": 5 * D}
        after = {"rp": a["w_rnn_proj"][0], "cp": a["w_conv_proj"][0], "wo": a["w_out"][0]}
        blocks = [(k, i) for i in range(2) for k in ("cv", "cg")]
        blocks += [(k, i) for k in ("ux", "uy", "gr", "gc", "rp", "cp", "wo") for i in range(2)]
        NBLK = len(blocks)
        tiles = [(k, c) for c in range(KT) for k in ("cv", "cg")]
        tiles += [(k, c) for k in ("ux", "uy", "gr", "gc", "rp", "cp") for c in range(KT)]
        tile_at = {t: m for m, t in enumerate(tiles)}
        NACT = len(tiles) - 2 * KT

        def block_src(k, i):
            w = after[k][:, i * WB:(i + 1) * WB] if k in after else w_in[:, first[k] + i * WB:first[k] + (i + 1) * WB]
            return w.rearrange("(k p) n -> p k n", p=P)

        def seqs(ap, at, stride, lo, n):
            return ap[:, at:at + NS * stride].rearrange("p (s j) -> p s j", s=NS)[:, :, lo:lo + n]

        def state_cols(buf, at, stride):
            return buf[:, :, at:at + NS * stride].rearrange("p c (s j) -> p s j c", s=NS)

        def weight_block(j, t):
            return (t * PT + j) * P if t < NT - 1 else (NT - 1) * PT * P + j * ROWS[t]

        first_split, first_tile = blocks.index(("gr", 0)), tile_at["gr", 0]
        WO_UNIT = 2 * (blocks.index(("wo", 0)) - first_split)

        def split_halves(u):
            s = (first_split + u // 2) % MIX_SLOTS
            if u >= WO_UNIT:
                k = slice(HB * (u % 2), HB * (u % 2) + HB)
                return mix_w[s][:, k], w_lo[s][:, k], w_hi[u % HI_SLOTS].rearrange("p (k n) -> p k n", k=HB)
            n = slice(WB // 2 * (u % 2), WB // 2 * (u % 2 + 1))
            return mix_w[s][:, :, n], w_lo[s][:, :, n], w_hi[u % HI_SLOTS].rearrange("p (k n) -> p k n", k=KT)

        def low_ready(u):
            if u in POOL_UNITS:
                return wlo_pool, POOL_UNITS.index(u) + 1
            return wlo_done, u + 1 - sum(v < u for v in POOL_UNITS)

        def split_used(u):
            return (half_mm, 1) if u == WO_UNIT else (tile_mm, first_tile + 2 * u + 2)

        def block_used(b):
            k, i = blocks[b]
            return (wo_mm, (i + 1) * NT) if k == "wo" else (tile_mm, tile_at[k, i * MB + MB - 1] + 1)

        def wT_parts(i):
            runs = []
            for t in range(NT):
                for j in range(PT):
                    lo = weight_block(j, t) - 512 * i
                    if 0 <= lo < 512:
                        k = min(P, SLOTS - j * P)
                        if runs and runs[-1][2] == k:
                            runs[-1][1] = lo + ROWS[t]
                        else:
                            runs.append([lo, lo + ROWS[t], k])
            return runs

        block = ctx.enter_context(nc.Block())

        @block.sync
        def _(sp):
            sp.dma_start(x[0:N_META, 0], a["meta_tokens"]).then_inc(x_in[0], 16)
            sp.dma_start(x[N_META:P, 0], a["x_prompt"][0, 0:P - N_META]).then_inc(x_in[0], 16)
            sp.dma_start(x[:, 1], a["x_prompt"][0, P - N_META:2 * P - N_META]).then_inc(x_in[1], 16)
            sp.dma_start(x[0:TP - 2 * P, 2], a["x_prompt"][0, 2 * P - N_META:]).then_inc(x_in[2], 16)
            sp.dma_start(x[TP - 2 * P:ROWS[2], 2], a["x_sample"].rearrange("s t d -> (s t) d")).then_inc(x_in[2], 16)

            sp.dma_start(mix_w[0][:, 0:HB], block_src(*blocks[0])[:, 0:HB]).then_inc(first_in, 16)
            for i, n in enumerate(("norm1_g", "conf_conv_b", "conf_ln_g", "conf_ln_b",
                                   "rnn_conv_b", "b_rg_a", "b_rg_i", "rg_lambda")):
                sp.dma_start(prow[i * KT:(i + 1) * KT, 0], a[n][0].rearrange("(c p) -> c p", p=P)).then_inc(par_in, 16)

            def load_block(b):
                if b == 2:
                    sp.wait_ge(xT_done, KT)
                if b == 3:
                    sp.wait_ge(cst_T, 4)
                if b >= MIX_SLOTS:
                    sp.wait_ge(*block_used(b - MIX_SLOTS))
                k = slice(HB if b == 0 else 0, KT)
                sp.dma_start(mix_w[b % MIX_SLOTS][:, k], block_src(*blocks[b])[:, k]).then_inc(mix_in[b % MIX_SLOTS], 16)

            def load_expert(e, s):
                for m, n in enumerate(("w_exp_gate", "w_exp_up")):
                    sp.dma_start(w_gu_flat[s][m], a[n][0, bass.ds(e, 1)].rearrange("e (p k) f -> p (e k f)", p=P))\
                      .then_inc(gu_in[s], 16)
                sp.dma_start(w_dn_flat[s], a["w_exp_down"][0, bass.ds(e, 1)].rearrange("e (p k) n -> p (e k n)", p=P))\
                  .then_inc(dn_in[s], 16)

            for b in range(NBLK):
                load_block(b)
            sp.wait_ge(*block_used(blocks.index(("cp", 1))))
            load_expert(1, 1)
            sp.wait_ge(wo_mm, 2 * NT)
            for e in (0, 2, 3):
                load_expert(e, e)
            with sp.Fori(1, NE // EXP_SLOTS) as g:
                for s in range(EXP_SLOTS):
                    sp.wait_ge(dn_mm, g * EXP_SLOTS + (s + 1 - EXP_SLOTS))
                    load_expert(g * EXP_SLOTS + s, s)
            sp.wait_ge(pick_done, 1)
            passes = sp.value_load(npass[0:1, 0:1], min_val=1, max_val=MAX_PASSES)
            with sp.If(passes > 1):
                with sp.Fori(1, passes) as r:
                    for s in range(EXP_SLOTS):
                        sp.wait_ge(y_mm, r * (2 * NT))
                        load_expert(s, s)
                    with sp.Fori(1, NE // EXP_SLOTS) as g:
                        for s in range(EXP_SLOTS):
                            sp.wait_ge(dn_mm, r * NE + g * EXP_SLOTS + (s + 1 - EXP_SLOTS))
                            load_expert(g * EXP_SLOTS + s, s)
            with sp.Else():
                sp.nop()
            for t in range(NT):
                sp.wait_ge(fin_done, t + 1)
                if t == 0:
                    sp.dma_start(o["y_p"][0, 0:P - N_META], x[N_META:P, 0]).then_inc(y_out, 16)
                elif t == 1:
                    sp.dma_start(o["y_p"][0, P - N_META:2 * P - N_META], x[:, 1]).then_inc(y_out, 16)
                else:
                    sp.dma_start(o["y_p"][0, 2 * P - N_META:], x[0:TP - 2 * P, 2]).then_inc(y_out, 16)
                    sp.dma_start(o["y_s"].rearrange("s t d -> (s t) d"), x[TP - 2 * P:ROWS[2], 2]).then_inc(y_out, 16)
            sp.wait_ge(y_out, 16 * 4)
            sp.wait_ge(st_out, 16 * ST_DMAS)

        @block.gpsimd
        def _(pool):
            step = Steps(pool, pstep)
            step(nc.gpsimd.memset(ident, 0.0))
            nc.gpsimd.affine_select(out=ident, in_=ident, compare_op=ALU.not_equal, fill=1.0, base=0,
                                    pattern=[[-1, P]], channel_multiplier=1).then_inc(consts, 1)
            nc.gpsimd.memset(wbd_f, 0.0).then_inc(zeros, 1)
            step(nc.gpsimd.memset(tri, 1.0))
            nc.gpsimd.affine_select(out=tri, in_=tri, compare_op=ALU.is_gt, fill=0.0, base=0,
                                    pattern=[[1, P]], channel_multiplier=-1).then_inc(consts, 1)
            nc.gpsimd.iota(gpri, [[-1, NG]], base=NG, channel_multiplier=0,
                           allow_small_or_imprecise_dtypes=True).then_inc(consts, 1)
            nc.gpsimd.iota(epri, [[-1, NE]], base=NE, channel_multiplier=0,
                           allow_small_or_imprecise_dtypes=True).then_inc(consts, 1)

            for c in range(KT):
                pool.wait_ge(tile_act, 2 * c + 2)
                nc.gpsimd.tensor_tensor(glu[:, c, CW - 1:GLP], cv_sb[:, c % 2, 0:TP], sg_sb[:, c % 2, 0:TP], ALU.mult)
                nc.gpsimd.tensor_tensor(seqs(glu[:, c], GLP, GLS, CW - 1, TS), seqs(cv_sb[:, c % 2], TP, TS, 0, TS),
                                        seqs(sg_sb[:, c % 2], TP, TS, 0, TS), ALU.mult).then_inc(glu_done, 1)

            def gated_input(b):
                pool.wait_ge(gate_act, HB * (b + 1))
                if b:
                    pool.wait_ge(scan_done, HB)
                nc.gpsimd.tensor_tensor(inp, gate_i, xc[:, b * HB:(b + 1) * HB], ALU.mult).then_inc(inp_done, 1)

            def windows(c):
                if c == 0:
                    pool.wait_ge(cst_done, NS)
                    pool.wait_ge(glu_done, KT)
                else:
                    pool.wait_ge(win_used, c)
                g = glu[:, c, GLP:GLN].rearrange("p (s j) -> p s j", s=NS)
                for t in range(TS):
                    ins = nc.gpsimd.tensor_tensor(win4[:, :, t, :], g[:, :, t:t + CW],
                                                  pcw[:, :, c].unsqueeze(1).broadcast_to([P, NS, CW]), ALU.mult)
                ins.then_inc(win_done, 1)

            gated_input(0)
            for c in range(3):
                windows(c)
            gated_input(1)
            pool.wait_ge(gate_mm, KT)
            nc.gpsimd.tensor_copy(st_ux.rearrange("p (s r c) -> p s r c", s=NS, r=RW - 1),
                                  state_cols(ux, UXP, UXS)[:, :, UXS - RW + 1:UXS])
            nc.gpsimd.tensor_copy(st_uxp.rearrange("p (r c) -> p c r", c=KT), ux[:, :, UXP - RW + 1:UXP]).then_inc(st_cp, 1)
            windows(3)
            pool.wait_ge(scan_done, KT)
            nc.gpsimd.tensor_copy(st_h.rearrange("p (s c) -> p s c", s=NS), state_cols(h, TP, HS)[:, :, HS - 1])
            nc.gpsimd.tensor_copy(st_glup.rearrange("p (r c) -> p c r", c=KT), glu[:, :, GLP - CW + 1:GLP])
            nc.gpsimd.tensor_copy(st_glu.rearrange("p (s r c) -> p s r c", s=NS, r=TS),
                                  state_cols(glu, GLP, GLS)[:, :, CW - 1:GLS]).then_inc(st_cp, 1)
            pool.wait_ge(gelu_done, 1)
            pool.wait_ge(scan_done, KT)
            for c in range(KT):
                nc.gpsimd.tensor_tensor(gel[:, c, 0:TP], gel[:, c, 0:TP], h[:, c, 0:TP], ALU.mult)
                nc.gpsimd.tensor_tensor(seqs(gel[:, c], TP, TS, 0, TS), seqs(gel[:, c], TP, TS, 0, TS),
                                        seqs(h[:, c], TP, HS, 1, TS), ALU.mult).then_inc(prod_done, 1)

            def weight_low(u):
                w, lo, hi = split_halves(u)
                pool.wait_ge(whi_done, u + 1)
                nc.gpsimd.tensor_tensor(lo, w, as_f32(hi), ALU.subtract).then_inc(wlo_pool, 1)

            weight_low(3)
            windows(4)
            weight_low(5)
            windows(5)
            windows(6)
            weight_low(7)
            windows(7)
            pool.wait_ge(win_used, KT)
            nc.gpsimd.iota(iota, [[1, SLOTS]], base=1, channel_multiplier=0,
                           allow_small_or_imprecise_dtypes=True).then_inc(iota_done, 1)
            for c in range(KT):
                pool.wait_ge(tile_dve, KT + c + 1)
                nc.gpsimd.tensor_tensor(sgr[:, c], sgr[:, c], sgc[:, c], ALU.add).then_inc(merged, 1)
            nc.gpsimd.memset(ys[:, 0:KT // 2], 0.0).then_inc(ys_act, 1)
            nc.gpsimd.memset(ys[:, KT // 2:], 0.0).then_inc(ys_dve, 1)
            pool.wait_ge(g_in, 48)
            for t in range(NT - 1):
                pool.wait_ge(xsc_done, t + 1)
                xt = xn2[0:ROWS[t], t]
                nc.gpsimd.tensor_tensor(xt, xt, g2_bc[0:ROWS[t]], ALU.mult).then_inc(xn2_done, 1)
            pool.wait_ge(xn2_done, NT - 1)
            pool.wait_ge(xn2_last, 1)
            for i, t in enumerate(SPLIT_ORDER):
                n = ROWS[t]
                pool.wait_ge(hi_done, i + 1)
                nc.gpsimd.tensor_tensor(xn2_lo[t][0:n], xn2[0:n, t], as_f32(xn2_hi[t][0:n]), ALU.subtract)\
                  .then_inc(lo_done, 1)
            pool.wait_ge(log_mm, 1)
            nc.gpsimd.memset(xs[:, :, SLOTS:XS], 0.0).then_inc(tail_done, 1)

        @block.scalar
        def _(act):
            act.dma_start(prow[64:96, 0], a["rnn_conv_w"][0].rearrange("w (c p) -> (w c) p", p=P)).then_inc(par_in, 16)
            act.dma_start(prow[0:124, 1:3], a["conf_conv_w"][0].rearrange("w (c p) -> (w c) p", p=P)
                          .rearrange("(i r) p -> r i p", i=2)).then_inc(par_in, 16)
            act.dma_start(prow[0:64, 3], a["state_rglru_h"][0].rearrange("s (c p) -> (s c) p", p=P)).then_inc(par_in, 16)
            act.dma_start(prow[0:96, 4:6], a["state_rglru_conv"][0].rearrange("s r (c p) -> (s r c) p", p=P)
                          .rearrange("(i q) p -> q i p", i=2)).then_inc(par_in, 16)

            def load_table(func):
                act.wait_ge(dconst, 1)
                nc.scalar.activation(spare, spare, func).then_inc(table, 1)
                tables[0] += 1
                act.wait_ge(table, tables[0])

            tables = [0]
            load_table(ACT.Sqrt)
            act.wait_ge(dconst, 1)
            for t in range(NT):
                act.wait_ge(x_in[t], 16 if t == 1 else 32)
                nc.scalar.activation(xn[0:ROWS[t], t], x[0:ROWS[t], t], ACT.Square,
                                     accum_out=stat[0:ROWS[t], t:t + 1]).then_inc(ss_done, 1)
            act.wait_ge(ms_done, 1)
            nc.scalar.activation(stat[:, 3:6], stat[:, 3:6], ACT.Sqrt).then_inc(rs_done, 1)
            act.wait_ge(par_done, 1)
            for j in range(1, KT, 2):
                act.wait_ge(xT_done, j + 1)
                nc.scalar.activation(xnT[:, j], bank[4 + j % 4][:, 0:T], ACT.Copy, scale=pn1[:, j:j + 1]).then_inc(xnT_act, 1)
            act.dma_start(crow[0:120], a["state_conformer_conv"][0].rearrange("s r (c p) -> (s r c) p", p=P)
                          .rearrange("(i q) p -> q i p", i=16)).then_inc(cst_in, 16)
            act.wait_ge(zeros, 1)
            for g, n in enumerate(("w_rg_a", "w_rg_i")):
                for e in range(2):
                    act.dma_start(wbd[64 * e:64 * e + 64, g, :, 64 * e:64 * e + 64],
                                  a[n][0].rearrange("(c e) i j -> e i c j", e=2)[e]).then_inc(wbd_in, 16)
            act.dma_start(o["cc_s"][0][:, 0:CW - 1 - TS], a["state_conformer_conv"][0][:, TS:]).then_inc(st_out, 16)

            nc.scalar.activation(lam[:, 0], plam, ACT.Abs).then_inc(astep, 1)
            act.wait_ge(astep, 1)
            nc.scalar.activation(lam[:, 0], lam[:, 0], ACT.Exp, scale=-1.0).then_inc(lam_e, 1)

            def tile(m):
                k, c = tiles[m]
                act.wait_ge(tile_mm, m + 1)
                b = bank[m % 4][:, 0:T]
                if k == "cv":
                    if c >= 2:
                        act.wait_ge(glu_done, c - 1)
                    ins = nc.scalar.activation(cv_sb[:, c % 2], b, ACT.Copy)
                elif k == "cg":
                    ins = nc.scalar.activation(sg_sb[:, c % 2], b, ACT.Sigmoid)
                elif k == "ux":
                    nc.scalar.activation(ux[:, c, RW - 1:UXP], b[:, 0:TP], ACT.Copy)
                    ins = nc.scalar.activation(seqs(ux[:, c], UXP, UXS, RW - 1, TS), seqs(b, TP, TS, 0, TS), ACT.Copy)
                elif k == "uy":
                    ins = nc.scalar.activation(gel[:, c], b, ACT.Copy)
                elif k == "gr":
                    if c == 0:
                        act.wait_ge(st_cp, 1)
                        act.wait_ge(xc_done, KT)
                    ins = nc.scalar.activation(sgr[:, c], b, ACT.Sigmoid)
                else:
                    if c == 0:
                        act.wait_ge(inp_done, 2)
                    ins = nc.scalar.activation(sgc[:, c], b, ACT.Sigmoid)
                ins.then_inc(tile_act, 1)

            def gates(c):
                act.wait_ge(gate_mm, c + 1)
                if c == HB:
                    act.wait_ge(inp_done, 1)
                    act.wait_ge(vsq_done, 1)
                q = 4 + 2 * (c % 2)
                nc.scalar.activation(gate_r[:, c % HB], bank[q][:, 0:HN], ACT.Sigmoid, bias=pba[:, c:c + 1])
                nc.scalar.activation(gate_i[:, c % HB], bank[q + 1][:, 0:HN], ACT.Sigmoid,
                                     bias=pbi[:, c:c + 1]).then_inc(gate_act, 1)

            def decay(b):
                act.wait_ge(gate_act, HB * (b + 1))
                if b:
                    act.wait_ge(scan_done, HB)
                else:
                    act.wait_ge(kappa_done, 1)
                for c in range(HB):
                    ch = b * HB + c
                    nc.scalar.activation(tau[:, c], gate_r[:, c], ACT.Tanh, scale=lam[:, 1, ch:ch + 1])
                    ins = nc.scalar.activation(dec[:, c], gate_r[:, c], ACT.Exp, scale=lam[:, 2, ch:ch + 1])
                ins.then_inc(dec_done, 1)

            def root(b):
                act.wait_ge(vsq_done, b + 1)
                nc.scalar.activation(tau, tau, ACT.Sqrt).then_inc(vrt_done, 1)

            def weight_high(u):
                b = first_split + u // 2
                act.wait_ge(mix_in[b % MIX_SLOTS], 16 * (b // MIX_SLOTS + 1))
                if u == 0:
                    act.wait_ge(scan_done, KT)
                    act.wait_ge(glu_done, KT)
                if u >= HI_SLOTS:
                    act.wait_ge(*split_used(u - HI_SLOTS))
                w, _, hi = split_halves(u)
                nc.scalar.activation(hi, w, ACT.Copy).then_inc(whi_done, 1)

            for m in range(NACT):
                tile(m)
                k, c = tiles[m]
                if (k, c) == ("uy", 6):
                    weight_high(0)
                    act.wait_ge(gate_mm, KT)
                    for i in range(KT):
                        nc.scalar.activation(xn_hi[i], xnT[:, i], ACT.Copy).then_inc(xhi_done, 1)
                    weight_high(1)
                if (k, c) == ("gr", 0):
                    weight_high(2)
                if m > first_tile and (m - first_tile) % 2:
                    weight_high((m - first_tile) // 2 + HI_SLOTS)
                if k == "gc" and 1 <= c <= 4:
                    if c == 1:
                        act.wait_ge(st_T, 2)
                    for i in (2 * c - 2, 2 * c - 1):
                        act.wait_ge(prod_done, i + 1)
                        nc.scalar.activation(gel_hi[:, i], gel[:, i], ACT.Copy).then_inc(ghi_done, 1)
                if k == "ux" and c >= 2:
                    gates(c - 2)
                if k == "uy" and c in (1, 2):
                    gates(c + 5)
                if (k, c) == ("ux", 5):
                    decay(0)
                if (k, c) == ("ux", 6):
                    root(0)
                if (k, c) == ("uy", 2):
                    decay(1)
                if (k, c) == ("uy", 4):
                    root(1)
                if (k, c) == ("uy", 7):
                    act.wait_ge(tile_act, m + 1)
                    nc.scalar.activation(gel, gel, ACT.Gelu_apprx_tanh).then_inc(gelu_done, 1)
            act.wait_ge(cen_done, 1)
            nc.scalar.activation(sq, cc, ACT.Square).then_inc(sq_done, 1)
            weight_high(11)
            act.wait_ge(var_done, 1)
            nc.scalar.activation(sq[:, 0], sq[:, 0], ACT.Sqrt).then_inc(std_done, 1)
            weight_high(12)
            act.wait_ge(conv_done, KT)
            act.wait_ge(st_cp, 2)
            for c in range(KT + 1):
                if c < KT:
                    act.wait_ge(nrm_done, c + 1)
                    nc.scalar.activation(cc[:, c], cc[:, c], ACT.Silu, scale=plg[:, c:c + 1],
                                         bias=plb[:, c:c + 1]).then_inc(silu_done, 1)
                if c:
                    act.wait_ge(silu_done, c)
                    nc.scalar.activation(cc_hi[:, c - 1], cc[:, c - 1], ACT.Copy).then_inc(chi_done, 1)
            weight_high(13)
            weight_high(14)
            act.wait_ge(st_ev, 3)
            act.dma_start(o["rc_s"][0].rearrange("s r (c p) -> (s r c) p", p=P).rearrange("(i q) p -> q i p", i=2),
                          outst[0:96, 0:2 * P].rearrange("q (i p) -> q i p", i=2)).then_inc(st_out, 16)
            act.dma_start(o["rc_p"][0, 0].rearrange("r (c p) -> (r c) p", p=P), outst[0:24, 2 * P:3 * P]).then_inc(st_out, 16)
            act.dma_start(o["h_p"][0, 0].rearrange("(c p) -> c p", p=P), outst[0:KT, 3 * P:4 * P]).then_inc(st_out, 16)
            act.dma_start(o["h_s"][0].rearrange("s (c p) -> (s c) p", p=P), outst[0:NS * KT, 4 * P:5 * P]).then_inc(st_out, 16)
            act.dma_start(o["cc_p"][0, 0].rearrange("r (c p) -> (r c) p", p=P).rearrange("(i q) p -> q i p", i=2),
                          outst[0:120, 5 * P:7 * P].rearrange("q (i p) -> q i p", i=2)).then_inc(st_out, 16)
            for s in range(NS):
                act.dma_start(o["cc_s"][0, s, CW - 1 - TS:].rearrange("t (c p) -> (t c) p", p=P),
                              outst[32 * (s % 4):32 * (s % 4) + 32, (7 + s // 4) * P:(8 + s // 4) * P]).then_inc(st_out, 16)
            act.wait_ge(st_T, 3)
            act.dma_start(g2_bc, a["norm2_g"][0:1, :].broadcast_to([P, D])).then_inc(g_in, 16)
            act.dma_start(gf_bc, a["final_norm_g"].unsqueeze(0).broadcast_to([P, D])).then_inc(g_in, 16)
            act.wait_ge(silu_done, KT)
            act.wait_ge(conv_done, KT)
            act.dma_start(g2_row, a["norm2_g"][0].rearrange("(p j) -> p j", p=P)).then_inc(g_in, 16)
            act.dma_start(wr[:, :, 0:NG], a["w_group"][0].rearrange("(p j) e -> p j e", p=P)).then_inc(router_in, 16)
            act.dma_start(wr[:, :, NG:], a["w_erouter"][0].rearrange("(p j) e -> p j e", p=P)).then_inc(router_in, 16)
            act.dma_start(rbias[:, 0:NG], a["b_group"][0:1, :].broadcast_to([P, NG])).then_inc(router_in, 16)
            act.dma_start(rbias[:, NG:], a["b_erouter"][0].rearrange("g e -> (g e)").unsqueeze(0).broadcast_to([P, NE]))\
               .then_inc(router_in, 16)
            for c in range(1, KT + 1, 2):
                weight_high(c // 2 + 15)
                for i in (c - 1, c):
                    act.wait_ge(merged, i + 1)
                    nc.scalar.activation(mrg_hi[:, i], sgr[:, i], ACT.Copy).then_inc(mhi_done, 1)
            weight_high(19)
            load_table(ACT.Sqrt)
            for t in range(NT + 1):
                if t < NT:
                    act.wait_ge(x1_done, NT + t + 1)
                    if t:
                        act.wait_ge(ss2_done, t)
                    nc.scalar.activation(junk[0:ROWS[t]], x[0:ROWS[t], t], ACT.Square,
                                         accum_out=stat[0:ROWS[t], 6 + t:7 + t]).then_inc(ss2_done, 1)
                j = 2 * t + 1
                act.wait_ge(xT2_mm, j + 1)
                nc.scalar.activation(xT2[:, j], bank[j % 4][:, 0:T], ACT.Copy).then_inc(xT2_act, 1)
            act.wait_ge(ms2_done, 1)
            nc.scalar.activation(stat[:, 9:12], stat[:, 9:12], ACT.Sqrt).then_inc(rs2_done, 1)
            act.wait_ge(ms2_done, 2)
            for t in range(NT - 1):
                nc.scalar.activation(xn2[0:ROWS[t], t], x[0:ROWS[t], t], ACT.Copy,
                                     scale=stat[0:ROWS[t], 9 + t:10 + t]).then_inc(xsc_done, 1)

            def high_parts(first):
                for t in SPLIT_ORDER:
                    n = ROWS[t]
                    if first:
                        act.wait_ge(xn2_last if t == NT - 1 else xn2_done, 1 if t == NT - 1 else t + 1)
                    nc.scalar.activation(xn2_hi[t][0:n], xn2[0:n, t], ACT.Copy).then_inc(hi_done, 1)

            load_table(ACT.Exp)
            act.wait_ge(ys_act, 1)
            act.wait_ge(ys_dve, 1)
            high_parts(True)
            act.wait_ge(ex_req, 1)
            nc.scalar.activation(gex, gex, ACT.Exp)
            nc.scalar.activation(pick[:, 3], pick[:, 2], ACT.Exp).then_inc(ex_done, 1)

            act.wait_ge(pick_done, 1)
            passes = act.value_load(npass[0:1, 0:1], min_val=1, max_val=MAX_PASSES)
            with act.Fori(0, passes) as r:
                with act.If(r > 0):
                    act.wait_ge(yT_mm, r * (2 * PT))
                    high_parts(False)
                with act.Else():
                    act.nop()
                for q in range(2 * KT):
                    act.wait_ge(gat_mm, r * (2 * KT) + (q + 1))
                    nc.scalar.activation(xs[:, q // 2, (q % 2) * T:(q % 2 + 1) * T], bank[q % 4][:, 0:T],
                                         ACT.Copy).then_inc(gat_done, 1)

                with act.Fori(0, NE // EXP_SLOTS) as g:
                    def results(s):
                        act.wait_ge(dn_mm, r * NE + g * EXP_SLOTS + (s + 1))
                        act.wait_ge(ys_act, r * NE + g * EXP_SLOTS + (s + 1))
                        at = act.value_load(off_i[0:1, bass.ds(g * EXP_SLOTS + s, 1)], min_val=0, max_val=SLOTS)
                        nc.scalar.activation(ys[:, 0:4, bass.ds(at, C)],
                                             bank[2 + 2 * (s % 2)][:, 0:4 * C].rearrange("p (m n) -> p m n", m=4),
                                             ACT.Copy).then_inc(ys_act, 1)

                    for s in range(EXP_SLOTS):
                        act.wait_ge(gu_mm, r * NE + g * EXP_SLOTS + (s + 1))
                        nc.scalar.activation(sg2[s % 2], bank[s % 2][:, 0:2 * C].rearrange("p (f n) -> p f n", f=FT),
                                             ACT.Silu).then_inc(silu2, 1)
                        if s >= 1:
                            results(s - 1)
                    results(EXP_SLOTS - 1)
                act.wait_ge(wT_done, r * 4 + 4)
                for q in range(2 * PT):
                    j, w = q // 2, min(P, SLOTS - q // 2 * P)
                    act.wait_ge(yT_mm, r * (2 * PT) + (q + 1))
                    nc.scalar.activation(yrow_hi[0:w, j, q % 2 * 512:(q % 2 + 1) * 512], bank[q % 2][0:w],
                                         ACT.Copy, scale=wpair[0:w, j:j + 1]).then_inc(yT_act, 1)
            load_table(ACT.Sqrt)
            for t in range(NT):
                if t:
                    act.wait_ge(ss3_done, t)
                act.wait_ge(y_done, passes * (2 * NT) + (2 * t + 2))
                nc.scalar.activation(junk[0:ROWS[t]], x[0:ROWS[t], t], ACT.Square,
                                     accum_out=stat[0:ROWS[t], 12 + t:13 + t]).then_inc(ss3_done, 1)
            act.wait_ge(ms3_done, 1)
            nc.scalar.activation(stat[:, 15:18], stat[:, 15:18], ACT.Sqrt).then_inc(rs3_done, 1)

        @block.vector
        def _(dve):
            step = Steps(dve, dstep)
            vec = nc.vector

            def bc(ap, n):
                return ap.unsqueeze(2).broadcast_to([P, NT, n])

            def bt(ap, n):
                return ap.unsqueeze(1).broadcast_to([P, NT, n])

            vec.memset(ones_b, 1.0)
            vec.memset(ones_d, 1.0 / D)
            vec.memset(ux[:, :, 0:RW - 1], 0.0)
            vec.memset(glu[:, :, 0:CW - 1], 0.0)
            vec.memset(xc[:, :, TP:HN].rearrange("p c (s j) -> p c s j", s=NS)[:, :, :, 0], 0.0)
            vec.memset(rbase, 0.0)
            vec.memset(spare, 1.0)
            vec.memset(stat, 1.0).then_inc(dconst, 1)

            def inverse_root(i, done, ms, rs):
                dve.wait_ge(done, NT)
                vec.tensor_scalar(stat[:, i + 3:i + 6], stat[:, i:i + 3], 1.0 / D, EPS, ALU.mult, ALU.add).then_inc(ms, 1)
                dve.wait_ge(rs, 1)
                step(vec.reciprocal(stat[:, i + 3:i + 6], stat[:, i + 3:i + 6]))

            inverse_root(0, ss_done, ms_done, rs_done)
            for t in range(NT):
                vec.tensor_scalar(xn[0:ROWS[t], t], x[0:ROWS[t], t], stat[0:ROWS[t], 3 + t:4 + t], None,
                                  ALU.mult).then_inc(xn_done, 1)
            dve.wait_ge(par_T, 1)
            vec.tensor_copy(par, bank[0][:, 0:408]).then_inc(par_done, 1)
            dve.wait_ge(rst_T, 1)
            vec.tensor_copy(state_cols(ux, UXP, UXS)[:, :, 0:RW - 1],
                            bank[1][:, 0:192].rearrange("p (s r c) -> p s r c", s=NS, r=RW - 1)).then_inc(rst_done, 1)
            dve.wait_ge(par_done, 1)
            for j in range(0, KT, 2):
                dve.wait_ge(xT_done, j + 1)
                vec.tensor_scalar(xnT[:, j], bank[4 + j % 4][:, 0:T], pn1[:, j:j + 1], None, ALU.mult).then_inc(xnT_done, 1)
            dve.wait_ge(lam_e, 1)
            e, z, z2, q = lam[:, 0], lam[:, 3], lam[:, 4], lam[:, 1]
            step(vec.tensor_scalar(z, e, 2.0, None, ALU.add))
            step(vec.reciprocal(z, z))
            step(vec.tensor_tensor(z, z, e, ALU.mult))
            step(vec.tensor_tensor(z2, z, z, ALU.mult))
            step(vec.tensor_scalar(q, z2, 1.0 / 17, None, ALU.mult))
            for k in range(7, 0, -1):
                step(vec.scalar_tensor_tensor(q, q, 1.0 / (2 * k + 1), z2, ALU.add, ALU.mult))
            step(vec.scalar_tensor_tensor(q, q, 1.0, z, ALU.add, ALU.mult))
            step(vec.tensor_scalar(z, plam, -1.0, 0.0, ALU.mult, ALU.max))
            step(vec.scalar_tensor_tensor(q, q, 2.0, z, ALU.mult, ALU.add))
            step(vec.tensor_scalar(lam[:, 2], q, -LRU_C, None, ALU.mult))
            vec.tensor_scalar(lam[:, 1], q, LRU_C, None, ALU.mult).then_inc(kappa_done, 1)

            for s in range(NS):
                dve.wait_ge(cst_T, s // 2 + 1)
                at = GLP + s * GLS
                b = bank[4 + s // 2][:, 240 * (s % 2):240 * (s % 2) + 240]
                vec.tensor_copy(glu[:, :, at:at + CW - 1], b.rearrange("p (r c) -> p c r", c=KT)).then_inc(cst_done, 1)

            def conv_prompts(c, taps=range(CW), between=None):
                dve.wait_ge(glu_done, c + 2)
                for w in taps:
                    if between and w in between:
                        between[w]()
                    for b in range(2):
                        y, ch = cc[:, c + b, 0:TP], c + b
                        if w:
                            dve.wait_ge(tap_done[b], (c // 2) * CW + w)
                            ins = vec.scalar_tensor_tensor(y, glu[:, ch, w:w + TP], pcw[:, w, ch:ch + 1], y, ALU.mult, ALU.add)
                        else:
                            ins = vec.tensor_scalar(y, glu[:, ch, 0:TP], pcw[:, 0, ch:ch + 1], pccb[:, ch:ch + 1],
                                                    ALU.mult, ALU.add)
                        ins.then_inc(tap_done[b], 1)
                for b in range(2 if CW - 1 in taps else 0):
                    dve.wait_ge(tap_done[b], (c // 2 + 1) * CW)

            def conv_samples(c):
                y = cc[:, c, TP:T]
                dve.wait_ge(win_done, c + 1)
                ins = vec.tensor_reduce(y, win.rearrange("p (n w) -> p n w", w=CW), AX_X, ALU.add)
                ins.then_inc(win_used, 1)
                dve.wait_ge(win_used, c + 1)
                vec.tensor_scalar(y, y, pccb[:, c:c + 1], None, ALU.add).then_inc(conv_done, 1)

            def conv_rnn(c):
                n = UXN - RW + 1
                for w in range(RW):
                    for b in range(2):
                        ch = c + b
                        v, u, tap = cv4[b][:, 0:n], ux[:, ch, w:w + n], prw[:, w, ch:ch + 1]
                        if w:
                            dve.wait_ge(rtap_done[b], (c // 2) * (RW - 1) + w)
                        else:
                            dve.wait_ge(tile_act, tile_at["ux", ch] + 1)
                            if ch >= 2:
                                dve.wait_ge(xc_done, ch - 1)
                        if w == 0:
                            vec.tensor_scalar(v, u, tap, prcb[:, ch:ch + 1], ALU.mult, ALU.add).then_inc(rtap_done[b], 1)
                        elif w < RW - 1:
                            vec.scalar_tensor_tensor(v, u, tap, v, ALU.mult, ALU.add).then_inc(rtap_done[b], 1)
                        else:
                            vec.scalar_tensor_tensor(xc[:, ch, 0:TP], ux[:, ch, RW - 1:UXP], tap, v[:, 0:TP], ALU.mult, ALU.add)
                            vec.scalar_tensor_tensor(seqs(xc[:, ch], TP, HS, 1, TS), seqs(ux[:, ch], UXP, UXS, RW - 1, TS), tap,
                                                     seqs(cv4[b], UXP, UXS, 0, TS), ALU.mult, ALU.add).then_inc(xc_done, 1)

            def variance(b):
                dve.wait_ge(dec_done, b + 1)
                step(vec.tensor_tensor(gate_r, dec, dec, ALU.mult))
                vec.scalar_tensor_tensor(tau, gate_r, 1.0, tau, ALU.add, ALU.mult).then_inc(vsq_done, 1)

            def scans(b):
                dve.wait_ge(inp_done, b + 1)
                dve.wait_ge(vrt_done, b + 1)
                dve.wait_ge(vsq_done, b + 1)
                step(vec.tensor_tensor(inp, inp, tau, ALU.mult))
                step(vec.memset(dec[:, :, TP:HN].rearrange("p c (s j) -> p c s j", s=NS)[:, :, :, 0], 0.0))
                step(vec.tensor_copy(inp[:, :, TP:HN].rearrange("p c (s j) -> p s j c", s=NS)[:, :, 0],
                                     ph0[:, :, b * HB:(b + 1) * HB]))
                for c in range(HB):
                    vec.tensor_tensor_scan(h[:, b * HB + c], dec[:, c], inp[:, c], 0.0, ALU.mult, ALU.add)\
                       .then_inc(scan_done, 1)

            def tile(k, c):
                m = tile_at[k, c]
                g = sgr if k == "rp" else sgc
                dve.wait_ge(tile_mm, m + 1)
                dve.wait_ge(tile_act, tile_at["gr" if k == "rp" else "gc", c] + 1)
                vec.tensor_tensor(g[:, c], bank[m % 4][:, 0:T], g[:, c], ALU.mult).then_inc(tile_dve, 1)

            dve.wait_ge(dconst, 1)
            def low(part, value, high, done, lo_sem, i):
                dve.wait_ge(done, i + 1)
                vec.tensor_tensor(part, value, as_f32(high), ALU.subtract).then_inc(lo_sem, 1)

            def weight_low(u):
                w, lo, hi = split_halves(u)
                low(lo, w, hi, whi_done, wlo_done, u)

            conv_prompts(0)
            conv_prompts(2)
            dve.wait_ge(rst_done, 1)
            conv_rnn(0)
            conv_prompts(4, range(0, 5))
            conv_rnn(2)
            conv_prompts(4, range(5, 10))
            conv_rnn(4)
            conv_prompts(4, range(10, 12))
            variance(0)
            conv_prompts(4, range(12, 15))
            conv_rnn(6)
            scans(0)
            for c in range(3):
                conv_samples(c)
                conv_prompts(4, range(15 + 3 * c, 18 + 3 * c))
            variance(1)
            conv_prompts(4, range(24, 27))
            scans(1)
            weight_low(0)
            dve.wait_ge(tile_mm, first_tile)
            for c in range(KT):
                low(xn_lo[:, c], xnT[:, c], xn_hi[c], xhi_done, xlo_done, c)
            weight_low(1)
            conv_prompts(4, range(27, CW))
            conv_prompts(6, between={
                3: lambda: weight_low(2), 5: lambda: conv_samples(3), 12: lambda: conv_samples(4),
                13: lambda: weight_low(4), 19: lambda: conv_samples(5), 22: lambda: weight_low(6),
                27: lambda: conv_samples(6)})
            conv_samples(7)
            weight_low(8)
            for c in range(KT):
                low(gel_lo[:, c], gel[:, c], gel_hi[:, c], ghi_done, glo_done, c)
            dve.wait_ge(conv_done, KT)
            vec.tensor_reduce(csum, cc.rearrange("p c n -> p n c"), AX_X, ALU.add).then_inc(sum_done, 1)
            dve.wait_ge(st_T, 1)
            vec.tensor_copy(outst[0:96, 0:2 * P], bank[4][0:96, 0:2 * P])
            vec.tensor_copy(outst[0:24, 2 * P:3 * P], bank[4][0:24, 2 * P:3 * P]).then_inc(st_ev, 1)
            dve.wait_ge(st_T, 2)
            vec.tensor_copy(outst[0:KT, 3 * P:4 * P], bank[5][0:KT, 0:P])
            vec.tensor_copy(outst[0:NS * KT, 4 * P:5 * P], bank[5][0:NS * KT, P:2 * P]).then_inc(st_ev, 1)
            dve.wait_ge(st_T, 3)
            vec.tensor_copy(outst[0:120, 5 * P:7 * P], bank[6][0:120, 0:2 * P])
            vec.tensor_copy(outst[:, 7 * P:9 * P], bank[6][:, 2 * P:4 * P]).then_inc(st_ev, 1)

            weight_low(9)
            dve.wait_ge(mean_mm, 1)
            vec.tensor_tensor(cc, cc, bank[4][:, 0:T].unsqueeze(1).broadcast_to([P, KT, T]), ALU.subtract)\
               .then_inc(cen_done, 1)
            tile("rp", 0)
            weight_low(10)
            tile("rp", 1)
            dve.wait_ge(sq_done, 1)
            vec.tensor_reduce(csum, sq.rearrange("p c n -> p n c"), AX_X, ALU.add).then_inc(sum_done, 1)
            tile("rp", 2)
            weight_low(11)
            tile("rp", 3)
            tile("rp", 4)
            dve.wait_ge(var_mm, 1)
            vec.tensor_scalar(sq[:, 0], bank[5][:, 0:T], EPS, None, ALU.add).then_inc(var_done, 1)
            dve.wait_ge(std_done, 1)
            step(vec.reciprocal(sq[:, 0], sq[:, 0]))
            for c in range(KT):
                vec.tensor_tensor(cc[:, c], cc[:, c], sq[:, 0], ALU.mult).then_inc(nrm_done, 1)
            tile("rp", 5)
            weight_low(12)
            tile("rp", 6)
            for c in range(KT):
                low(cc_lo[:, c], cc[:, c], cc_hi[:, c], chi_done, clo_done, c)
                if c == 3:
                    tile("rp", 7)
            weight_low(13)
            weight_low(14)
            for c in range(KT):
                tile("cp", c)
                if c % 2:
                    weight_low(c // 2 + 15)
                if c >= 2:
                    low(mrg_lo[:, c - 2], sgr[:, c - 2], mrg_hi[:, c - 2], mhi_done, mlo_done, c - 2)
            for c in range(KT - 2, KT):
                low(mrg_lo[:, c], sgr[:, c], mrg_hi[:, c], mhi_done, mlo_done, c)
            weight_low(19)

            for n in range(2):
                for t in range(NT):
                    dve.wait_ge(wo_mm, n * NT + t + 1)
                    xt = x[0:ROWS[t], t, n * 512:(n + 1) * 512]
                    vec.tensor_tensor(xt, bank[WO_BANKS[n * NT + t]][0:ROWS[t]], xt, ALU.add).then_inc(x1_done, 1)
            vec.memset(logit, 0.0).then_inc(dconst, 1)
            dve.wait_ge(router_in, 64)
            dve.wait_ge(g_in, 48)
            vec.tensor_tensor(wr, wr, g2_row.unsqueeze(2).broadcast_to([P, KT, NG + NE]), ALU.mult).then_inc(wr_done, 1)
            for j in range(0, KT, 2):
                dve.wait_ge(xT2_mm, j + 1)
                vec.tensor_copy(xT2[:, j], bank[j % 4][:, 0:T]).then_inc(xT2_dve, 1)
            dve.wait_ge(ss2_done, NT)
            vec.tensor_scalar(stat[:, 9:12], stat[:, 6:9], 1.0 / D, EPS, ALU.mult, ALU.add).then_inc(ms2_done, 1)
            dve.wait_ge(rs2_done, 1)
            vec.reciprocal(stat[:, 9:12], stat[:, 9:12]).then_inc(ms2_done, 1)
            dve.wait_ge(ms2_done, 2)

            dve.wait_ge(log_mm, 1)
            dve.wait_ge(router_in, 64)
            dve.wait_ge(dconst, 2)
            n = ROWS[NT - 1]
            vec.scalar_tensor_tensor(xn2[0:n, NT - 1], x[0:n, NT - 1], stat[0:n, 9 + NT - 1:9 + NT], g2_bc[0:n],
                                     ALU.mult, ALU.mult).then_inc(xn2_last, 1)
            for t in range(NT):
                ins = vec.scalar_tensor_tensor(logit[0:ROWS[t], t], bank[(5, 6, 7)[t]][0:ROWS[t], 0:NG + NE],
                                               stat[0:ROWS[t], 9 + t:10 + t], rbias[0:ROWS[t]], ALU.mult, ALU.add)
                step(ins)
            dve.wait_ge(consts, 4)
            gl, m0, m1, dm, ex = logit[:, :, 0:NG], pick[:, 0], pick[:, 1], pick[:, 2], pick[:, 3]
            pos1, pos2, w1, w2, m2 = pick[:, 4], pick[:, 5], pick[:, 6], pick[:, 7], pick[:, 8]

            def first_of(oh, src, m, pri, n):
                step(vec.tensor_reduce(m, src, AX_X, ALU.max))
                step(vec.tensor_tensor(oh, src, bc(m, n), ALU.is_equal))
                step(vec.tensor_tensor(oh, oh, bt(pri, n), ALU.mult))
                step(vec.tensor_reduce(pick[:, 9], oh, AX_X, ALU.max))
                step(vec.tensor_tensor(oh, oh, bc(pick[:, 9], n), ALU.is_equal))

            first_of(goh, gl, m0, gpri, NG)
            step(vec.tensor_tensor(gex, gl, bc(m0, NG), ALU.subtract))
            step(vec.tensor_scalar(gtmp, goh, -1.0, BIG, ALU.add, ALU.mult))
            by_group = lambda ap: ap.rearrange("p t (g e) -> p t g e", g=NG)
            over = lambda ap: ap.unsqueeze(3).broadcast_to([P, NT, NG, EG])
            step(vec.tensor_tensor(by_group(el), by_group(logit[:, :, NG:]), over(goh), ALU.mult))
            step(vec.tensor_tensor(by_group(el), by_group(el), over(gtmp), ALU.add))
            first_of(oh1, el, m1, epri, NE)
            step(vec.scalar_tensor_tensor(el, oh1, -BIG, el, ALU.mult, ALU.add))
            first_of(oh2, el, m2, epri, NE)
            vec.tensor_tensor(dm, m2, m1, ALU.subtract).then_inc(ex_req, 1)
            vec.tensor_tensor(mo, oh1, oh2, ALU.add).then_inc(mo_done, 1)
            def place(step):
                step.beside(vec.tensor_scalar(cwin, cnt, rbase, 0.0, ALU.subtract, ALU.max))
                step(vec.tensor_scalar(rtmp, rank, rbase, None, ALU.subtract))
                step(vec.tensor_scalar(cwin, cwin, float(C), None, ALU.min))
                step.beside(vec.tensor_tensor_scan(off, ones_b[:, 0:NE], cwin, 0.0, ALU.mult, ALU.add))
                step(vec.scalar_tensor_tensor(inw, rtmp, 0.0, mo, ALU.is_ge, ALU.mult))
                step.beside(vec.tensor_tensor(off, off, cwin, ALU.subtract))
                step(vec.scalar_tensor_tensor(inw, rtmp, float(C), inw, ALU.is_lt, ALU.mult))
                step.beside(vec.tensor_copy(off_i, off))
                step(vec.tensor_tensor(rtmp, rtmp, bt(off, NE), ALU.add))
                step(vec.scalar_tensor_tensor(rtmp, rtmp, 1.0, inw, ALU.add, ALU.mult))
                step.beside(vec.tensor_tensor(el, rtmp, oh2, ALU.mult))
                step(vec.tensor_tensor(inw, rtmp, oh1, ALU.mult))
                step.beside(vec.tensor_reduce(pos2, el, AX_X, ALU.add))
                step(vec.tensor_reduce(pos1, inw, AX_X, ALU.add))
                for t in range(NT):
                    n = ROWS[t]
                    step(vec.tensor_scalar(sel[0:n, t], iota[0:n], pos2[0:n, t:t + 1], None, ALU.is_equal))
                    vec.scalar_tensor_tensor(sel[0:n, t], iota[0:n], pos1[0:n, t:t + 1], as_f32(sel[0:n, t]),
                                             ALU.is_equal, ALU.add).then_inc(sel_done, 1)
                assert step.n == PLACE_STEPS, step.n

            dve.wait_ge(rank_mm, 1)
            dve.wait_ge(iota_done, 1)
            step.beside(vec.tensor_copy(cnt, bank[6][:, NE * NT:NE * (NT + 1)]))
            step(vec.tensor_copy(rank, bank[6][:, 0:NE * NT].rearrange("p (t e) -> p t e", t=NT)))
            step(vec.tensor_reduce(fpass[:, 0:1], cnt, AX_X, ALU.max))
            step(vec.tensor_scalar(fpass[:, 1:2], fpass[:, 0:1], float(C), 1.0, ALU.is_gt, ALU.add))
            for i in range(2, MAX_PASSES):
                step(vec.scalar_tensor_tensor(fpass[:, 1:2], fpass[:, 0:1], float(C * i), fpass[:, 1:2], ALU.is_gt, ALU.add))
            vec.tensor_copy(npass[:, 0:1], fpass[:, 1:2]).then_inc(pick_done, 1)
            place(Steps(dve, place_step))
            dve.wait_ge(st_out, 16 * ST_DMAS)
            dve.wait_ge(pick_done, 1)
            passes = dve.value_load(npass[0:1, 0:1], min_val=1, max_val=MAX_PASSES)

            dve.nop().then_inc(y_done, 2 * NT)
            with dve.Fori(0, passes) as r:
                step = Steps(dve, rstep, r * PASS_STEPS)
                with dve.If(r > 0):
                    for i, t in enumerate(SPLIT_ORDER):
                        n = ROWS[t]
                        dve.wait_ge(hi_done, r * NT + (i + 1))
                        vec.tensor_tensor(xn2_lo[t][0:n], xn2[0:n, t], as_f32(xn2_hi[t][0:n]), ALU.subtract)\
                           .then_inc(lo_done, 1)
                    place(Steps(dve, place_step, r * PLACE_STEPS))
                with dve.Else():
                    dve.nop()
                dve.wait_ge(ex_done, 1)
                step(vec.tensor_reduce(m0, gex, AX_X, ALU.add))
                step(vec.tensor_scalar(m1, ex, 1.0, None, ALU.add))
                step(vec.tensor_tensor(m0, m0, m1, ALU.mult))
                step(vec.reciprocal(w1, m0))
                step(vec.tensor_tensor(w2, w1, ex, ALU.mult))

                def weights(t):
                    n, w = ROWS[t], wsel[0:ROWS[t], t % 2]
                    if t == NT - 1:
                        dve.wait_ge(wT_used, r * NT + 1)
                    step(vec.tensor_scalar(w, iota[0:n], pos1[0:n, t:t + 1], w1[0:n, t:t + 1], ALU.is_equal, ALU.mult))
                    step(vec.tensor_scalar(wtmp[0:n], iota[0:n], pos2[0:n, t:t + 1], w2[0:n, t:t + 1],
                                           ALU.is_equal, ALU.mult))
                    vec.tensor_tensor(w, w, wtmp[0:n], ALU.add).then_inc(wsel_done, 1)
                    dve.wait_ge(wsel_done, r * NT + (t + 1))

                for t in range(NT):
                    weights(t)
                dve.wait_ge(wT_used, r * NT + NT)
                step(vec.memset(wpair_t, 0.0))
                for t in range(NT):
                    for j in range(PT):
                        at, k = weight_block(j, t), min(P, SLOTS - j * P)
                        ins = vec.tensor_reduce(wpair_t[0:k, t, j:j + 1], bank[4 + at // 512][0:k, at % 512:at % 512 + ROWS[t]],
                                                AX_X, ALU.add)
                step(ins)
                vec.tensor_reduce(wpair, wpair_t.rearrange("p t j -> p j t"), AX_X, ALU.add).then_inc(wT_done, 1)
                for i in range(3):
                    for lo, hi, k in wT_parts(i):
                        ins = vec.tensor_scalar(selT[0:k, 512 * i + lo:512 * i + hi], bank[4 + i][0:k, lo:hi],
                                                0.0, None, ALU.is_gt)
                    ins.then_inc(wT_done, 1)

                with dve.Fori(0, NE // EXP_SLOTS) as g:
                    def results(s):
                        dve.wait_ge(dn_mm, r * NE + g * EXP_SLOTS + (s + 1))
                        dve.wait_ge(ys_dve, r * NE + g * EXP_SLOTS + (s + 1))
                        at = dve.value_load(off_i[0:1, bass.ds(g * EXP_SLOTS + s, 1)], min_val=0, max_val=SLOTS)
                        vec.tensor_copy(ys[:, 4:8, bass.ds(at, C)],
                                        bank[3 + 2 * (s % 2)][:, 0:4 * C].rearrange("p (m n) -> p m n", m=4)).then_inc(ys_dve, 1)

                    for s in range(EXP_SLOTS):
                        dve.wait_ge(silu2, r * NE + g * EXP_SLOTS + (s + 1))
                        vec.tensor_tensor(hid[s % 2], bank[s % 2][:, 2 * C:4 * C].rearrange("p (f n) -> p f n", f=FT),
                                          sg2[s % 2], ALU.mult).then_inc(hid_done, 1)
                        if s >= 1:
                            results(s - 1)
                    results(EXP_SLOTS - 1)
                dve.wait_ge(wT_done, r * 4 + 4)
                for q in range(2 * PT):
                    j, w = q // 2, min(P, SLOTS - q // 2 * P)
                    lo, hi = q % 2 * 512, (q % 2 + 1) * 512
                    dve.wait_ge(yT_act, r * (2 * PT) + (q + 1))
                    vec.scalar_tensor_tensor(yrow_lo[0:w, j, lo:hi], bank[q % 2][0:w], wpair[0:w, j:j + 1],
                                             as_f32(yrow_hi[0:w, j, lo:hi]), ALU.mult, ALU.subtract).then_inc(yT_dve, 1)
                for t in range(NT):
                    for n in range(2):
                        dve.wait_ge(y_mm, r * (2 * NT) + (2 * t + n + 1))
                        xt = x[0:ROWS[t], t, n * 512:(n + 1) * 512]
                        vec.tensor_tensor(xt, bank[2 + 2 * t + n][0:ROWS[t]], xt, ALU.add).then_inc(y_done, 1)
                step(vec.tensor_scalar(rbase, rbase, float(C), None, ALU.add))
                assert step.n == PASS_STEPS, step.n

            dve.wait_ge(ss3_done, NT)
            vec.tensor_scalar(stat[:, 15:18], stat[:, 12:15], 1.0 / D, EPS, ALU.mult, ALU.add).then_inc(ms3_done, 1)
            dve.wait_ge(rs3_done, 1)
            vec.reciprocal(stat[:, 15:18], stat[:, 15:18]).then_inc(ms3_done, 1)
            dve.wait_ge(ms3_done, 2)
            for t in range(NT):
                xt = x[0:ROWS[t], t]
                vec.scalar_tensor_tensor(xt, xt, stat[0:ROWS[t], 15 + t:16 + t], gf_bc[0:ROWS[t]],
                                         ALU.mult, ALU.mult).then_inc(fin_done, 1)

        @block.tensor
        def _(pe):
            mm, tp = nc.tensor.matmul, nc.tensor.transpose

            def keep_clock(q, n):
                for _ in range(n):
                    mm(bank[q][:, 0:P], ident, ident, start=True, stop=True)

            pe.wait_ge(consts, 1)
            keep_clock(2, 24)
            pe.wait_ge(par_in, 16 * 12)
            for n, i, at in ((96, 0, 0), (124, 1, 96), (124, 2, 220), (64, 3, 344)):
                ins = tp(bank[0][:, at:at + n], prow[0:n, i], ident[0:n, 0:n])
            ins.then_inc(par_T, 1)
            for i in range(2):
                ins = tp(bank[1][:, 96 * i:96 * i + 96], prow[0:96, 4 + i], ident[0:96, 0:96])
            ins.then_inc(rst_T, 1)

            def conf_states(g):
                for i in range(4):
                    ins = tp(bank[4 + g][:, 120 * i:120 * i + 120], crow[0:120, 4 * g + i], ident[0:120, 0:120])
                ins.then_inc(cst_T, 1)

            pe.wait_ge(xn_done, NT)
            for j in range(KT):
                if j >= 4:
                    pe.wait_ge(xnT_done if j % 2 == 0 else xnT_act, (j - 4) // 2 + 1)
                for t in range(NT):
                    n = ROWS[t]
                    ins = tp(bank[4 + j % 4][:, t * P:t * P + n], xn[0:n, t, j * P:(j + 1) * P], ident[0:n, 0:n])
                ins.then_inc(xT_done, 1)
            pe.wait_ge(par_done, 1)
            pe.wait_ge(rst_done, 1)
            pe.wait_ge(xnT_done, KT // 2)
            pe.wait_ge(xnT_act, KT // 2)

            def tile(m):
                k, c = tiles[m]
                b = blocks.index((k, c // MB))
                if m == 0:
                    pe.wait_ge(first_in, 16)
                if c % MB == 0:
                    pe.wait_ge(mix_in[b % MIX_SLOTS], 16 * (b // MIX_SLOTS + 1))
                if m >= 4:
                    if m - 4 < NACT:
                        pe.wait_ge(tile_act, m - 3)
                    else:
                        pe.wait_ge(tile_dve, m - 3 - NACT)
                if m >= first_tile:
                    u = (m - first_tile) // 2
                    pe.wait_ge(*low_ready(u))
                    _, lo, hi = split_halves(u)
                    def rows(ap):
                        return [ap[:, i] for i in range(KT)]
                    x_hi, x_lo, ready = {"rp": (rows(gel_hi), rows(gel_lo), glo_done),
                                         "cp": (rows(cc_hi), rows(cc_lo), clo_done)}.get(k, (xn_hi, rows(xn_lo), xlo_done))
                    cols = slice((c % 2) * P, (c % 2 + 1) * P)
                    for i in range(KT):
                        if c == 0:
                            pe.wait_ge(ready, i + 1)
                        for j, (w, xp) in enumerate(((hi, x_hi), (hi, x_lo), (lo, x_hi))):
                            ins = mm(bank[m % 4][:, 0:T], w[:, i, cols], xp[i],
                                     start=(i == 0 and j == 0), stop=(i == KT - 1 and j == 2))
                    ins.then_inc(tile_mm, 1)
                    return
                for i in range(KT):
                    ins = mm(bank[m % 4][:, 0:T], mix_w[b % MIX_SLOTS][:, i, (c % MB) * P:(c % MB + 1) * P], xnT[:, i],
                             start=(i == 0), stop=(i == KT - 1))
                ins.then_inc(tile_mm, 1)

            def gates(c):
                q = 4 + 2 * (c % 2)
                pe.wait_ge(xc_done, c + 1)
                if c == 0:
                    pe.wait_ge(wbd_in, 64)
                    pe.wait_ge(cst_done, NS)
                if c >= 2:
                    pe.wait_ge(gate_act, c - 1)
                mm(bank[q][:, 0:HN], wbd[:, 0, c], xc[:, c], start=True, stop=True)
                mm(bank[q + 1][:, 0:HN], wbd[:, 1, c], xc[:, c], start=True, stop=True).then_inc(gate_mm, 1)

            for m in range(len(tiles)):
                k, c = tiles[m]
                if (k, c) == ("gc", 0):
                    pe.wait_ge(gate_act, KT)
                    pe.wait_ge(st_cp, 2)
                    for i in range(2):
                        tp(bank[4][0:96, i * P:(i + 1) * P], st_ux[:, 96 * i:96 * i + 96], ident)
                    tp(bank[4][0:24, 2 * P:3 * P], st_uxp, ident).then_inc(st_T, 1)
                    tp(bank[5][0:KT, 0:P], h[:, :, TP - 1], ident)
                    tp(bank[5][0:NS * KT, P:2 * P], st_h, ident).then_inc(st_T, 1)
                    for i in range(2):
                        tp(bank[6][0:120, i * P:(i + 1) * P], st_glup[:, 120 * i:120 * i + 120], ident)
                    for i in range(2):
                        ins = tp(bank[6][:, (2 + i) * P:(3 + i) * P], st_glu[:, i * P:(i + 1) * P], ident)
                    ins.then_inc(st_T, 1)
                if (k, c) == ("rp", 1):
                    pe.wait_ge(sum_done, 1)
                    pe.wait_ge(st_ev, 2)
                    mm(bank[4][:, 0:T], ones_d, csum, start=True, stop=True).then_inc(mean_mm, 1)
                if (k, c) == ("rp", 5):
                    pe.wait_ge(sum_done, 2)
                    mm(bank[5][:, 0:T], ones_d, csum, start=True, stop=True).then_inc(var_mm, 1)
                tile(m)
                if m == 2:
                    pe.wait_ge(cst_in, 16)
                    for g in range(4):
                        conf_states(g)
                if k == "ux" and c >= 2:
                    gates(c - 2)
                if k == "uy" and c in (1, 2):
                    gates(c + 5)

            pe.wait_ge(st_ev, 3)
            for n in range(2):
                for half in range(2):
                    u = WO_UNIT + 2 * n + half
                    pe.wait_ge(*low_ready(u))
                    _, lo, hi = split_halves(u)
                    for t in range(NT):
                        q = WO_BANKS[n * NT + t]
                        if q < 4 and half == 0:
                            pe.wait_ge(tile_dve, 2 * KT - 3 + q)
                        tok = slice(t * P, t * P + ROWS[t])
                        for i in range(HB):
                            c = half * HB + i
                            if n == 0 and t == 0:
                                pe.wait_ge(mlo_done, c + 1)
                            for j, (xp, w) in enumerate(((mrg_hi, hi), (mrg_lo, hi), (mrg_hi, lo))):
                                ins = mm(bank[q][0:ROWS[t]], xp[:, c, tok], w[:, i],
                                         start=(c == 0 and j == 0), stop=(c == KT - 1 and j == 2))
                        if half:
                            ins.then_inc(wo_mm, 1)
                    if n == 0 and half == 0:
                        ins.then_inc(half_mm, 1)

            by_j = lambda ap: ap.rearrange("p t (m j) -> p t j m", j=KT)

            def logits(j):
                if j == 0:
                    pe.wait_ge(wr_done, 1)
                pe.wait_ge(xT2_dve if j % 2 == 0 else xT2_act, j // 2 + 1)
                for t in range(NT):
                    ins = mm(bank[(5, 6, 7)[t]][0:ROWS[t], 0:NG + NE], xT2[:, j, t * P:t * P + ROWS[t]], wr[:, j],
                             start=(j == 0), stop=(j == KT - 1))
                if j == KT - 1:
                    ins.then_inc(log_mm, 1)

            for j in range(KT):
                if j == 0:
                    pe.wait_ge(x1_done, 2 * NT)
                if j >= 4:
                    pe.wait_ge(xT2_dve if j % 2 == 0 else xT2_act, (j - 4) // 2 + 1)
                for t in range(NT):
                    n = ROWS[t]
                    ins = tp(bank[j % 4][:, t * P:t * P + n], by_j(x)[0:n, t, j], ident[0:n, 0:n])
                ins.then_inc(xT2_mm, 1)
                if j >= 2:
                    logits(j - 2)
            for j in range(KT - 2, KT):
                logits(j)
            keep_clock(3, 30)
            pe.wait_ge(mo_done, 1)
            pe.wait_ge(consts, 2)
            for t in range(NT + 1):
                last = min(t, NT - 1)
                for i in range(last + 1):
                    w = tri if i == t else ones_b
                    n = ROWS[i]
                    ins = mm(bank[6][:, t * NE:(t + 1) * NE], w[0:n], mo[0:n, i], start=(i == 0), stop=(i == last))
            ins.then_inc(rank_mm, 1)
            keep_clock(3, 26)

            pe.wait_ge(pick_done, 1)
            passes = pe.value_load(npass[0:1, 0:1], min_val=1, max_val=MAX_PASSES)
            with pe.Fori(0, passes) as r:
                def gather(q, t):
                    n = ROWS[t]
                    for part in (xn2_hi, xn2_lo):
                        ins = mm(bank[q % 4][:, 0:T], part[t][0:n].rearrange("p (m j) -> p j m", j=KT)[:, q // 2],
                                 sel[0:n, t, (q % 2) * T:(q % 2 + 1) * T],
                                 start=(t == 0 and part is xn2_hi), stop=(t == NT - 1 and part is xn2_lo))
                    return ins

                for t in range(NT):
                    if t == 0:
                        pe.wait_ge(hi_done, r * NT + NT)
                        pe.wait_ge(lo_done, r * NT + NT)
                    pe.wait_ge(sel_done, r * NT + (t + 1))
                    for q in range(4):
                        ins = gather(q, t)
                        if t == NT - 1:
                            ins.then_inc(gat_mm, 1)
                def turn_weights(t):
                    if t == 1:
                        pe.wait_ge(gat_done, r * (2 * KT) + 2 * KT)
                        pe.wait_ge(tail_done, 1)
                    if t < NT - 1:
                        pe.wait_ge(wsel_done, r * NT + (t + 1))
                    for j in range(PT):
                        if t == NT - 2 and j == PT - 1:
                            pe.wait_ge(wsel_done, r * NT + NT)
                        w = min(P, SLOTS - j * P)
                        at = weight_block(j, t)
                        ins = tp(bank[4 + at // 512][0:w, at % 512:at % 512 + ROWS[t]],
                                 wsel[0:ROWS[t], t % 2, j * P:j * P + w], ident[0:ROWS[t], 0:ROWS[t]])
                    ins.then_inc(wT_used, 1)

                for q in range(4, 2 * KT):
                    if q == 10:
                        turn_weights(0)
                    pe.wait_ge(gat_done, r * (2 * KT) + (q - 3))
                    for t in range(NT):
                        ins = gather(q, t)
                    ins.then_inc(gat_mm, 1)
                turn_weights(1)
                turn_weights(2)

                with pe.Fori(0, NE // EXP_SLOTS) as g:
                    def gate_up(s):
                        at = pe.value_load(off_i[0:1, bass.ds(g * EXP_SLOTS + s, 1)], min_val=0, max_val=SLOTS)
                        pe.wait_ge(gu_in[s], r * (32 * NE // EXP_SLOTS) + g * 32 + 32)
                        if s >= 2:
                            pe.wait_ge(hid_done, r * NE + g * EXP_SLOTS + (s - 1))
                        for m in range(2):
                            for f in range(FT):
                                for k in range(KT):
                                    ins = mm(bank[s % 2][:, (2 * m + f) * C:(2 * m + f + 1) * C], w_gu[s][m][:, k, f],
                                             xs[:, k, bass.ds(at, C)], start=(k == 0), stop=(k == KT - 1))
                        ins.then_inc(gu_mm, 1)

                    def down(s):
                        pe.wait_ge(dn_in[s], r * (16 * NE // EXP_SLOTS) + g * 16 + 16)
                        pe.wait_ge(hid_done, r * NE + g * EXP_SLOTS + (s + 1))
                        if s == 1:
                            pe.wait_ge(wT_done, r * 4 + 4)
                        done = r * NE + g * EXP_SLOTS + (1 if s < 2 else s)
                        pe.wait_ge(ys_act, done)
                        pe.wait_ge(ys_dve, done)
                        for m in range(KT):
                            for f in range(FT):
                                ins = mm(bank[2 + 2 * (s % 2) + m // 4][:, (m % 4) * C:(m % 4 + 1) * C],
                                         w_dn[s][:, f, m * P:(m + 1) * P], hid[s % 2][:, f], start=(f == 0), stop=(f == FT - 1))
                        ins.then_inc(dn_mm, 1)

                    gate_up(0)
                    for s in range(1, EXP_SLOTS):
                        gate_up(s)
                        down(s - 1)
                    down(EXP_SLOTS - 1)

                keep_clock(0, 7)
                pe.wait_ge(ys_act, r * NE + (NE + 1))
                pe.wait_ge(ys_dve, r * NE + (NE + 1))

                def turn(q):
                    if q >= 2:
                        pe.wait_ge(yT_dve, r * (2 * PT) + (q - 1))
                    j, w = q // 2, min(P, SLOTS - q // 2 * P)
                    for i in range(4):
                        ins = tp(bank[q % 2][0:w, i * P:(i + 1) * P], ys[:, 4 * (q % 2) + i, j * P:j * P + w], ident)
                    ins.then_inc(yT_mm, 1)

                turn(0)
                turn(1)
                keep_clock(7, 5)
                for j in range(PT):
                    if j + 1 < PT:
                        turn(2 * j + 2)
                        turn(2 * j + 3)
                    pe.wait_ge(yT_dve, r * (2 * PT) + (2 * j + 2))
                    w = min(P, SLOTS - j * P)
                    for t in range(NT):
                        at = weight_block(j, t)
                        for n in range(2):
                            for part in (yrow_hi, yrow_lo):
                                ins = mm(bank[2 + 2 * t + n][0:ROWS[t]], selT[0:w, at:at + ROWS[t]],
                                         part[0:w, j, n * 512:(n + 1) * 512],
                                         start=(j == 0 and part is yrow_hi), stop=(j == PT - 1 and part is yrow_lo))
                            if j == PT - 1:
                                ins.then_inc(y_mm, 1)


_OUTS = {"y_p": (1, SEQ, D), "y_s": (NS, TS, D), "h_p": (1, 1, D), "rc_p": (1, 1, RW - 1, D), "cc_p": (1, 1, CW - 1, D),
         "h_s": (1, NS, D), "rc_s": (1, NS, RW - 1, D), "cc_s": (1, NS, CW - 1, D)}


def kernel(**inputs):
    import concourse.bacc as bacc
    from concourse.bass_utils import run_bass_kernel_spmd

    nc = bacc.Bacc("TRN2", target_bir_lowering=False, num_devices=1)
    arrays, a, o = {}, {}, {}
    for name, value in inputs.items():
        arrays[name] = np.ascontiguousarray(value)
        a[name] = nc.dram_tensor(name, arrays[name].shape, F32, kind="ExternalInput").ap()
    for name, shape in _OUTS.items():
        o[name] = nc.dram_tensor(f"out_{name}", shape, F32, kind="ExternalOutput").ap()
    trunk(nc, a, o)
    got = run_bass_kernel_spmd(nc, [arrays], core_ids=[0]).results[0]
    return tuple(got[f"out_{name}"] for name in _OUTS)
```
